# Optimizing a Trainium2 kernel written in Bass

```python
import jax, jax.numpy as jnp
from jax import lax
import numpy as np
import math
import jax
import jax.numpy as jnp

D_MODEL = 1024
BATCH = 1
SEQ = 512
DEPTH = 1

GRID_W = 64
CTX_LEN = 256
HEAD_DIM = 64
ATTN_HEADS = 8
ATTN_KV_HEADS = 2
GQA_GROUP = ATTN_HEADS // ATTN_KV_HEADS
RET_HEADS = 8
ATTN_WIDTH = ATTN_HEADS * HEAD_DIM
KV_WIDTH = ATTN_KV_HEADS * HEAD_DIM
RET_WIDTH = RET_HEADS * HEAD_DIM
MIX_WIDTH = ATTN_WIDTH + RET_WIDTH
IN_PROJ_WIDTH = ATTN_WIDTH + 2 * KV_WIDTH + 4 * RET_WIDTH
SPLITS = (ATTN_WIDTH, ATTN_WIDTH + KV_WIDTH, ATTN_WIDTH + 2 * KV_WIDTH,
          ATTN_WIDTH + 2 * KV_WIDTH + RET_WIDTH, ATTN_WIDTH + 2 * KV_WIDTH + 2 * RET_WIDTH,
          ATTN_WIDTH + 2 * KV_WIDTH + 3 * RET_WIDTH)
FFN_HIDDEN = -(-8 * D_MODEL // (3 * 256)) * 256
N_MOD = 6
QBLOCK = 128
RET_CHUNK = 128
ROPE_BASE = 10000.0
ATTN_SCALE = HEAD_DIM ** -0.5
EPS = 1e-6


def rms_norm(x, g):
    xf = x.astype(jnp.float32)
    y = xf * lax.rsqrt(jnp.mean(xf * xf, axis=-1, keepdims=True) + EPS)
    return (y * g.astype(jnp.float32)).astype(x.dtype)

def head_group_norm(o):
    mu = jnp.mean(o, axis=-1, keepdims=True)
    var = jnp.mean(jnp.square(o - mu), axis=-1, keepdims=True)
    return (o - mu) * lax.rsqrt(var + EPS)

def modulate(h, shift, scale):
    return h * (1 + scale) + shift

def axial_rope(rows):
    row = jnp.broadcast_to(jnp.arange(rows)[:, None], (rows, GRID_W)).reshape(-1).astype(jnp.float32)
    col = jnp.broadcast_to(jnp.arange(GRID_W)[None, :], (rows, GRID_W)).reshape(-1).astype(jnp.float32)
    n_freq = HEAD_DIM // 4
    inv = ROPE_BASE ** (-jnp.arange(n_freq, dtype=jnp.float32) / n_freq)
    ang = jnp.concatenate([row[:, None] * inv, col[:, None] * inv], axis=-1)
    return jnp.cos(ang), jnp.sin(ang)

def apply_rope(x, cos, sin):
    half = HEAD_DIM // 2
    x1, x2 = x[..., :half], x[..., half:]
    c, s = cos[None, :, None, :], sin[None, :, None, :]
    return jnp.concatenate([x1 * c - x2 * s, x1 * s + x2 * c], axis=-1).astype(x.dtype)

def project(h, w_in, q_norm_g, k_norm_g):
    B, N, _ = h.shape
    qa, ka, va, qr, kr, vr, gr = jnp.split(h @ w_in, SPLITS, axis=-1)
    heads = lambda a: a.reshape(B, N, -1, HEAD_DIM)
    qa = rms_norm(heads(qa), q_norm_g)
    ka = rms_norm(heads(ka), k_norm_g)
    return qa, ka, heads(va), heads(qr), heads(kr) * ATTN_SCALE, heads(vr), gr

def gqa_block(q, k, v):
    B, Q = q.shape[:2]
    qg = q.reshape(B, Q, ATTN_KV_HEADS, GQA_GROUP, HEAD_DIM)
    s = jnp.einsum('bqkgd,btkd->bkgqt', qg, k, preferred_element_type=jnp.float32) * ATTN_SCALE
    p = jax.nn.softmax(s, axis=-1).astype(v.dtype)
    o = jnp.einsum('bkgqt,btkd->bqkgd', p, v)
    return o.reshape(B, Q, ATTN_WIDTH)

def latent_attention(q, k_lat, v_lat, k_ctx, v_ctx):
    B, N = q.shape[:2]
    k_all = jnp.concatenate([k_ctx, k_lat], axis=1)
    v_all = jnp.concatenate([v_ctx, v_lat], axis=1)
    qb = q.reshape(B, N // QBLOCK, QBLOCK, ATTN_HEADS, HEAD_DIM).swapaxes(0, 1)
    o = lax.map(lambda qi: gqa_block(qi, k_all, v_all), qb)
    return o.swapaxes(0, 1).reshape(B, N, ATTN_WIDTH)

def retention_chunkwise(q, k, v, log_gamma, state0):
    B, N, H, d = q.shape
    C = RET_CHUNK
    nc = N // C
    lg = log_gamma.astype(jnp.float32)
    chunks = lambda a: a.astype(jnp.float32).reshape(B, nc, C, H, d).transpose(1, 0, 3, 2, 4)
    pos = jnp.arange(C, dtype=jnp.float32)
    diff = pos[:, None] - pos[None, :]
    decay_mat = jnp.where(diff >= 0, jnp.exp(lg[:, None, None] * jnp.maximum(diff, 0.0)), 0.0)
    q_decay = jnp.exp(lg[:, None] * (pos + 1.0))[..., None]
    k_decay = jnp.exp(lg[:, None] * (C - 1.0 - pos))[..., None]
    chunk_decay = jnp.exp(lg * C)[:, None, None]

    def step(state, qkv):
        qc, kc, vc = qkv
        inner = jnp.einsum('bhid,bhjd->bhij', qc, kc) * decay_mat
        o = jnp.einsum('bhij,bhjd->bhid', inner, vc) + jnp.einsum('bhid,bhde->bhie', qc, state) * q_decay
        state = state * chunk_decay + jnp.einsum('bhjd,bhje->bhde', kc * k_decay, vc)
        return state, o

    state, o = lax.scan(step, state0.astype(jnp.float32), (chunks(q), chunks(k), chunks(v)))
    return o.transpose(1, 0, 3, 2, 4).reshape(B, N, H, d), state

def bidir_retention(q, k, v, lg_f, lg_b, state_f, state_b):
    o_f, s_f = retention_chunkwise(q, k, v, lg_f, state_f)
    o_b, s_b = retention_chunkwise(q[:, ::-1], k[:, ::-1], v[:, ::-1], lg_b, state_b)
    return o_f + o_b[:, ::-1], s_f, s_b

def merge_heads(att, ret, g_r, w_out):
    B, N = att.shape[:2]
    ret = head_group_norm(ret).reshape(B, N, RET_WIDTH).astype(g_r.dtype) * jax.nn.silu(g_r)
    return jnp.concatenate([att, ret], axis=-1) @ w_out

def swiglu(h, w_ffn_in, w_ffn_out):
    a, b = jnp.split(h @ w_ffn_in, 2, axis=-1)
    return (jax.nn.silu(a) * b) @ w_ffn_out

def first_inputs(seed: int = 0) -> dict:
    key = jax.random.key(seed)
    ks = jax.random.split(key, 18)
    D = D_MODEL
    nrm = lambda k, shape: jax.random.normal(k, shape, jnp.float32)
    w = lambda k, shape, fan_in, g=1.0: nrm(k, shape) * (g * fan_in ** -0.5)
    gain = lambda k, shape: 1.0 + 0.05 * nrm(k, shape)
    gammas = 1.0 - 2.0 ** (-5.0 - jnp.arange(RET_HEADS, dtype=jnp.float32))
    base = jnp.log(-jnp.log(gammas))
    return {
        'x': nrm(ks[0], (BATCH, SEQ, D)),
        'c': nrm(ks[1], (BATCH, D)),
        'ctx': nrm(ks[2], (BATCH, CTX_LEN, D)),
        'c_ctx': nrm(ks[3], (D,)),
        'w_mod': w(ks[4], (DEPTH, D, N_MOD * D), D, 0.5),
        'b_mod': 0.02 * nrm(ks[5], (DEPTH, N_MOD * D)),
        'g_pre_mix': gain(ks[6], (DEPTH, D)),
        'g_post_mix': gain(ks[7], (DEPTH, D)),
        'g_pre_ffn': gain(ks[8], (DEPTH, D)),
        'g_post_ffn': gain(ks[9], (DEPTH, D)),
        'w_in': w(ks[10], (DEPTH, D, IN_PROJ_WIDTH), D),
        'q_norm_g': gain(ks[11], (DEPTH, HEAD_DIM)),
        'k_norm_g': gain(ks[12], (DEPTH, HEAD_DIM)),
        'ret_decay_fwd': base + 0.1 * nrm(ks[13], (DEPTH, RET_HEADS)),
        'ret_decay_bwd': base + 0.1 * nrm(ks[14], (DEPTH, RET_HEADS)),
        'w_out': w(ks[15], (DEPTH, MIX_WIDTH, D), MIX_WIDTH),
        'w_ffn_in': w(ks[16], (DEPTH, D, 2 * FFN_HIDDEN), D),
        'w_ffn_out': w(ks[17], (DEPTH, FFN_HIDDEN, D), FFN_HIDDEN),
    }

def first_block(x, c, ctx, c_ctx, w_mod, b_mod, g_pre_mix, g_post_mix, g_pre_ffn, g_post_ffn,
              w_in, q_norm_g, k_norm_g, ret_decay_fwd, ret_decay_bwd, w_out, w_ffn_in, w_ffn_out):
    B, n_lat, _ = x.shape
    rows = n_lat // GRID_W
    cos, sin = axial_rope(rows)
    for layer in range(DEPTH):
        mod_x = (jax.nn.silu(c) @ w_mod[layer] + b_mod[layer])[:, None, :]
        mod_c = jax.nn.silu(c_ctx) @ w_mod[layer] + b_mod[layer]
        sh_m, sc_m, gt_m, sh_f, sc_f, gt_f = jnp.split(mod_x, N_MOD, axis=-1)
        csh_m, csc_m, cgt_m, csh_f, csc_f, cgt_f = jnp.split(mod_c, N_MOD, axis=-1)
        lg_f = -jnp.exp(ret_decay_fwd[layer].astype(jnp.float32))
        lg_b = -jnp.exp(ret_decay_bwd[layer].astype(jnp.float32))

        hx = modulate(rms_norm(x, g_pre_mix[layer]), sh_m, sc_m)
        hc = modulate(rms_norm(ctx, g_pre_mix[layer]), csh_m, csc_m)
        qa_x, ka_x, va_x, qr_x, kr_x, vr_x, gr_x = project(hx, w_in[layer], q_norm_g[layer], k_norm_g[layer])
        qa_c, ka_c, va_c, qr_c, kr_c, vr_c, gr_c = project(hc, w_in[layer], q_norm_g[layer], k_norm_g[layer])

        zero_state = jnp.zeros((B, RET_HEADS, HEAD_DIM, HEAD_DIM), jnp.float32)
        ret_c, st_f, st_b = bidir_retention(qr_c, kr_c, vr_c, lg_f, lg_b, zero_state, zero_state)

        att_x = latent_attention(apply_rope(qa_x, cos, sin), apply_rope(ka_x, cos, sin), va_x, ka_c, va_c)
        ret_x, _, _ = bidir_retention(apply_rope(qr_x, cos, sin), apply_rope(kr_x, cos, sin), vr_x,
                                      lg_f, lg_b, st_f, st_b)
        mix_x = merge_heads(att_x, ret_x, gr_x, w_out[layer])
        x_new = x + gt_m * rms_norm(mix_x, g_post_mix[layer])
        hf = modulate(rms_norm(x_new, g_pre_ffn[layer]), sh_f, sc_f)
        x_new = x_new + gt_f * rms_norm(swiglu(hf, w_ffn_in[layer], w_ffn_out[layer]), g_post_ffn[layer])

        if layer < DEPTH - 1:
            att_c = gqa_block(qa_c, ka_c, va_c)
            mix_c = merge_heads(att_c, ret_c, gr_c, w_out[layer])
            ctx = ctx + cgt_m * rms_norm(mix_c, g_post_mix[layer])
            hfc = modulate(rms_norm(ctx, g_pre_ffn[layer]), csh_f, csc_f)
            ctx = ctx + cgt_f * rms_norm(swiglu(hfc, w_ffn_in[layer], w_ffn_out[layer]), g_post_ffn[layer])
        x = x_new
    return x


N_MIXERS = 2
N_HY_LAYERS = (DEPTH + N_MIXERS - 1) // N_MIXERS
N_ML_LAYERS = DEPTH // N_MIXERS
SHORT_W = 3

HY_EMB_BANDS = 16
HY_EMB_DIM = 1 + 2 * HY_EMB_BANDS
HY_FILTER_WIDTH = 64
HY_MAX_DECAY = math.log(1e-2) / 0.3
HY_MIN_DECAY = math.log(1e-2) / 1.5

ML_INNER = 2 * D_MODEL
ML_HEADS = 4
ML_HEAD_DIM = ML_INNER // ML_HEADS
ML_QKV_BLOCK = 4
ML_N_BLOCKS = ML_INNER // ML_QKV_BLOCK
ML_CHUNK = 128
ML_NORM_EPS = 1e-5

FFN_HIDDEN_2 = 2816


def _f32(a):
    return a.astype(jnp.float32)

def rmsnorm(x, g):
    x32 = _f32(x)
    y = x32 * lax.rsqrt(jnp.mean(x32 * x32, axis=-1, keepdims=True) + EPS)
    return (y * _f32(g)).astype(x.dtype)

def modulate_2(h, shift, scale):
    return h * (1.0 + scale) + shift

def adaln_params(cond, w, b):
    mod = jax.nn.silu(cond) @ w + b
    return jnp.split(mod[..., None, :], 6, axis=-1)

def short_conv(x, w, b):
    xp = jnp.pad(x, ((0, 0), (1, 1), (0, 0)))
    return w[0] * xp[:, :-2] + w[1] * xp[:, 1:-1] + w[2] * xp[:, 2:] + b

def grid_dwconv(x, w, b, rows, cols):
    B, L, C = x.shape
    img = x.reshape(B, rows, cols, C)
    y = lax.conv_general_dilated(img, w.astype(x.dtype)[:, :, None, :], window_strides=(1, 1),
                                 padding='SAME', dimension_numbers=('NHWC', 'HWIO', 'NHWC'),
                                 feature_group_count=C)
    return y.reshape(B, L, C) + b

def conv_ffn(u, w_up, conv_w, conv_b, w_down, rows, cols):
    a, g = jnp.split(u @ w_up, 2, axis=-1)
    g = grid_dwconv(g, conv_w, conv_b, rows, cols)
    return (jax.nn.silu(g) * a) @ w_down

def hyena_filters(L, f_w1, f_b1, f_w2, f_b2, f_w3, f_b3, f_wout, freq):
    t = jnp.linspace(0.0, 1.0, L, dtype=jnp.float32)[:, None]
    w = 2.0 * math.pi * jnp.arange(L, dtype=jnp.float32)[:, None] / L
    bands = jnp.linspace(1e-4, HY_EMB_BANDS - 1, HY_EMB_BANDS, dtype=jnp.float32)[None, :]
    pos = jnp.concatenate([t, jnp.cos(bands * w), -jnp.sin(bands * w)], axis=-1)
    fr = _f32(freq)
    h = jnp.sin(fr * (pos @ _f32(f_w1) + _f32(f_b1)))
    h = jnp.sin(fr * (h @ _f32(f_w2) + _f32(f_b2)))
    h = jnp.sin(fr * (h @ _f32(f_w3) + _f32(f_b3)))
    h = (h @ _f32(f_wout)).reshape(L, 2, D_MODEL)
    deltas = jnp.linspace(HY_MIN_DECAY, HY_MAX_DECAY, D_MODEL, dtype=jnp.float32)
    h = h * jnp.exp(-t * jnp.abs(deltas))[:, None, :]
    kern = jnp.concatenate([h[:, 0], jnp.zeros((1, D_MODEL), jnp.float32), h[:0:-1, 1]], axis=0)
    return kern / jnp.sum(jnp.abs(kern), axis=0, keepdims=True)

def hyena_mix(u, p):
    (w_in, b_in, sc_w, sc_b, f_w1, f_b1, f_w2, f_b2, f_w3, f_b3, f_wout, freq,
     bias, w_out, b_out) = p
    L = u.shape[1]
    proj = short_conv(u @ w_in + b_in, sc_w, sc_b)
    x0, x1, v = jnp.split(proj, 3, axis=-1)
    kern = hyena_filters(L, f_w1, f_b1, f_w2, f_b2, f_w3, f_b3, f_wout, freq)
    z = _f32(x1 * v)
    y = jnp.fft.irfft(jnp.fft.rfft(z, n=2 * L, axis=1) * jnp.fft.rfft(kern, n=2 * L, axis=0)[None],
                      n=2 * L, axis=1)[:, :L]
    y = (y + z * _f32(bias)).astype(u.dtype)
    return (x0 * y) @ w_out + b_out

def headwise(a, w):
    B, L, _ = a.shape
    out = jnp.einsum('blnc,nce->blne', a.reshape(B, L, ML_N_BLOCKS, ML_QKV_BLOCK), w)
    return out.reshape(B, L, ML_INNER)

def to_heads(a):
    B, L, _ = a.shape
    return _f32(a).reshape(B, L, ML_HEADS, ML_HEAD_DIM).transpose(0, 2, 1, 3)

def mlstm_chunkwise(q, k, v, ig, lf, state):
    B, H, L, dh = q.shape
    nc = L // ML_CHUNK

    def chunks(a):
        return jnp.moveaxis(a.reshape(B, H, nc, ML_CHUNK, *a.shape[3:]), 2, 0)

    lower = jnp.tril(jnp.ones((ML_CHUNK, ML_CHUNK), dtype=bool))

    def step(carry, xs):
        C, n, m = carry
        qc, kc, vc, igc, lfc = xs
        b = jnp.cumsum(lfc, axis=-1)
        a_inter = b + m[..., None]
        d = jnp.where(lower, b[..., :, None] - b[..., None, :] + igc[..., None, :], -jnp.inf)
        m_row = jnp.maximum(a_inter, jnp.max(d, axis=-1))
        w_inter = jnp.exp(a_inter - m_row)
        s = jnp.einsum('bhid,bhjd->bhij', qc, kc) * jnp.exp(d - m_row[..., None])
        num = (w_inter[..., None] * jnp.einsum('bhed,bhid->bhie', C, qc)
               + jnp.einsum('bhij,bhje->bhie', s, vc))
        den = w_inter * jnp.einsum('bhd,bhid->bhi', n, qc) + jnp.sum(s, axis=-1)
        h = num / jnp.maximum(jnp.abs(den), jnp.exp(-m_row))[..., None]
        b_last = b[..., -1]
        e = b_last[..., None] - b + igc
        m_new = jnp.maximum(b_last + m, jnp.max(e, axis=-1))
        g_old = jnp.exp(b_last + m - m_new)
        w_new = jnp.exp(e - m_new[..., None])
        C_new = g_old[..., None, None] * C + jnp.einsum('bhje,bhjd->bhed', vc * w_new[..., None], kc)
        n_new = g_old[..., None] * n + jnp.einsum('bhj,bhjd->bhd', w_new, kc)
        return (C_new, n_new, m_new), h

    state, h = lax.scan(step, state, (chunks(q), chunks(k), chunks(v), chunks(ig), chunks(lf)))
    return jnp.moveaxis(h, 0, 2).reshape(B, H, L, dh), state

def mlstm_final_state(k, v, ig, lf):
    b = jnp.cumsum(lf, axis=-1)
    b_last = b[..., -1]
    e = b_last[..., None] - b + ig
    m = jnp.maximum(b_last, jnp.max(e, axis=-1))
    w = jnp.exp(e - m[..., None])
    return (jnp.einsum('bhje,bhjd->bhed', v * w[..., None], k),
            jnp.einsum('bhj,bhjd->bhd', w, k), m)

def mlstm_prep(u, w_in, conv_w, conv_b, wq, wk, wv, w_gate, b_gate):
    B, L, _ = u.shape
    xm, z = jnp.split(u @ w_in, 2, axis=-1)
    xc = jax.nn.silu(short_conv(xm, conv_w, conv_b))
    q = headwise(xc, wq)
    k = headwise(xc, wk)
    v = headwise(xm, wv)
    gates = (q @ w_gate[:ML_INNER] + k @ w_gate[ML_INNER:2 * ML_INNER]
             + v @ w_gate[2 * ML_INNER:] + b_gate)
    gates = jnp.transpose(_f32(gates).reshape(B, L, 2, 2, ML_HEADS), (2, 3, 0, 4, 1))
    ig = gates[:, 0]
    lf = jax.nn.log_sigmoid(gates[:, 1])
    return to_heads(q), to_heads(k) * (ML_HEAD_DIM ** -0.5), to_heads(v), ig, lf, xc, z

def mlstm_out(h, xc, z, norm_w, skip, w_down):
    B, H, L, dh = h.shape
    mu = jnp.mean(h, axis=-1, keepdims=True)
    var = jnp.mean(jnp.square(h - mu), axis=-1, keepdims=True)
    hn = ((h - mu) * lax.rsqrt(var + ML_NORM_EPS)).transpose(0, 2, 1, 3).reshape(B, L, H * dh)
    hs = (hn * _f32(norm_w)).astype(xc.dtype) + skip * xc
    return (hs * jax.nn.silu(z)) @ w_down

def mlstm_mix(u_lat, u_ctx, p, need_ctx):
    w_in, conv_w, conv_b, wq, wk, wv, w_gate, b_gate, norm_w, skip, w_down = p

    def prep(u):
        return mlstm_prep(u, w_in, conv_w, conv_b, wq, wk, wv, w_gate, b_gate)

    def flip(a):
        return jnp.flip(a, axis=2)

    q, k, v, ig, lf, xc, z = prep(u_lat)
    qc, kc, vc, igc, lfc, xcc, zc = prep(u_ctx)
    if need_ctx:
        B = u_ctx.shape[0]
        zero = (jnp.zeros((B, ML_HEADS, ML_HEAD_DIM, ML_HEAD_DIM), jnp.float32),
                jnp.zeros((B, ML_HEADS, ML_HEAD_DIM), jnp.float32),
                jnp.zeros((B, ML_HEADS), jnp.float32))
        hcf, st_f = mlstm_chunkwise(qc, kc, vc, igc[0], lfc[0], zero)
        hcb, st_b = mlstm_chunkwise(flip(qc), flip(kc), flip(vc), flip(igc[1]), flip(lfc[1]), zero)
        y_ctx = mlstm_out(hcf + flip(hcb), xcc, zc, norm_w, skip, w_down)
    else:
        st_f = mlstm_final_state(kc, vc, igc[0], lfc[0])
        st_b = mlstm_final_state(flip(kc), flip(vc), flip(igc[1]), flip(lfc[1]))
        y_ctx = None
    hf, _ = mlstm_chunkwise(q, k, v, ig[0], lf[0], st_f)
    hb, _ = mlstm_chunkwise(flip(q), flip(k), flip(v), flip(ig[1]), flip(lf[1]), st_b)
    y_lat = mlstm_out(hf + flip(hb), xc, z, norm_w, skip, w_down)
    return y_lat, y_ctx

def second_inputs(seed: int = 0) -> dict:
    key = jax.random.key(seed)
    keys = iter(jax.random.split(key, 48))

    def nrm(shape, scale):
        return jax.random.normal(next(keys), shape, dtype=jnp.float32) * scale

    D, NH, NM = D_MODEL, N_HY_LAYERS, N_ML_LAYERS
    fb = jnp.linspace(3.0, 6.0, ML_HEADS, dtype=jnp.float32)
    ml_b_gate = jnp.stack([nrm((NM, 2, ML_HEADS), 0.1), fb + nrm((NM, 2, ML_HEADS), 0.1)],
                          axis=2).reshape(NM, 4 * ML_HEADS)
    return {
        'x': nrm((BATCH, SEQ, D), 1.0),
        'c': nrm((BATCH, D), 1.0),
        'ctx': nrm((BATCH, CTX_LEN, D), 1.0),
        'c_ctx': nrm((D,), 1.0),
        'mod_w': nrm((DEPTH, D, 6 * D), 0.5 * D ** -0.5),
        'mod_b': nrm((DEPTH, 6 * D), 0.02),
        'norm_g': 1.0 + nrm((DEPTH, 2, D), 0.02),
        'final_g': 1.0 + nrm((D,), 0.02),
        'hy_w_in': nrm((NH, D, 3 * D), D ** -0.5),
        'hy_b_in': nrm((NH, 3 * D), 0.02),
        'hy_sc_w': nrm((NH, SHORT_W, 3 * D), SHORT_W ** -0.5),
        'hy_sc_b': nrm((NH, 3 * D), 0.02),
        'hy_f_w1': nrm((NH, HY_EMB_DIM, HY_FILTER_WIDTH), HY_EMB_DIM ** -0.5),
        'hy_f_b1': nrm((NH, HY_FILTER_WIDTH), 0.1),
        'hy_f_w2': nrm((NH, HY_FILTER_WIDTH, HY_FILTER_WIDTH), HY_FILTER_WIDTH ** -0.5),
        'hy_f_b2': nrm((NH, HY_FILTER_WIDTH), 0.1),
        'hy_f_w3': nrm((NH, HY_FILTER_WIDTH, HY_FILTER_WIDTH), HY_FILTER_WIDTH ** -0.5),
        'hy_f_b3': nrm((NH, HY_FILTER_WIDTH), 0.1),
        'hy_f_wout': nrm((NH, HY_FILTER_WIDTH, 2 * D), HY_FILTER_WIDTH ** -0.5),
        'hy_freq': 1.0 + nrm((NH, HY_FILTER_WIDTH), 0.1),
        'hy_bias': nrm((NH, D), 0.2),
        'hy_w_out': nrm((NH, D, D), D ** -0.5),
        'hy_b_out': nrm((NH, D), 0.02),
        'ml_w_in': nrm((NM, D, 2 * ML_INNER), D ** -0.5),
        'ml_conv_w': nrm((NM, SHORT_W, ML_INNER), SHORT_W ** -0.5),
        'ml_conv_b': nrm((NM, ML_INNER), 0.02),
        'ml_wq': nrm((NM, ML_N_BLOCKS, ML_QKV_BLOCK, ML_QKV_BLOCK), ML_QKV_BLOCK ** -0.5),
        'ml_wk': nrm((NM, ML_N_BLOCKS, ML_QKV_BLOCK, ML_QKV_BLOCK), ML_QKV_BLOCK ** -0.5),
        'ml_wv': nrm((NM, ML_N_BLOCKS, ML_QKV_BLOCK, ML_QKV_BLOCK), ML_QKV_BLOCK ** -0.5),
        'ml_w_gate': nrm((NM, 3 * ML_INNER, 4 * ML_HEADS), 0.1 * (3 * ML_INNER) ** -0.5),
        'ml_b_gate': ml_b_gate,
        'ml_norm_w': 1.0 + nrm((NM, ML_INNER), 0.02),
        'ml_skip': 1.0 + nrm((NM, ML_INNER), 0.02),
        'ml_w_down': nrm((NM, ML_INNER, D), ML_INNER ** -0.5),
        'ffn_w_up': nrm((DEPTH, D, 2 * FFN_HIDDEN_2), D ** -0.5),
        'ffn_conv_w': nrm((DEPTH, 3, 3, FFN_HIDDEN_2), 1.0 / 3.0),
        'ffn_conv_b': nrm((DEPTH, FFN_HIDDEN_2), 0.02),
        'ffn_w_down': nrm((DEPTH, FFN_HIDDEN_2, D), FFN_HIDDEN_2 ** -0.5),
    }

def second_block(x, c, ctx, c_ctx, mod_w, mod_b, norm_g, final_g,
              hy_w_in, hy_b_in, hy_sc_w, hy_sc_b, hy_f_w1, hy_f_b1, hy_f_w2, hy_f_b2,
              hy_f_w3, hy_f_b3, hy_f_wout, hy_freq, hy_bias, hy_w_out, hy_b_out,
              ml_w_in, ml_conv_w, ml_conv_b, ml_wq, ml_wk, ml_wv, ml_w_gate, ml_b_gate,
              ml_norm_w, ml_skip, ml_w_down,
              ffn_w_up, ffn_conv_w, ffn_conv_b, ffn_w_down):
    rows = x.shape[1] // GRID_W
    ctx_len = ctx.shape[1]
    hy_params = (hy_w_in, hy_b_in, hy_sc_w, hy_sc_b, hy_f_w1, hy_f_b1, hy_f_w2, hy_f_b2,
                 hy_f_w3, hy_f_b3, hy_f_wout, hy_freq, hy_bias, hy_w_out, hy_b_out)
    ml_params = (ml_w_in, ml_conv_w, ml_conv_b, ml_wq, ml_wk, ml_wv, ml_w_gate, ml_b_gate,
                 ml_norm_w, ml_skip, ml_w_down)
    for i in range(DEPTH):
        last = i == DEPTH - 1
        sh1, sc1, g1, sh2, sc2, g2 = adaln_params(c, mod_w[i], mod_b[i])
        csh1, csc1, cg1, csh2, csc2, cg2 = adaln_params(c_ctx, mod_w[i], mod_b[i])
        h_lat = modulate_2(rmsnorm(x, norm_g[i, 0]), sh1, sc1)
        h_ctx = modulate_2(rmsnorm(ctx, norm_g[i, 0]), csh1, csc1)
        j = i // N_MIXERS
        if i % N_MIXERS == 0:
            p = tuple(a[j] for a in hy_params)
            y_lat = hyena_mix(h_lat, p)
            y_ctx = None if last else hyena_mix(h_ctx, p)
        else:
            p = tuple(a[j] for a in ml_params)
            y_lat, y_ctx = mlstm_mix(h_lat, h_ctx, p, not last)
        x = x + g1 * y_lat
        ffn_p = (ffn_w_up[i], ffn_conv_w[i], ffn_conv_b[i], ffn_w_down[i])
        x = x + g2 * conv_ffn(modulate_2(rmsnorm(x, norm_g[i, 1]), sh2, sc2), *ffn_p, rows, GRID_W)
        if not last:
            ctx = ctx + cg1 * y_ctx
            ctx = ctx + cg2 * conv_ffn(modulate_2(rmsnorm(ctx, norm_g[i, 1]), csh2, csc2),
                                       *ffn_p, 1, ctx_len)
    return rmsnorm(x, final_g)


def setup_inputs(seed=0):
    out = dict(first_inputs(seed))
    for name, value in second_inputs(seed + 1).items():
        if name != "x":
            out[name + "_2"] = value
    return out


def reference(
    x, c, ctx, c_ctx, w_mod, b_mod, g_pre_mix, g_post_mix, g_pre_ffn, g_post_ffn, w_in,
    q_norm_g, k_norm_g, ret_decay_fwd, ret_decay_bwd, w_out, w_ffn_in, w_ffn_out, c_2, ctx_2,
    c_ctx_2, mod_w_2, mod_b_2, norm_g_2, final_g_2, hy_w_in_2, hy_b_in_2, hy_sc_w_2, hy_sc_b_2,
    hy_f_w1_2, hy_f_b1_2, hy_f_w2_2, hy_f_b2_2, hy_f_w3_2, hy_f_b3_2, hy_f_wout_2, hy_freq_2,
    hy_bias_2, hy_w_out_2, hy_b_out_2, ml_w_in_2, ml_conv_w_2, ml_conv_b_2, ml_wq_2, ml_wk_2,
    ml_wv_2, ml_w_gate_2, ml_b_gate_2, ml_norm_w_2, ml_skip_2, ml_w_down_2, ffn_w_up_2,
    ffn_conv_w_2, ffn_conv_b_2, ffn_w_down_2,
):
    x = first_block(
        x, c, ctx, c_ctx, w_mod, b_mod, g_pre_mix, g_post_mix, g_pre_ffn, g_post_ffn, w_in,
        q_norm_g, k_norm_g, ret_decay_fwd, ret_decay_bwd, w_out, w_ffn_in, w_ffn_out,
    )
    return second_block(
        x, c_2, ctx_2, c_ctx_2, mod_w_2, mod_b_2, norm_g_2, final_g_2, hy_w_in_2, hy_b_in_2,
        hy_sc_w_2, hy_sc_b_2, hy_f_w1_2, hy_f_b1_2, hy_f_w2_2, hy_f_b2_2, hy_f_w3_2, hy_f_b3_2,
        hy_f_wout_2, hy_freq_2, hy_bias_2, hy_w_out_2, hy_b_out_2, ml_w_in_2, ml_conv_w_2,
        ml_conv_b_2, ml_wq_2, ml_wk_2, ml_wv_2, ml_w_gate_2, ml_b_gate_2, ml_norm_w_2,
        ml_skip_2, ml_w_down_2, ffn_w_up_2, ffn_conv_w_2, ffn_conv_b_2, ffn_w_down_2,
    )


_drawn_inputs = setup_inputs


def setup_inputs(seed=0):
    import zlib

    import numpy as np

    out = dict(_drawn_inputs(seed))
    spreads = {}
    factors = {'g_post_mix': 3.685,
     'g_pre_ffn': 2.929,
     'g_post_ffn': 3.753,
     'q_norm_g': 8.0,
     'k_norm_g': 8.0,
     'mod_b_2': 3.708,
     'norm_g_2': 8.0,
     'final_g_2': 19.845,
     'hy_b_in_2': 8.0,
     'hy_sc_b_2': 8.0,
     'hy_f_b1_2': 8.0,
     'hy_f_b2_2': 8.0,
     'hy_f_b3_2': 7.363,
     'hy_freq_2': 8.0,
     'hy_b_out_2': 200.0,
     'ffn_conv_b_2': 58.98}
    for name, (base, spread) in spreads.items():
        noise = np.random.default_rng([zlib.crc32(name.encode()), seed]).standard_normal(out[name].shape)
        drawn = base * np.exp(spread * noise) if base else spread * noise
        out[name] = jnp.asarray(drawn.astype(out[name].dtype))
    for name, factor in factors.items():
        out[name] = (out[name] * factor).astype(out[name].dtype)
    return out
```

```python
from contextlib import ExitStack

import numpy as np

import concourse.bass as bass
from concourse import mybir

F32 = mybir.dt.float32
F32R = mybir.dt.float32r
ALU = mybir.AluOpType
ACT = mybir.ActivationFunctionType

P = 128
D = 1024
KT = D // P
L = 512
LC = 256
LA = L + LC
HD = 64
HALF = HD // 2
NPAIR = 4
FFN = 2816
FT = FFN // P
NCHUNK = 6
MODU = NCHUNK * KT
GRID_W = 64
ROWS = L // GRID_W
HYF = 64
BANDS = 16
EPS = 1e-6
TWO_PI = 2.0 * np.pi
PI_A = 6.28125
PI_B = float(np.float32(np.round((TWO_PI - PI_A) * 2**21) / 2**21))
PI_C = float(np.float32(TWO_PI - PI_A - PI_B))
PI_SAFE = float(np.nextafter(np.float32(np.pi), np.float32(0)))
MAGIC = 1.5 * 2.0**23
DIST = L + 3 * P
CDIST = L + P

COLS = [("g_pre_mix", KT), ("g_post_mix", KT), ("g_pre_ffn", KT), ("g_post_ffn", KT),
        ("b_mod", 2 * MODU), ("b_mod2", MODU), ("g_hy", KT), ("g_ffn2", KT), ("g_final", KT),
        ("hy_b_in", 3 * KT), ("hy_sc_w", 9 * KT), ("hy_sc_b", 3 * KT), ("hy_bias", KT), ("hy_b_out", KT),
        ("conv_w", 9 * FT), ("conv_b", FT), ("q_g", 1), ("k_g", 1), ("dec_f", 8), ("dec_b", 8),
        ("freq", 1), ("fb1", 1), ("fb2", 1), ("fb3", 1), ("eps", 1), ("not_first", 1), ("c", 3 * KT)]
COL = {}
NCOL = 0
for _name, _w in COLS:
    COL[_name] = NCOL
    NCOL += _w
DERS = [("mod", 2 * MODU), ("mod2", MODU), ("a_mix", KT), ("a_ctx", KT), ("p_mix", KT), ("a_ffn", KT),
        ("p_ffn", KT), ("a_hy", KT), ("p_hy", KT), ("a_ffn2", KT), ("silu_c", 3 * KT), ("lg_f", 8), ("lg_b", 8),
        ("fb", 3), ("inv_norm", KT)]
DER = {}
NDER = 0
for _name, _w in DERS:
    DER[_name] = NDER
    NDER += _w

U1 = KT * P
U2 = FFN // 2
FH = FT // 2
PHASES = [("mod_a", 16, U1, False), ("w_in", 22, U1, True), ("mod_b", 2 * MODU - 16, U1, False),
          ("w_out", 8, U1, True), ("ffn_in", 2 * FT, U1, True), ("ffn_out", 16, U2, True),
          ("hy_in", 24, U1, True), ("hy_out", 8, U1, True), ("up", 2 * FT, U1, True), ("down", 16, U2, True)]
RAW = 4
START, ORD, NUNIT, WIDTH = {}, {}, {}, {}
_g, _o = 0, {True: 0, False: 0}
for _name, _n, _w, _s in PHASES:
    START[_name], ORD[_name], NUNIT[_name], WIDTH[_name] = _g, _o[_s], _n, _w
    _g += _n
    _o[_s] += _n
    assert _name == "mod_a" or _s is False or START[_name] % RAW == ORD[_name] % RAW
KIND = [(s, ORD[name] + i) for name, n, w, s in PHASES for i in range(n)]


class Own:

    def __init__(self, eng, sem):
        self.eng, self.sem, self.n, self.i, self.per = eng, sem, 0, None, 0

    def __call__(self, ins):
        ins.then_inc(self.sem, 1)
        self.n += 1
        self.eng.wait_ge(self.sem, self.n if self.i is None else self.base + self.i * self.per + (self.n - self.base))

    def enter(self, i, per):
        self.base, self.i, self.per = self.n, i, per

    def leave(self, times):
        assert self.n - self.base == self.per, (self.n - self.base, self.per)
        self.n = self.base + times * self.per
        self.i = None


def build(nc, xT, ctxT, cols, mats, w, rope, dist, posT, fw, fwout, decay, fwd, inv, out):
    def sb(name, at, shape, dt=F32):
        return nc.alloc_sbuf_tensor_at(name, shape, dt, offset=BASE + at)

    with ExitStack() as stack:
        BASE = (nc.sbuf_base + 63) // 64 * 64
        K = 1024
        COLB = 3712
        colt = sb("colt", 0, [P, NCOL])
        o_der = (NCOL * 4 + 63) // 64 * 64
        dert = sb("dert", o_der, [P, NDER])
        assert o_der + NDER * 4 <= COLB
        feat = sb("feat", COLB, [HYF, L])
        o_mat = COLB + 2 * K
        ones = sb("ones", o_mat, [P, P])
        bones = sb("bones", o_mat + 512, [P, P])
        swap = sb("swap", o_mat + 1024, [P, P])
        ident = sb("ident", o_mat + 1536, [P, P])
        o_x = o_mat + 2 * K
        X = sb("X", o_x, [P, KT, L])
        o_raw = o_x + 16 * K
        wraw = sb("wraw", o_raw, [P, RAW, U2])
        o_ws = o_raw + RAW * U2 * 4
        wsp = sb("wsp", o_ws, [P, 2, 2, U2], F32R)
        o_t = o_ws + 4 * U2 * 4
        o_h = o_t + 20 * K
        H = sb("H", o_h, [P, 2, KT, L], F32R)
        Y = sb("Y", o_h, [P, KT, L])
        o_r = o_h + 32 * K
        assert BASE + o_r + 88 * K <= nc.sbuf_usable_end, (BASE + o_r + 88 * K, nc.sbuf_usable_end)
        sqb = sb("sqb", o_t, [P, 2, L])
        rstd = sb("rstd", o_t + 4 * K, [P, L])
        tb = sb("tb", o_t + 6 * K, [P, 2, L])
        val = sb("val", o_t + 10 * K, [P, 2, L])
        acc = sb("acc", o_t + 14 * K, [P, L])
        rtmp = sb("rtmp", o_t + 16 * K, [P, L])
        posb = sb("posb", o_r + 40 * K, [2 * BANDS + 1, L])
        fwb = sb("fwb", o_r + 42 * K, [HYF, 3, HYF])
        fa = sb("fa", o_r + 44 * K, [HYF, L])
        fk = sb("fk", o_r + 46 * K, [HYF, L])
        fh = sb("fh", o_r + 48 * K, [HYF, L])
        Hc = sb("Hc", o_r, [P, 2, KT, LC], F32R)
        Xc = sb("Xc", o_r + 16 * K, [P, KT, LC])
        V = sb("V", o_r + 16 * K, [P, LA // P, 5 * P])
        ropet = sb("ropet", o_r + 31 * K, [P, 2, L])
        KA = sb("KA", o_r + 35 * K, [P, LA])
        KR = sb("KR", o_r + 38 * K, [P, NPAIR, LA])
        QA = sb("QA", o_r + 50 * K, [P, NPAIR, L])
        QR = sb("QR", o_r + 58 * K, [P, NPAIR, L])
        G = sb("G", o_r + 66 * K, [P, NPAIR, L])
        VT = sb("VT", o_t, [P, 2, LA])
        RU = sb("RU", o_t + 6 * K, [P, 2, LA])
        SQ = sb("SQ", o_t + 12 * K, [P, LA])
        RT = sb("RT", o_t + 15 * K, [P, LA])
        RM = sb("RM", o_t + 18 * K, [P, L])
        Pb = sb("Pb", o_r + 74 * K, [P, 2, LA])
        PT = sb("PT", o_r + 80 * K, [P, 2, LA])
        strip = sb("strip", o_r, [P, 2, DIST + CDIST])
        ea = sb("ea", o_r + 12 * K, [P, DIST])
        ec = sb("ec", o_r + 31 * K, [P, CDIST])
        smx = sb("smx", o_r + 86 * K, [P, 2])
        mxr = sb("mxr", o_r + 86 * K + 128, [P, 2])
        rinv = sb("rinv", o_r + 86 * K + 192, [P, 2])
        rsum = sb("rsum", o_r + 86 * K + 64, [P, 2])
        distt = sb("distt", o_t, [P, 3 * DIST + 2 * CDIST])
        pr = sb("pr", o_t + (3 * DIST + 2 * CDIST) * 4, [P, 2, L])
        assert (3 * DIST + 2 * CDIST) * 4 + 4 * K <= 20 * K
        Ym = sb("Ym", o_r, [P, KT, L])
        hid = sb("hid", o_r, [P, 2, FT, L], F32R)
        sl = sb("sl", o_t, [P, 2, L])
        hv = sb("hv", o_t + 4 * K, [P, 2, L])
        PW = GRID_W + 2
        gb = sb("gb", o_t + 8 * K, [P, 2, ROWS + 2, PW])
        cva = sb("cva", o_t + 14 * K, [P, 2, ROWS, GRID_W])
        fwdt = sb("fwdt", o_r, [P, 4, 2, 256])
        invt = sb("invt", o_r + 8 * K, [P, 4, 2, 256])
        dect = sb("dect", o_r + 8 * K, [P, 2, D])
        KS = sb("KS", o_r + 16 * K, [P, 2, 2, 4, 512])
        Z = sb("Z", o_r + 48 * K, [P, KT, L])
        X0 = sb("X0", o_r + 64 * K, [P, KT, L])
        HP = sb("HP", o_r + 48 * K, [P, 4, D])
        HM = sb("HM", o_r + 64 * K, [P, 4, D])
        fwo = sb("fwo", o_r + 80 * K, [HYF, 2 * D])
        fA = sb("fA", o_r + 16 * K, [P, 2, 512])
        fB = sb("fB", o_r + 20 * K, [P, 2, 512])
        aab = sb("aab", o_r + 24 * K, [P, 2, 2, 512])
        kE = sb("kE", o_r + 8 * K, [P, 2, 512])
        absum = sb("absum", o_r + 44 * K, [P, D])
        cb_ = sb("cb_", o_t, [P, 2, L + 2])
        ca = sb("ca", o_t + 5 * K, [P, 2, L])
        x1c = sb("x1c", o_t + 9 * K, [P, L])
        zN = sb("zN", o_h, [P, 4, D])
        zs = sb("zs", o_h + 16 * K, [P, 8, 512])
        zE = sb("zE", o_t, [P, 2, 512])
        zpD = sb("zpD", o_t + 4 * K, [P, 3, 512])
        zpP = sb("zpP", o_t + 10 * K, [P, 3, 512])
        row = sb("row", o_t + 16 * K, [1, 2, 512])
        yt = sb("yt", o_t, [P, 2, L])
        yv = sb("yv", o_t + 4 * K, [P, 2, L])
        hyt = sb("hyt", o_t + 16 * K, [P, 2, L])
        cen = sb("cen", o_t, [P, 2, L])
        gsq = sb("gsq", o_t + 4 * K, [P, 2, L])
        grs = sb("grs", o_t + 8 * K, [P, L])
        gv = sb("gv", o_t + 10 * K, [P, 2, L])

        PS = stack.enter_context(nc.psum_tensor("PS", [P, 8, 512], F32))

        def col(name, i=0, n=1):
            return colt[:, COL[name] + i:COL[name] + i + n]

        def der(name, i=0, n=1):
            return dert[:, DER[name] + i:DER[name] + i + n]

        def sem(name):
            return stack.enter_context(nc.semaphore(name))

        s_small = sem("s_small")
        s_feat = sem("s_feat")
        s_x = sem("s_x")
        s_xc = sem("s_xc")
        s_rope = sem("s_rope")
        s_dist = sem("s_dist")
        s_hyc = sem("s_hyc")
        s_dec = [sem(f"s_dec{i}") for i in range(2)]
        s_inv = sem("s_inv")
        s_out = sem("s_out")
        wload = [sem(f"wload{i}") for i in range(RAW)]
        w_hi = sem("w_hi")
        w_lo = sem("w_lo")
        w_done = sem("w_done")
        mod_done = sem("mod_done")
        s_act = sem("s_act")
        s_dve = sem("s_dve")
        s_pool = sem("s_pool")
        silu_c = sem("silu_c")
        f_mm, f_arg, f_sin = sem("f_mm"), sem("f_arg"), sem("f_sin")
        n_sq, n_acc, n_ss, n_rt = sem("n_sq"), sem("n_acc"), sem("n_ss"), sem("n_rt")
        n_rs, n_t, n_val, n_hi, n_h, n_x = sem("n_rs"), sem("n_t"), sem("n_val"), sem("n_hi"), sem("n_h"), sem("n_x")
        n_y = sem("n_y")
        m_cols = sem("m_cols")
        q_ev, q_sw, q_ss, q_rt, q_done, v_tr, v_ev = (sem("q_ev"), sem("q_sw"), sem("q_ss"), sem("q_rt"),
                                                      sem("q_done"), sem("v_tr"), sem("v_ev"))
        a_s, a_mx, a_exp, a_p, a_tr, a_pt, a_pv, a_o = (sem("a_s"), sem("a_mx"), sem("a_exp"), sem("a_p"),
                                                        sem("a_tr"), sem("a_pt"), sem("a_pv"), sem("a_o"))
        r_u, r_e, r_strip, r_s, r_p, r_pv, r_o = (sem("r_u"), sem("r_e"), sem("r_strip"), sem("r_s"), sem("r_p"),
                                                  sem("r_pv"), sem("r_o"))
        a_h = sem("a_h")
        g_c, g_sq, g_var, g_rt, g_y, g_h = (sem("g_c"), sem("g_sq"), sem("g_var"), sem("g_rt"), sem("g_y"),
                                            sem("g_h"))
        g_hi = sem("g_hi")
        h_sl, h_val, h_hi, h_lo, h_g, h_cv = (sem("h_sl"), sem("h_val"), sem("h_hi"), sem("h_lo"), sem("h_g"),
                                              sem("h_cv"))
        k_h, k_ab, k_hp, k_col, k_f, k_e, k_k = (sem("k_h"), sem("k_ab"), sem("k_hp"), sem("k_col"), sem("k_f"),
                                                 sem("k_e"), sem("k_k"))
        y_b, y_c, y_z, z_tr, z_n, z_f, z_e, z_b, z_q, z_y = (
            sem("y_b"), sem("y_c"), sem("y_z"), sem("z_tr"), sem("z_n"), sem("z_f"), sem("z_e"), sem("z_b"),
            sem("z_q"), sem("z_y"))
        i_mm, i_ev, i_val, i_hi, i_h = sem("i_mm"), sem("i_ev"), sem("i_val"), sem("i_hi"), sem("i_h")
        o_ev = sem("o_ev")
        z_p, z_w = sem("z_p"), sem("z_w")
        k_abs, k_sum = sem("k_abs"), sem("k_sum")
        m_lg, g_rs, g_val = sem("m_lg"), sem("g_rs"), sem("g_val")
        a_hi = sem("a_hi")

        block = stack.enter_context(nc.Block())

        NCTX = 10
        NV = 5
        NROPE = 13

        @block.sync
        def _(sp):
            def load(name, i, dst_slot, src):
                sp.dma_start(wraw[:, dst_slot, 0:WIDTH[name]], src).then_inc(wload[dst_slot], 16)

            def load_static(name, i):
                g = START[name] + i
                if g >= RAW:
                    split, ordinal = KIND[g - RAW]
                    sp.wait_ge(w_lo if split else mod_done, ordinal + 1)
                load(name, i, g % RAW, w[name][i])

            def load_loop(name, first, times):
                with sp.Fori(0, times) as i:
                    for u in range(RAW):
                        sp.wait_ge(w_lo, i * RAW + (ORD[name] + first + u - RAW + 1))
                        load(name, i, (START[name] + first + u) % RAW, w[name][i * RAW + (first + u)])

            sp.dma_start(colt[:, :], cols).then_inc(s_small, 16)
            sp.dma_start(posb[:, :], posT).then_inc(s_feat, 16)
            sp.dma_start(fwb[:, :, :], fw).then_inc(s_feat, 16)
            for j, m in enumerate((ones, bones, swap, ident)):
                sp.dma_start(m[:, :], mats[j]).then_inc(s_small, 16)
            for i in range(RAW):
                load_static("mod_a", i)
            sp.dma_start(X[:, :, :], xT).then_inc(s_x, 16)
            sp.dma_start(Xc[:, :, :], ctxT).then_inc(s_xc, 16)
            sp.dma_start(ropet[:, :, :], rope).then_inc(s_rope, 16)
            for i in range(RAW, 16):
                load_static("mod_a", i)
            for i in range(22):
                load_static("w_in", i)
            for i in range(RAW):
                load_static("mod_b", i)
            sp.wait_ge(q_done, NROPE)
            sp.wait_ge(v_ev, NV)
            sp.dma_start(distt[:, :], dist).then_inc(s_dist, 16)
            with sp.Fori(1, (2 * MODU - 16) // RAW) as i:
                for u in range(RAW):
                    sp.wait_ge(mod_done, i * RAW + (16 - RAW + u + 1))
                    load("mod_b", i, (START["mod_b"] + u) % RAW, w["mod_b"][i * RAW + u])
            for i in range(8):
                load_static("w_out", i)
            load_loop("ffn_in", 0, 2 * FT // RAW)
            load_loop("ffn_out", 0, 4)
            for i in range(RAW):
                load_static("hy_in", i)
            sp.wait_ge(w_done, ORD["hy_in"])
            sp.dma_start(fwo[:, :], fwout).then_inc(s_hyc, 16)
            sp.dma_start(dect[:, 0, :], decay[0]).then_inc(s_dec[0], 16)
            sp.dma_start(dect[:, 1, :], decay[1]).then_inc(s_dec[1], 16)
            sp.dma_start(fwdt[:, :, :, :], fwd).then_inc(s_hyc, 16)
            for t in range(2, 4):
                sp.wait_ge(k_ab, 2 * (t - 1))
                sp.dma_start(dect[:, t % 2, :], decay[t]).then_inc(s_dec[t % 2], 16)
            sp.wait_ge(k_k, 4)
            sp.dma_start(invt[:, :, :, :], inv).then_inc(s_inv, 16)
            load_loop("hy_in", RAW, 5)
            for i in range(8):
                load_static("hy_out", i)
            load_loop("up", 0, 2 * FT // RAW)
            load_loop("down", 0, 4)
            sp.wait_ge(n_val, 6 * KT)
            sp.dma_start(out, Y[:, :, :]).then_inc(s_out, 16)
            sp.wait_ge(s_out, 16)

        def split_hi(act, name, i, r=None):
            o, g, n = ORD[name] + i, START[name] + i, WIDTH[name]
            k = 0 if r is None else r
            act.wait_ge(wload[g % RAW], k * 16 + 16 * (g // RAW + 1))
            if o >= 2:
                act.wait_ge(w_done, k * RAW + (o - 1))
            nc.scalar.activation(wsp[:, o % 2, 0, 0:n], wraw[:, g % RAW, 0:n], ACT.Copy).then_inc(w_hi, 1)

        def split_lo(dve, name, i, r=None):
            o, g, n = ORD[name] + i, START[name] + i, WIDTH[name]
            k = 0 if r is None else r
            dve.wait_ge(w_hi, k * RAW + (o + 1))
            nc.vector.tensor_tensor(wsp[:, o % 2, 1, 0:n], wraw[:, g % RAW, 0:n],
                                    wsp[:, o % 2, 0, 0:n].bitcast(F32), ALU.subtract).then_inc(w_lo, 1)

        def split_matmuls(pe, o, psum, h, kts, wk0, first, last):
            mm = None
            for kt in kts:
                wk = kt - wk0
                for a, b in ((0, 0), (0, 1), (1, 0)):
                    mm = nc.tensor.matmul(psum, wsp[:, o % 2, a, wk * P:(wk + 1) * P], h[:, b, kt, :],
                                          start=first and kt == kts[0] and (a, b) == (0, 0),
                                          stop=last and kt == kts[-1] and (a, b) == (1, 0))
            return mm

        @block.tensor
        def _(pe):
            pe.wait_ge(s_feat, 32)
            pe.wait_ge(s_small, 80)
            for l in range(3):
                if l:
                    pe.wait_ge(f_sin, l)
                k = 2 * BANDS + 1 if l == 0 else HYF
                nc.tensor.matmul(PS[0:HYF, 6, :], fwb[0:k, l, :], posb[:, :] if l == 0 else fh[:, :],
                                 start=True, stop=True).then_inc(f_mm, 1)

            def modulation(m):
                g = m if m < 16 else START["mod_b"] + m - 16
                pe.wait_ge(wload[g % RAW], 16 * (g // RAW + 1))
                if m < MODU:
                    dst, a, b = PS[:, 7, 2 * m:2 * m + 2], 0, 2
                else:
                    dst, a, b = PS[:, 7, MODU + m:MODU + m + 1], 2, 3
                for kt in range(KT):
                    mm = nc.tensor.matmul(dst, wraw[:, g % RAW, kt * P:(kt + 1) * P],
                                          dert[:, DER["silu_c"] + 3 * kt + a:DER["silu_c"] + 3 * kt + b],
                                          start=kt == 0, stop=kt == KT - 1)
                mm.then_inc(mod_done, 1)

            def total(k, bank=6):
                pe.wait_ge(n_acc, KT * (k + 1))
                n = LC if k == 1 else L
                nc.tensor.matmul(PS[:, bank, 0:n], ones[:, :], acc[:, 0:n], start=True, stop=True).then_inc(n_ss, 1)

            pe.wait_ge(silu_c, 1)
            for m in range(8):
                modulation(m)
            pe.wait_ge(f_arg, 3)
            total(0)
            for m in range(8, 16):
                modulation(m)
            pe.wait_ge(n_rt, 1)
            total(1)

            def aux(n):
                if n < NV:
                    pe.wait_ge(q_ev, n + 1)
                    if n == 0:
                        pe.wait_ge(m_cols, 1)
                    else:
                        pe.wait_ge(v_ev, n)
                    for t in range(LA // P):
                        tr = nc.tensor.transpose(PS[:, 6 + t // 4, (t % 4) * P:(t % 4 + 1) * P],
                                                 VT[:, n % 2, t * P:(t + 1) * P], ident[:, :])
                    tr.then_inc(v_tr, 1)
                elif n < NV + NROPE:
                    pe.wait_ge(q_ev, n + 1)
                    pe.wait_ge(v_ev, NV)
                    if n > NV:
                        pe.wait_ge(q_done, n - NV)
                    nc.tensor.matmul(PS[:, 4, :], swap[:, :], RU[:, n % 2, 0:L], start=True, stop=True).then_inc(q_sw, 1)
                    if n == NV or 10 <= n < 14:
                        mm = nc.tensor.matmul(PS[:, 5, :], bones[:, :], SQ[:, 0:L], start=True, stop=True)
                        if n == NV:
                            mm = nc.tensor.matmul(PS[:, 6, 0:LC], bones[:, :], SQ[:, L:LA], start=True, stop=True)
                        mm.then_inc(q_ss, 1)

            for n in range(22):
                pe.wait_ge(w_lo, ORD["w_in"] + n + 1)
                if n >= 2:
                    pe.wait_ge(q_ev, n - 1)
                if n == 0:
                    pe.wait_ge(n_h, KT)
                mm = split_matmuls(pe, ORD["w_in"] + n, PS[:, n % 2, :], H, range(KT), 0, True, True)
                if n < NCTX:
                    if n == 0:
                        pe.wait_ge(n_h, 2 * KT)
                    mm = split_matmuls(pe, ORD["w_in"] + n, PS[:, 2 + n % 2, 0:LC], Hc, range(KT), 0, True, True)
                mm.then_inc(w_done, 1)
                if n:
                    aux(n - 1)

            def att_scores(s):
                t, lo, qt = s // 8, (s // 4) % 2 * HD, s % 4
                if s == 0:
                    pe.wait_ge(q_ev, 22)
                    pe.wait_ge(q_done, NROPE)
                else:
                    pe.wait_ge(a_exp, s)
                for a, b, bank in ((0, L, 0), (L, LA, 1)):
                    mm = nc.tensor.matmul(PS[:, bank, 0:b - a], QA[lo:lo + HD, t, qt * P:(qt + 1) * P],
                                          KA[lo:lo + HD, a:b], start=True, stop=True)
                mm.then_inc(a_s, 1)

            def att_transposes(s):
                pe.wait_ge(a_p, s + 1)
                if s:
                    pe.wait_ge(a_pt, s)
                for kt in range(LA // P):
                    tr = nc.tensor.transpose(PS[:, 2 + kt // 4, (kt % 4) * P:(kt % 4 + 1) * P],
                                             Pb[:, s % 2, kt * P:(kt + 1) * P], ident[:, :])
                tr.then_inc(a_tr, 1)

            def att_values(s):
                lo, qt = (s // 4) % 2 * HD, s % 4
                pe.wait_ge(a_pt, s + 1)
                if s % 8 == 0 and s:
                    pe.wait_ge(a_o, s // 8)
                for kt in range(LA // P):
                    mm = nc.tensor.matmul(PS[lo:lo + HD, 4, qt * P:(qt + 1) * P], V[:, kt, lo:lo + HD],
                                          PT[:, s % 2, kt * P:(kt + 1) * P], start=kt == 0, stop=kt == LA // P - 1)
                mm.then_inc(a_pv, 1)

            def ret_scores(r):
                h, kt = r // 6, r % 6
                lo = h % 2 * HD
                if r:
                    pe.wait_ge(r_p, r)
                nc.tensor.matmul(PS[:, 5, :], KR[lo:lo + HD, h // 2, kt * P:(kt + 1) * P],
                                 QR[lo:lo + HD, h // 2, :], start=True, stop=True).then_inc(r_s, 1)

            def ret_values(r):
                h, kt = r // 6, r % 6
                lo = h % 2 * HD
                pe.wait_ge(r_p, r + 1)
                if r % 12 == 0 and r:
                    pe.wait_ge(r_o, r // 12)
                nc.tensor.matmul(PS[lo:lo + HD, 6, :], V[:, kt, P + h * HD:P + (h + 1) * HD], pr[:, r % 2, :],
                                 start=kt == 0, stop=kt == 5).then_inc(r_pv, 1)

            m_next = 16
            for s in range(32):
                att_scores(s)
                if s:
                    att_values(s - 1)
                rs = range(s * 3 // 2, (s + 1) * 3 // 2)
                for r in rs:
                    ret_scores(r)
                    for m in range(m_next, min(m_next + (2 if len(rs) == 1 else 1), 2 * MODU)):
                        modulation(m)
                        m_next += 1
                    ret_values(r)
                if m_next < 2 * MODU:
                    modulation(m_next)
                    m_next += 1
                att_transposes(s)
            att_values(31)
            assert m_next == 2 * MODU

            pe.wait_ge(r_o, 4)
            for t in range(4):
                nc.tensor.matmul(PS[:, t, :], bones[:, :], QR[:, t, :], start=True, stop=True).then_inc(g_c, 1)
            for t in range(4):
                pe.wait_ge(g_sq, t + 1)
                nc.tensor.matmul(PS[:, t, :], bones[:, :], gsq[:, t % 2, :], start=True, stop=True).then_inc(g_var, 1)

            for n in range(8):
                pe.wait_ge(w_lo, ORD["w_out"] + n + 1)
                if n == 0:
                    pe.wait_ge(a_o, 4)
                    pe.wait_ge(g_h, 4)
                if n >= 2:
                    pe.wait_ge(n_y, n - 1)
                split_matmuls(pe, ORD["w_out"] + n, PS[:, n % 2, :], H, range(KT), 0, True, True).then_inc(w_done, 1)
            total(2)
            total(3)

            def pairs(name, normed, free_a, base_a, free_b, base_b):
                def four(i, first):
                    for u in range(4):
                        pe.wait_ge(w_lo, i * 4 + (ORD[name] + u + 1))
                        if not first:
                            free, base = (free_a, base_a) if u % 2 == 0 else (free_b, base_b)
                            pe.wait_ge(free, i * 2 + (base + u // 2 - 1))
                        elif u == 0:
                            pe.wait_ge(n_h, normed)
                        split_matmuls(pe, ORD[name] + u, PS[:, u, :], H, range(KT), 0, True,
                                      True).then_inc(w_done, 1)
                four(0, True)
                with pe.Fori(1, FT // 2) as i:
                    four(i, False)

            def down(name, base_h, free, base):
                def four(i, first):
                    for u in range(4):
                        pe.wait_ge(w_lo, i * 4 + (ORD[name] + u + 1))
                        if first and u == 0:
                            pe.wait_ge(h_lo, base_h + FT)
                        if not first and u % 2 == 0:
                            pe.wait_ge(free, i * 2 + (base + u // 2 - 1))
                        k0 = u % 2 * FH
                        split_matmuls(pe, ORD[name] + u, PS[:, u // 2, :], hid, range(k0, k0 + FH), k0, u % 2 == 0,
                                      u % 2 == 1).then_inc(w_done, 1)
                four(0, True)
                with pe.Fori(1, 4) as i:
                    four(i, False)

            pairs("ffn_in", 3 * KT, h_sl, 0, h_val, 0)
            down("ffn_out", 0, n_y, KT)

            total(4)
            pe.wait_ge(s_hyc, 32)
            for j in range(8):
                t, c = j // 2, j % 2
                par, mt = t // 2, t % 2
                if j:
                    pe.wait_ge(k_ab, j)
                for d in range(2):
                    mm = nc.tensor.matmul(PS[:, 4 + d, :], feat[:, mt * 256 + par:(mt + 1) * 256:2],
                                          fwo[:, d * D + c * 512:d * D + c * 512 + 512], start=True, stop=True)
                mm.then_inc(k_h, 1)
            pe.wait_ge(k_sum, 1)
            for j in range(KT):
                mm = nc.tensor.matmul(PS[:, 7, j:j + 1], absum[:, j * P:(j + 1) * P], ones[:, 0:1],
                                      start=True, stop=True)
            mm.then_inc(k_col, 1)
            total(5)

            def spectrum(cos_src, sin_src, c, f, b0):
                for a in range(4):
                    src = cos_src if a % 2 == 0 else sin_src
                    for mt in range(2):
                        mm = nc.tensor.matmul(PS[:, b0 + a, :], fwdt[:, a, mt, f * P:(f + 1) * P],
                                              src[:, (a // 2) * 2 + mt, c * 512:(c + 1) * 512], start=mt == 0,
                                              stop=mt == 1)
                    if cos_src is not sin_src and a == 1 and f == 0:
                        for mt in range(2):
                            mm = nc.tensor.matmul(PS[0:1, b0 + a, :], fwdt[:, a, mt, 0:1],
                                                  cos_src[:, mt, c * 512:(c + 1) * 512], start=mt == 0, stop=mt == 1)
                return mm

            for k in range(4):
                if k:
                    pe.wait_ge(k_k, k)
                spectrum(HP, HM, k // 2, k % 2, 0).then_inc(k_f, 1)

            def hy_four(i, first):
                for u in range(4):
                    pe.wait_ge(w_lo, i * 4 + (ORD["hy_in"] + u + 1))
                    if first and u == 0:
                        pe.wait_ge(n_h, 4 * KT)
                        pe.wait_ge(k_k, 4)
                    if not (first and u < 2):
                        pe.wait_ge(y_b, i * 4 + (u - 1))
                    split_matmuls(pe, ORD["hy_in"] + u, PS[:, u % 2, :], H, range(KT), 0, True,
                                  True).then_inc(w_done, 1)
            hy_four(0, True)
            with pe.Fori(1, 6) as i:
                hy_four(i, False)

            pe.wait_ge(y_z, KT)
            pe.wait_ge(y_b, 24)
            for g in range(8):
                par, mt, c = g // 4, g // 2 % 2, g % 2
                if g >= 4:
                    pe.wait_ge(z_n, g - 3)
                for j in range(4):
                    tr = nc.tensor.transpose(PS[:, g % 4, j * P:(j + 1) * P],
                                             Z[:, 4 * c + j, mt * 256 + par:(mt + 1) * 256:2], ident[:, :])
                tr.then_inc(z_tr, 1)
            pe.wait_ge(z_n, 8)
            for k in range(4):
                if k >= 2:
                    pe.wait_ge(z_b, k - 1)
                spectrum(zN, zN, k // 2, k % 2, 4 * (k % 2)).then_inc(z_f, 1)
            pe.wait_ge(s_inv, 16)
            pe.wait_ge(z_y, 4)
            for j in range(KT):
                if j >= 4:
                    pe.wait_ge(i_ev, j - 3)
                for par in range(2):
                    for n in range(4):
                        a, f = 2 * par + n // 2, n % 2
                        mm = nc.tensor.matmul(PS[:, j % 4, par * 256:(par + 1) * 256],
                                              KS[:, j // 4, f, a, (j % 4) * P:(j % 4 + 1) * P], invt[:, a, f, :],
                                              start=n == 0, stop=n == 3)
                mm.then_inc(i_mm, 1)
            for n in range(8):
                pe.wait_ge(w_lo, ORD["hy_out"] + n + 1)
                if n == 0:
                    pe.wait_ge(i_h, KT)
                if n >= 2:
                    pe.wait_ge(o_ev, n - 1)
                split_matmuls(pe, ORD["hy_out"] + n, PS[:, n % 2, :], H, range(KT), 0, True, True).then_inc(w_done, 1)
            total(6)
            pairs("up", 5 * KT, h_g, 0, h_val, FT)
            down("down", FT, n_x, 3 * KT)
            total(7)

        @block.scalar
        def _(act):
            own = Own(act, s_act)
            SC = nc.scalar

            def root(k):
                act.wait_ge(n_ss, k + 1)
                if k:
                    act.wait_ge(n_rs, k)
                n = LC if k == 1 else L
                SC.activation(rtmp[:, 0:n], PS[:, 6, 0:n], ACT.Sqrt, bias=col("eps")).then_inc(n_rt, 1)

            def square(q, src, n=L):
                if q >= 2:
                    act.wait_ge(n_acc, q - 1)
                SC.activation(sqb[:, q % 2, 0:n], src, ACT.Square).then_inc(n_sq, 1)

            def high(c, dst, n=L):
                act.wait_ge(n_val, c + 1)
                SC.activation(dst, val[:, c % 2, 0:n], ACT.Copy).then_inc(n_hi, 1)

            act.wait_ge(s_small, 80)
            SC.activation(der("silu_c", 0, 3 * KT), col("c", 0, 3 * KT), ACT.Silu).then_inc(silu_c, 1)
            SC.activation(der("lg_f", 0, 8), col("dec_f", 0, 8), ACT.Exp).then_inc(m_lg, 1)
            SC.activation(der("lg_b", 0, 8), col("dec_b", 0, 8), ACT.Exp).then_inc(m_lg, 1)
            for l in range(3):
                act.wait_ge(f_arg, l + 1)
                if l:
                    act.wait_ge(f_mm, l + 1)
                SC.activation((fh if l < 2 else feat)[:, :], fa[:, :], ACT.Sin).then_inc(f_sin, 1)
            act.wait_ge(s_x, 16)
            for kt in range(KT):
                square(kt, X[:, kt, :])
            root(0)
            act.wait_ge(s_xc, 16)
            for kt in range(KT):
                square(KT + kt, Xc[:, kt, :], LC)
            root(1)
            split_hi(act, "w_in", 0)
            split_hi(act, "w_in", 1)
            for kt in range(KT):
                high(kt, H[:, 0, kt, :])
            for kt in range(KT):
                high(KT + kt, Hc[:, 0, kt, :], LC)

            def normed_head(n):
                return n == NV or 10 <= n < 14

            for n in range(22):
                act.wait_ge(w_done, ORD["w_in"] + n + 1)
                if n + 2 < 22:
                    split_hi(act, "w_in", n + 2)
                lat, ctx = PS[:, n % 2, :], PS[:, 2 + n % 2, 0:LC]
                if n == 0:
                    act.wait_ge(n_h, 2 * KT)
                m = n - 1
                if normed_head(m):
                    act.wait_ge(q_ss, 1 if m == NV else m - 8)
                    if m == NV:
                        own(SC.activation(RT[:, L:LA], PS[:, 6, 0:LC], ACT.Sqrt, bias=col("eps")))
                    else:
                        act.wait_ge(q_done, m - NV)
                    SC.activation(RT[:, 0:L], PS[:, 5, :], ACT.Sqrt, bias=col("eps")).then_inc(q_rt, 1)
                if n < NV:
                    if n >= 2:
                        act.wait_ge(v_tr, n - 1)
                    own(SC.activation(VT[:, n % 2, 0:L], lat, ACT.Copy))
                    SC.activation(VT[:, n % 2, L:LA], ctx, ACT.Copy).then_inc(q_ev, 1)
                    continue
                if n < 18 and n - NV >= 2:
                    act.wait_ge(q_done, n - NV - 1)
                if normed_head(n):
                    g = col("k_g") if n == NV else col("q_g")
                    own(SC.activation(SQ[:, 0:L], lat, ACT.Square))
                    if n == NV:
                        own(SC.activation(SQ[:, L:LA], ctx, ACT.Square))
                        own(SC.activation(RU[:, n % 2, L:LA], ctx, ACT.Copy, scale=g))
                    SC.activation(RU[:, n % 2, 0:L], lat, ACT.Copy, scale=g).then_inc(q_ev, 1)
                elif n < 10:
                    own(SC.activation(KR[:, n - 6, L:LA], ctx, ACT.Copy, scale=HD**-0.5))
                    SC.activation(RU[:, n % 2, 0:L], lat, ACT.Copy, scale=HD**-0.5).then_inc(q_ev, 1)
                elif n < 18:
                    SC.activation(RU[:, n % 2, 0:L], lat, ACT.Copy).then_inc(q_ev, 1)
                else:
                    SC.activation(G[:, n - 18, :], lat, ACT.Silu).then_inc(q_ev, 1)

            def exp_strip(h):
                act.wait_ge(r_u, h + 1)
                if h >= 2:
                    act.wait_ge(r_p, 6 * (h - 1))
                if h:
                    act.wait_ge(r_strip, h)
                own(SC.activation(ea[:, :], ea[:, :], ACT.Exp))
                own(SC.activation(strip[:, h % 2, DIST:], distt[:, 3 * DIST:3 * DIST + CDIST], ACT.Exp,
                                  scale=der("lg_f", h)))
                SC.activation(ec[:, :], distt[:, 3 * DIST + CDIST:], ACT.Exp, scale=der("lg_b", h)).then_inc(r_e, 1)

            def att_out(t):
                act.wait_ge(a_pv, 8 * (t + 1))
                SC.activation(H[:, 0, t, :], PS[:, 4, :], ACT.Copy).then_inc(a_hi, 1)

            def ret_out(t):
                act.wait_ge(r_pv, 12 * (t + 1))
                SC.activation(QR[:, t, :], PS[:, 6, :], ACT.Copy).then_inc(r_o, 1)

            act.wait_ge(s_dist, 16)
            exp_strip(0)
            for s in range(32):
                if s and s % 8 == 0:
                    ret_out(s // 8 - 1)
                act.wait_ge(a_mx, s + 1)
                if s >= 2:
                    act.wait_ge(a_tr, s - 1)
                    act.wait_ge(a_p, s - 1)
                SC.activation(Pb[:, s % 2, :], PS[:, 0:2, :].rearrange("p a b -> p (a b)")[:, 0:LA], ACT.Exp,
                              bias=smx[:, s % 2:s % 2 + 1], scale=HD**-0.5,
                              accum_out=rsum[:, s % 2:s % 2 + 1]).then_inc(a_exp, 1)
                if s % 4 == 2 and s // 4 < 7:
                    exp_strip(s // 4 + 1)
                act.wait_ge(a_tr, s + 1)
                if s >= 2:
                    act.wait_ge(a_pv, s - 1)
                SC.activation(PT[:, s % 2, :], PS[:, 2:4, :].rearrange("p a b -> p (a b)")[:, 0:LA],
                              ACT.Copy).then_inc(a_pt, 1)
                if s and s % 8 == 0:
                    att_out(s // 8 - 1)
            ret_out(3)
            att_out(3)

            def gn_square(t):
                act.wait_ge(g_y, t + 1)
                if t >= 2:
                    act.wait_ge(g_var, t - 1)
                SC.activation(gsq[:, t % 2, :], cen[:, t % 2, :], ACT.Square).then_inc(g_sq, 1)
            gn_square(0)
            gn_square(1)
            split_hi(act, "w_out", 0)
            split_hi(act, "w_out", 1)
            for t in range(4):
                act.wait_ge(g_var, t + 1)
                if t:
                    act.wait_ge(g_rs, t)
                SC.activation(rtmp[:, :], PS[:, t, :], ACT.Sqrt, bias=col("eps")).then_inc(g_rt, 1)
                act.wait_ge(g_val, t + 1)
                SC.activation(H[:, 0, 4 + t, :], gv[:, t % 2, :], ACT.Copy).then_inc(g_hi, 1)
                if t + 2 < 4:
                    gn_square(t + 2)

            for n in range(8):
                act.wait_ge(w_done, ORD["w_out"] + n + 1)
                if n + 2 < 8:
                    split_hi(act, "w_out", n + 2)
                if n == 0:
                    act.wait_ge(g_h, 4)
                square(2 * KT + n, PS[:, n % 2, :])
                SC.activation(Ym[:, n, :], PS[:, n % 2, :], ACT.Copy).then_inc(n_y, 1)
            root(2)
            for kt in range(KT):
                act.wait_ge(n_x, kt + 1)
                square(3 * KT + kt, X[:, kt, :])
            root(3)
            split_hi(act, "ffn_in", 0)
            split_hi(act, "ffn_in", 1)
            for kt in range(KT):
                high(2 * KT + kt, H[:, 0, kt, :])

            def ffn_four(i, last):
                for u in range(4):
                    act.wait_ge(w_done, i * 4 + (ORD["ffn_in"] + u + 1))
                    if not (last and u >= 2):
                        split_hi(act, "ffn_in", u + 2, i)
                    j = u // 2
                    if u % 2 == 0:
                        act.wait_ge(h_val, i * 2 + j)
                        SC.activation(sl[:, j, :], PS[:, u, :], ACT.Silu).then_inc(h_sl, 1)
                    else:
                        act.wait_ge(h_val, i * 2 + (j + 1))
                        SC.activation(hid[:, 0, i * 2 + j, :], hv[:, j, :], ACT.Copy).then_inc(h_hi, 1)
            with act.Fori(0, FT // 2 - 1) as i:
                ffn_four(i, False)
            ffn_four(FT // 2 - 1, True)

            split_hi(act, "ffn_out", 0)
            split_hi(act, "ffn_out", 1)

            def down_four(i, last):
                for u in range(4):
                    act.wait_ge(w_done, i * 4 + (ORD["ffn_out"] + u + 1))
                    if not (last and u >= 2):
                        split_hi(act, "ffn_out", u + 2, i)
                    j = u // 2
                    if u % 2:
                        act.wait_ge(n_acc, i * 2 + (4 * KT + j - 1))
                        SC.activation(sqb[:, j, :], PS[:, j, :], ACT.Square).then_inc(n_sq, 1)
                        SC.activation(Y[:, i * 2 + j, :], PS[:, j, :], ACT.Copy).then_inc(n_y, 1)
            act.wait_ge(h_lo, FT)
            with act.Fori(0, 3) as i:
                down_four(i, False)
            down_four(3, True)
            root(4)
            for kt in range(KT):
                act.wait_ge(n_x, KT + kt + 1)
                square(5 * KT + kt, X[:, kt, :])
                act.wait_ge(k_hp, kt + 1)
                own(SC.activation(aab[:, kt % 2, 0, :], fA[:, kt % 2, :], ACT.Abs))
                SC.activation(aab[:, kt % 2, 1, :], fB[:, kt % 2, :], ACT.Abs).then_inc(k_abs, 1)
            root(5)
            for k in range(4):
                for c in (3 * KT + 2 * k, 3 * KT + 2 * k + 1):
                    high(c, H[:, 0, c - 3 * KT, :])
                act.wait_ge(k_f, k + 1)
                act.wait_ge(k_hp, 8)
                if k:
                    act.wait_ge(k_k, k)
                own(SC.activation(kE[:, 0, :], PS[:, 0, :], ACT.Copy))
                SC.activation(kE[:, 1, :], PS[:, 1, :], ACT.Copy).then_inc(k_e, 1)

            split_hi(act, "hy_in", 0)
            split_hi(act, "hy_in", 1)
            act.wait_ge(y_c, 1)

            def hy_four(i, last):
                for u in range(4):
                    act.wait_ge(w_done, i * 4 + (ORD["hy_in"] + u + 1))
                    if not (last and u >= 2):
                        split_hi(act, "hy_in", u + 2, i)
                    act.wait_ge(y_c, i * 4 + u)
                    SC.activation(cb_[:, u % 2, 1:L + 1], PS[:, u % 2, :], ACT.Identity,
                                  bias=colt[:, bass.ds(i * 4 + (COL["hy_b_in"] + u), 1)]).then_inc(y_b, 1)
            with act.Fori(0, 5) as i:
                hy_four(i, False)
            hy_four(5, True)
            for g in range(8):
                par, mt, c = g // 4, g // 2 % 2, g % 2
                act.wait_ge(z_tr, g + 1)
                SC.activation(zN[:, par * 2 + mt, c * 512:(c + 1) * 512], PS[:, g % 4, :], ACT.Copy).then_inc(z_n, 1)
            act.wait_ge(y_c, 25)
            for k in range(4):
                act.wait_ge(z_f, k + 1)
                if k:
                    act.wait_ge(z_b, k)
                b = 4 * (k % 2)
                own(SC.activation(zE[:, 0, :], PS[:, b, :], ACT.Copy))
                SC.activation(zE[:, 1, :], PS[:, b + 1, :], ACT.Copy).then_inc(z_e, 1)

            def inv_high(j):
                act.wait_ge(i_val, j + 1)
                SC.activation(H[:, 0, j, :], yv[:, j % 2, :], ACT.Copy).then_inc(i_hi, 1)
            act.wait_ge(z_y, 4)
            for j in range(KT):
                act.wait_ge(i_mm, j + 1)
                if j >= 2:
                    act.wait_ge(i_val, j - 1)
                SC.activation(yt[:, j % 2, :].rearrange("p (m r) -> p r m", r=2),
                              PS[:, j % 4, :].rearrange("p (r m) -> p r m", r=2), ACT.Copy,
                              scale=der("inv_norm", j)).then_inc(i_ev, 1)
                if j:
                    inv_high(j - 1)
            inv_high(KT - 1)

            split_hi(act, "hy_out", 0)
            split_hi(act, "hy_out", 1)
            for n in range(8):
                act.wait_ge(w_done, ORD["hy_out"] + n + 1)
                if n + 2 < 8:
                    split_hi(act, "hy_out", n + 2)
                if n >= 2:
                    act.wait_ge(n_x, 2 * KT + n - 1)
                SC.activation(hyt[:, n % 2, :], PS[:, n % 2, :], ACT.Identity, bias=der("p_hy", n),
                              scale=dert[:, DER["mod2"] + 2 * KT + n:DER["mod2"] + 2 * KT + n + 1]).then_inc(o_ev, 1)
                if n:
                    act.wait_ge(n_x, 2 * KT + n)
                    square(6 * KT + n - 1, X[:, n - 1, :])
            act.wait_ge(n_x, 3 * KT)
            square(7 * KT - 1, X[:, KT - 1, :])
            root(6)
            split_hi(act, "up", 0)
            split_hi(act, "up", 1)
            for kt in range(KT):
                high(4 * KT + kt, H[:, 0, kt, :])

            act.wait_ge(h_cv, 1)

            def up_four(i, last):
                for u in range(4):
                    act.wait_ge(w_done, i * 4 + (ORD["up"] + u + 1))
                    if not (last and u >= 2):
                        split_hi(act, "up", u + 2, i)
                    j = u // 2
                    if u % 2 == 0:
                        act.wait_ge(h_cv, i * 2 + j)
                        SC.activation(gb[:, j, 1:ROWS + 1, 1:GRID_W + 1],
                                      PS[:, u, :].rearrange("p (a b) -> p a b", b=GRID_W), ACT.Copy).then_inc(h_g, 1)
                    else:
                        act.wait_ge(h_cv, i * 2 + (j + 2))
                        act.wait_ge(h_val, i * 2 + (FT + j - 1))
                        SC.activation(sl[:, j, :], cva[:, j, :, :].rearrange("p a b -> p (a b)"),
                                      ACT.Silu).then_inc(h_sl, 1)
                        act.wait_ge(h_val, i * 2 + (FT + j + 1))
                        SC.activation(hid[:, 0, i * 2 + j, :], hv[:, j, :], ACT.Copy).then_inc(h_hi, 1)
            with act.Fori(0, FT // 2 - 1) as i:
                up_four(i, False)
            up_four(FT // 2 - 1, True)

            split_hi(act, "down", 0)
            split_hi(act, "down", 1)
            act.wait_ge(h_lo, 2 * FT)

            def last_four(i, last):
                for u in range(4):
                    act.wait_ge(w_done, i * 4 + (ORD["down"] + u + 1))
                    if not (last and u >= 2):
                        split_hi(act, "down", u + 2, i)
                    j = u // 2
                    if u % 2:
                        act.wait_ge(n_x, i * 2 + (3 * KT + j + 1))
                        act.wait_ge(n_acc, i * 2 + (7 * KT + j - 1))
                        SC.activation(sqb[:, j, :], X[:, i * 2 + j, :], ACT.Square).then_inc(n_sq, 1)
            with act.Fori(0, 3) as i:
                last_four(i, False)
            last_four(3, True)
            root(7)

        @block.gpsimd
        def _(pool):
            own = Own(pool, s_pool)
            PL = nc.gpsimd
            VAL = {0: 0, 1: KT, 3: 2 * KT, 5: 3 * KT, 6: 4 * KT, 7: 5 * KT}
            XS = {2: 0, 4: KT}

            def sums(k, n=L, kts=range(KT)):
                for kt in kts:
                    q = k * KT + kt
                    pool.wait_ge(n_sq, q + 1)
                    if kt == 0:
                        if k:
                            pool.wait_ge(n_ss, k)
                        PL.tensor_copy(acc[:, 0:n], sqb[:, q % 2, 0:n]).then_inc(n_acc, 1)
                    else:
                        pool.wait_ge(n_acc, q)
                        PL.tensor_tensor(acc[:, 0:n], acc[:, 0:n], sqb[:, q % 2, 0:n], ALU.add).then_inc(n_acc, 1)

            def scaled(k, kts, src, n=L):
                for kt in kts:
                    t = k * KT + kt
                    pool.wait_ge(n_rs, k + 1)
                    if t >= 2:
                        kk, b = (t - 2) // KT, (t - 2) % KT
                        pool.wait_ge(n_x if kk in XS else n_val, (XS[kk] if kk in XS else VAL[kk]) + b + 1)
                    PL.tensor_tensor(tb[:, t % 2, 0:n], src[:, kt, 0:n], rstd[:, 0:n], ALU.mult).then_inc(n_t, 1)

            def scaled_sums(k, src):
                for kt in range(KT + 1):
                    if kt < KT:
                        scaled(k, [kt], src)
                    if kt:
                        sums(k + 1, L, [kt - 1])

            sums(0)
            sums(1, LC)
            scaled(0, range(KT), X)
            scaled(1, range(KT), Xc, LC)
            for h in range(8):
                pool.wait_ge(r_e, h + 1)
                own(PL.tensor_tensor(strip[:, h % 2, 0:DIST], ea[:, :], distt[:, 2 * DIST:3 * DIST], ALU.add))
                PL.tensor_tensor(strip[:, h % 2, DIST:], strip[:, h % 2, DIST:], ec[:, :], ALU.add).then_inc(r_strip, 1)
            sums(2)
            scaled_sums(2, Ym)
            scaled(3, range(KT), X)
            sums(4)
            scaled_sums(4, Y)
            scaled(5, range(KT), X)
            for k in range(4):
                pool.wait_ge(z_b, k + 1)
                c, f, z0 = k // 2, k % 2, 4 * (k % 2)
                kk = KS[:, c, f, :, :]
                if k:
                    pool.wait_ge(z_w, k)
                for d in range(2):
                    zr, zi, kr, ki = zs[:, z0 + 2 * d, :], zs[:, z0 + 2 * d + 1, :], kk[:, 2 * d, :], kk[:, 2 * d + 1, :]
                    own(PL.tensor_tensor(zpP[:, d, :], zr, ki, ALU.mult))
                    own(PL.tensor_tensor(zpP[:, 2, :], zi, kr, ALU.mult))
                    last = PL.tensor_tensor(zpP[:, d, :], zpP[:, d, :], zpP[:, 2, :], ALU.add)
                    if d == 0:
                        own(last)
                last.then_inc(z_q, 1)
                pool.wait_ge(z_q, k + 1)
                pool.wait_ge(z_p, k + 1)
                own(PL.tensor_tensor(kk[:, 1, :], zpP[:, 0, :], zpP[:, 1, :], ALU.add))
                PL.tensor_tensor(kk[:, 3, :], zpP[:, 0, :], zpP[:, 1, :], ALU.subtract).then_inc(z_w, 1)
            sums(6)
            scaled(6, range(KT), X)
            sums(7)
            scaled(7, range(KT), X)

        @block.vector
        def _(dve):
            own = Own(dve, s_dve)
            VE = nc.vector

            def stt(o, a, s, b, op0=ALU.mult, op1=ALU.add):
                return VE.scalar_tensor_tensor(out=o, in0=a, scalar=s, in1=b, op0=op0, op1=op1)

            def reciprocal_root(k):
                dve.wait_ge(n_rt, k + 1)
                n = LC if k == 1 else L
                VE.reciprocal(rstd[:, 0:n], rtmp[:, 0:n]).then_inc(n_rs, 1)

            def normed(k, c, kt, scale, shift, n=L):
                dve.wait_ge(n_t, k * KT + kt + 1)
                if c >= 2:
                    dve.wait_ge(n_h, c - 1)
                VE.tensor_scalar(val[:, c % 2, 0:n], tb[:, (k * KT + kt) % 2, 0:n], scale, shift, ALU.mult,
                                 ALU.add).then_inc(n_val, 1)

            def low(c, hi, lo, n=L):
                dve.wait_ge(n_hi, c + 1)
                VE.tensor_tensor(lo, val[:, c % 2, 0:n], hi.bitcast(F32), ALU.subtract).then_inc(n_h, 1)

            def normed_tiles(k, c0, h, scale, shift, n=L):
                for kt in range(KT + 1):
                    if kt < KT:
                        normed(k, c0 + kt, kt, scale(kt), shift(kt), n)
                    if kt:
                        low(c0 + kt - 1, h[:, 0, kt - 1, :], h[:, 1, kt - 1, :], n)

            def residual(k, x0, kt, gate):
                dve.wait_ge(n_t, k * KT + kt + 1)
                stt(X[:, kt, :], tb[:, (k * KT + kt) % 2, :], gate, X[:, kt, :]).then_inc(n_x, 1)

            dve.wait_ge(s_small, 80)
            for l in range(3):
                dve.wait_ge(f_mm, l + 1)
                if l:
                    dve.wait_ge(f_sin, l)
                b = ("fb1", "fb2", "fb3")[l]
                own(VE.tensor_scalar(fa[:, :], PS[0:HYF, 6, :], colt[0:HYF, COL[b]:COL[b] + 1],
                                     colt[0:HYF, COL["freq"]:COL["freq"] + 1], ALU.add, ALU.mult))
                own(VE.tensor_scalar(fk[:, :], fa[:, :], float(1 / TWO_PI), MAGIC, ALU.mult, ALU.add))
                own(VE.tensor_scalar(fk[:, :], fk[:, :], MAGIC, None, ALU.subtract))
                for part in (PI_A, PI_B, PI_C):
                    own(stt(fa[:, :], fk[:, :], -part, fa[:, :]))
                VE.tensor_scalar(fa[:, :], fa[:, :], PI_SAFE, -PI_SAFE, ALU.min, ALU.max).then_inc(f_arg, 1)

            dve.wait_ge(m_lg, 2)
            for name in ("lg_f", "lg_b"):
                own(VE.tensor_scalar(der(name, 0, 8), der(name, 0, 8), -1.0, None, ALU.mult))

            def mod_pair(chunk, which):
                a = DER["mod"] + 2 * KT * chunk + which
                return dert[:, a:a + 2 * KT - 1:2]

            def mod_col(chunk, kt, which=0):
                a = DER["mod"] + 2 * (KT * chunk + kt) + which
                return dert[:, a:a + 1]

            def mod2_col(chunk, kt):
                return der("mod2", KT * chunk + kt)

            reciprocal_root(0)
            dve.wait_ge(mod_done, 16)
            VE.tensor_tensor(der("mod", 0, 32), PS[:, 7, 0:32], col("b_mod", 0, 32), ALU.add).then_inc(m_cols, 1)
            dve.wait_ge(m_cols, 1)
            own(stt(der("a_mix", 0, KT), mod_pair(1, 0), 1.0, col("g_pre_mix", 0, KT), ALU.add, ALU.mult))
            own(stt(der("a_ctx", 0, KT), mod_pair(1, 1), 1.0, col("g_pre_mix", 0, KT), ALU.add, ALU.mult))
            normed_tiles(0, 0, H, lambda kt: der("a_mix", kt), lambda kt: mod_col(0, kt))
            reciprocal_root(1)
            split_lo(dve, "w_in", 0)
            split_lo(dve, "w_in", 1)
            normed_tiles(1, KT, Hc, lambda kt: der("a_ctx", kt), lambda kt: mod_col(0, kt, 1), LC)

            dve.wait_ge(s_rope, 16)
            for n in range(22):
                if n + 2 < 22:
                    split_lo(dve, "w_in", n + 2)
                m = n - 1
                if 0 <= m < NV:
                    dve.wait_ge(v_tr, m + 1)
                    VE.tensor_copy(V[:, :, m * P:(m + 1) * P],
                                   PS[:, 6:8, :].rearrange("p a b -> p (a b)")[:, 0:LA].rearrange(
                                       "p (t d) -> p t d", d=P)).then_inc(v_ev, 1)
                elif NV <= m < NV + NROPE:
                    normed_q = m == NV or 10 <= m < 14
                    dst = (KA[:, 0:L] if m == NV else KR[:, m - 6, 0:L] if m < 10 else QA[:, m - 10, :] if m < 14
                           else QR[:, m - 14, :])
                    dve.wait_ge(q_sw, m - NV + 1)
                    if m > NV:
                        dve.wait_ge(q_done, m - NV)
                    own(VE.tensor_tensor(RM[:, :], RU[:, m % 2, 0:L], ropet[:, 0, :], ALU.mult))
                    own(VE.tensor_tensor(dst, PS[:, 4, :], ropet[:, 1, :], ALU.mult))
                    if not normed_q:
                        VE.tensor_tensor(dst, dst, RM[:, :], ALU.add).then_inc(q_done, 1)
                        continue
                    own(VE.tensor_tensor(dst, dst, RM[:, :], ALU.add))
                    dve.wait_ge(q_rt, 1 if m == NV else m - 8)
                    w_ = LA if m == NV else L
                    own(VE.reciprocal(RT[:, 0:w_], RT[:, 0:w_]))
                    if m == NV:
                        own(VE.tensor_tensor(KA[:, L:LA], RU[:, m % 2, L:LA], RT[:, L:LA], ALU.mult))
                    VE.tensor_tensor(dst, dst, RT[:, 0:L], ALU.mult).then_inc(q_done, 1)

            def decay_arg(h):
                if h:
                    dve.wait_ge(r_strip, h)
                own(VE.tensor_scalar(ea[:, :], distt[:, DIST:2 * DIST], der("lg_b", h), None, ALU.mult))
                stt(ea[:, :], distt[:, 0:DIST], der("lg_f", h), ea[:, :]).then_inc(r_u, 1)

            dve.wait_ge(s_dist, 16)
            decay_arg(0)
            for s in range(32):
                dve.wait_ge(a_s, s + 1)
                own(VE.tensor_reduce(mxr[:, s % 2:s % 2 + 1], PS[:, 0:2, :].rearrange("p a b -> p (a b)")[:, 0:LA],
                                     mybir.AxisListType.X, ALU.max))
                if s >= 2:
                    dve.wait_ge(a_exp, s - 1)
                VE.tensor_scalar(smx[:, s % 2:s % 2 + 1], mxr[:, s % 2:s % 2 + 1], -HD**-0.5, None,
                                 ALU.mult).then_inc(a_mx, 1)
                for r in range(s * 3 // 2, (s + 1) * 3 // 2):
                    h, kt = r // 6, r % 6
                    a = L - P - P * kt if kt < 4 else DIST + P * (5 - kt)
                    dve.wait_ge(r_s, r + 1)
                    dve.wait_ge(r_strip, h + 1)
                    if r >= 2:
                        dve.wait_ge(r_pv, r - 1)
                    VE.tensor_tensor(pr[:, r % 2, :], PS[:, 5, :], strip[:, h % 2, a:a + L], ALU.mult).then_inc(r_p, 1)
                if s % 4 == 1 and s // 4 < 7:
                    decay_arg(s // 4 + 1)
                dve.wait_ge(a_exp, s + 1)
                own(VE.reciprocal(rinv[:, s % 2:s % 2 + 1], rsum[:, s % 2:s % 2 + 1]))
                VE.tensor_scalar(Pb[:, s % 2, :], Pb[:, s % 2, :], rinv[:, s % 2:s % 2 + 1], None,
                                 ALU.mult).then_inc(a_p, 1)
                if s and s % 8 == 0:
                    dve.wait_ge(a_hi, s // 8)
                    VE.tensor_tensor(H[:, 1, s // 8 - 1, :], PS[:, 4, :], H[:, 0, s // 8 - 1, :].bitcast(F32),
                                     ALU.subtract).then_inc(a_o, 1)
            dve.wait_ge(a_hi, 4)
            VE.tensor_tensor(H[:, 1, 3, :], PS[:, 4, :], H[:, 0, 3, :].bitcast(F32), ALU.subtract).then_inc(a_o, 1)

            def gn_centre(t):
                dve.wait_ge(g_c, t + 1)
                if t >= 2:
                    dve.wait_ge(g_h, t - 1)
                VE.tensor_tensor(cen[:, t % 2, :], QR[:, t, :], PS[:, t, :], ALU.subtract).then_inc(g_y, 1)
            gn_centre(0)
            gn_centre(1)
            dve.wait_ge(mod_done, 2 * MODU)
            own(VE.tensor_tensor(der("mod", 32, 64), PS[:, 7, 32:96], col("b_mod", 32, 64), ALU.add))
            own(VE.tensor_tensor(der("mod2", 0, MODU), PS[:, 7, 96:96 + MODU], col("b_mod2", 0, MODU), ALU.add))
            own(VE.tensor_tensor(der("p_mix", 0, KT), mod_pair(2, 0), col("g_post_mix", 0, KT), ALU.mult))
            own(stt(der("a_ffn", 0, KT), mod_pair(4, 0), 1.0, col("g_pre_ffn", 0, KT), ALU.add, ALU.mult))
            own(VE.tensor_tensor(der("p_ffn", 0, KT), mod_pair(5, 0), col("g_post_ffn", 0, KT), ALU.mult))
            own(stt(der("a_hy", 0, KT), der("mod2", KT, KT), 1.0, col("g_hy", 0, KT), ALU.add, ALU.mult))
            own(VE.tensor_tensor(der("p_hy", 0, KT), der("mod2", 2 * KT, KT), col("hy_b_out", 0, KT), ALU.mult))
            own(stt(der("a_ffn2", 0, KT), der("mod2", 4 * KT, KT), 1.0, col("g_ffn2", 0, KT), ALU.add, ALU.mult))
            for t in range(4):
                dve.wait_ge(g_rt, t + 1)
                VE.reciprocal(grs[:, :], rtmp[:, :]).then_inc(g_rs, 1)
                own(VE.tensor_tensor(gv[:, t % 2, :], cen[:, t % 2, :], G[:, t, :], ALU.mult))
                dve.wait_ge(g_rs, t + 1)
                VE.tensor_tensor(gv[:, t % 2, :], gv[:, t % 2, :], grs[:, :], ALU.mult).then_inc(g_val, 1)
                dve.wait_ge(g_hi, t + 1)
                VE.tensor_tensor(H[:, 1, 4 + t, :], gv[:, t % 2, :], H[:, 0, 4 + t, :].bitcast(F32),
                                 ALU.subtract).then_inc(g_h, 1)
                if t == 0:
                    split_lo(dve, "w_out", 0)
                    split_lo(dve, "w_out", 1)
                if t + 2 < 4:
                    gn_centre(t + 2)

            for n in range(2, 8):
                split_lo(dve, "w_out", n)
            reciprocal_root(2)
            for kt in range(KT):
                residual(2, 0, kt, der("p_mix", kt))
            reciprocal_root(3)
            split_lo(dve, "ffn_in", 0)
            split_lo(dve, "ffn_in", 1)
            normed_tiles(3, 2 * KT, H, lambda kt: der("a_ffn", kt), lambda kt: mod_col(3, kt))

            def ffn_four(i, last):
                for u in range(4):
                    if not (last and u >= 2):
                        split_lo(dve, "ffn_in", u + 2, i)
                    j = u // 2
                    if u % 2:
                        dve.wait_ge(w_done, i * 4 + (ORD["ffn_in"] + u + 1))
                        dve.wait_ge(h_sl, i * 2 + (j + 1))
                        dve.wait_ge(h_lo, i * 2 + j)
                        VE.tensor_tensor(hv[:, j, :], PS[:, u, :], sl[:, j, :], ALU.mult).then_inc(h_val, 1)
                        dve.wait_ge(h_hi, i * 2 + (j + 1))
                        VE.tensor_tensor(hid[:, 1, i * 2 + j, :], hv[:, j, :], hid[:, 0, i * 2 + j, :].bitcast(F32),
                                         ALU.subtract).then_inc(h_lo, 1)
            with dve.Fori(0, FT // 2 - 1) as i:
                ffn_four(i, False)
            ffn_four(FT // 2 - 1, True)
            for n in range(2):
                split_lo(dve, "ffn_out", n)
            with dve.Fori(0, 3) as i:
                for u in range(4):
                    split_lo(dve, "ffn_out", u + 2, i)
            for n in range(14, 16):
                split_lo(dve, "ffn_out", n)

            def abs_sum(j):
                t, c = j // 2, j % 2
                cs = slice(c * 512, (c + 1) * 512)
                dve.wait_ge(k_abs, j + 1)
                if t == 0:
                    own(VE.tensor_tensor(absum[:, cs], aab[:, c, 0, :], aab[:, c, 1, :], ALU.add))
                else:
                    own(VE.tensor_tensor(absum[:, cs], absum[:, cs], aab[:, c, 0, :], ALU.add))
                    last = VE.tensor_tensor(absum[:, cs], absum[:, cs], aab[:, c, 1, :], ALU.add)
                    if j == 7:
                        last.then_inc(k_sum, 1)
                    else:
                        own(last)
            reciprocal_root(4)
            for j in range(8):
                residual(4, KT, j, der("p_ffn", j))
                t, c = j // 2, j % 2
                cs = slice(c * 512, (c + 1) * 512)
                dve.wait_ge(s_dec[t % 2], 16 * (t // 2 + 1))
                dve.wait_ge(k_h, j + 1)
                if j:
                    dve.wait_ge(k_hp, j)
                own(VE.tensor_tensor(fA[:, j % 2, :], PS[:, 4, :], dect[:, t % 2, cs], ALU.mult))
                VE.tensor_tensor(fB[:, j % 2, :], PS[:, 5, :], dect[:, t % 2, cs], ALU.mult).then_inc(k_ab, 1)
                dve.wait_ge(k_ab, j + 1)
                if t == 0:
                    own(VE.memset(fB[0:1, j % 2, :], 0.0))
                own(VE.tensor_tensor(HP[:, t, cs], fA[:, j % 2, :], fB[:, j % 2, :], ALU.add))
                VE.tensor_tensor(HM[:, t, cs], fA[:, j % 2, :], fB[:, j % 2, :], ALU.subtract).then_inc(k_hp, 1)
                if j:
                    abs_sum(j - 1)
            abs_sum(7)
            reciprocal_root(5)
            dve.wait_ge(k_col, 1)
            own(VE.reciprocal(der("inv_norm", 0, KT), PS[:, 7, 0:KT]))
            for k in range(4):
                for kt in (2 * k, 2 * k + 1):
                    normed(5, 3 * KT + kt, kt, der("a_hy", kt), mod2_col(0, kt))
                    if kt:
                        low(3 * KT + kt - 1, H[:, 0, kt - 1, :], H[:, 1, kt - 1, :])
                c, f = k // 2, k % 2
                dve.wait_ge(k_e, k + 1)
                for part in range(2):
                    own(VE.tensor_tensor(KS[:, c, f, part, :], kE[:, part, :], PS[:, 2 + part, :], ALU.add))
                own(VE.tensor_tensor(KS[:, c, f, 2, :], kE[:, 0, :], PS[:, 2, :], ALU.subtract))
                VE.tensor_tensor(KS[:, c, f, 3, :], kE[:, 1, :], PS[:, 3, :], ALU.subtract).then_inc(k_k, 1)
            low(4 * KT - 1, H[:, 0, KT - 1, :], H[:, 1, KT - 1, :])

            split_lo(dve, "hy_in", 0)
            split_lo(dve, "hy_in", 1)
            dve.wait_ge(n_h, 4 * KT)
            VE.memset(cb_[:, :, 0:L + 2:L + 1], 0.0).then_inc(y_c, 1)

            def hy_four(i, gated, last):
                for u in range(4):
                    if not (last and u >= 2):
                        split_lo(dve, "hy_in", u + 2, i)
                    dve.wait_ge(y_b, i * 4 + (u + 1))
                    j = u // 2

                    def hcol(name, per, tap):
                        return colt[:, bass.ds(i * (4 * per) + (COL[name] + per * u + tap), 1)]
                    if gated:
                        dst = x1c[:, :] if u % 2 == 0 else ca[:, 1, :]
                    else:
                        dst = X0[:, i * 4 + (u - 16), :]
                    own(VE.tensor_scalar(ca[:, 0, :], cb_[:, u % 2, 1:L + 1], hcol("hy_sc_w", 3, 1),
                                         hcol("hy_sc_b", 1, 0), ALU.mult, ALU.add))
                    own(stt(ca[:, 0, :], cb_[:, u % 2, 0:L], hcol("hy_sc_w", 3, 0), ca[:, 0, :]))
                    stt(dst, cb_[:, u % 2, 2:L + 2], hcol("hy_sc_w", 3, 2), ca[:, 0, :]).then_inc(y_c, 1)
                    dve.wait_ge(y_c, i * 4 + (u + 2))
                    if gated and u % 2:
                        VE.tensor_tensor(Z[:, i * 2 + j, :], x1c[:, :], ca[:, 1, :], ALU.mult).then_inc(y_z, 1)
                        dve.wait_ge(y_z, i * 2 + (j + 1))
            with dve.Fori(0, 4) as i:
                own.enter(i, 8)
                hy_four(i, True, False)
            own.leave(4)
            hy_four(4, False, False)
            hy_four(5, False, True)

            for k in range(4):
                c, f, z0, b = k // 2, k % 2, 4 * (k % 2), 4 * (k % 2)
                kk = KS[:, c, f, :, :]
                dve.wait_ge(z_e, k + 1)
                if k >= 2:
                    dve.wait_ge(z_q, k - 1)
                for part in range(2):
                    own(VE.tensor_tensor(zs[:, z0 + part, :], zE[:, part, :], PS[:, b + 2 + part, :], ALU.add))
                own(VE.tensor_tensor(zs[:, z0 + 2, :], zE[:, 0, :], PS[:, b + 2, :], ALU.subtract))
                VE.tensor_tensor(zs[:, z0 + 3, :], zE[:, 1, :], PS[:, b + 3, :], ALU.subtract).then_inc(z_b, 1)
                dve.wait_ge(z_b, k + 1)
                for d in range(2):
                    zr, zi, kr, ki = zs[:, z0 + 2 * d, :], zs[:, z0 + 2 * d + 1, :], kk[:, 2 * d, :], kk[:, 2 * d + 1, :]
                    own(VE.tensor_tensor(zpD[:, d, :], zr, kr, ALU.mult))
                    own(stt(zpD[:, 2, :], zi, 1.0 if f else col("not_first"), ki, ALU.mult, ALU.mult))
                    last = VE.tensor_tensor(zpD[:, d, :], zpD[:, d, :], zpD[:, 2, :], ALU.subtract)
                    if d == 0 or f == 0:
                        own(last)
                if f == 0:
                    S, W, S_, W_ = zs[0:1, z0 + 1, :], zs[0:1, z0 + 3, :], kk[0:1, 1, :], kk[0:1, 3, :]
                    own(VE.tensor_tensor(row[:, 0, :], S, W_, ALU.mult))
                    own(VE.tensor_tensor(row[:, 1, :], W, S_, ALU.mult))
                    own(VE.tensor_tensor(row[:, 0, :], row[:, 0, :], row[:, 1, :], ALU.add))
                    own(VE.tensor_tensor(row[:, 1, :], S, S_, ALU.mult))
                    own(VE.tensor_tensor(zpD[0:1, 2, :], W, W_, ALU.mult))
                    last = VE.tensor_tensor(row[:, 1, :], row[:, 1, :], zpD[0:1, 2, :], ALU.subtract)
                last.then_inc(z_p, 1)
                dve.wait_ge(z_p, k + 1)
                dve.wait_ge(z_q, k + 1)
                own(VE.tensor_tensor(kk[:, 0, :], zpD[:, 0, :], zpD[:, 1, :], ALU.add))
                last = VE.tensor_tensor(kk[:, 2, :], zpD[:, 0, :], zpD[:, 1, :], ALU.subtract)
                if f == 0:
                    own(last)
                    dve.wait_ge(z_w, k + 1)
                    own(VE.tensor_copy(kk[0:1, 1, :], row[:, 0, :]))
                    last = VE.tensor_copy(kk[0:1, 3, :], row[:, 1, :])
                else:
                    own(last)
                    dve.wait_ge(z_w, k + 1)
                    last = VE.tensor_copy(row[:, 0, 0:1], row[:, 1, 0:1])
                last.then_inc(z_y, 1)
                dve.wait_ge(z_y, k + 1)

            def inv_low(j):
                dve.wait_ge(i_hi, j + 1)
                VE.tensor_tensor(H[:, 1, j, :], yv[:, j % 2, :], H[:, 0, j, :].bitcast(F32),
                                 ALU.subtract).then_inc(i_h, 1)
            for j in range(KT):
                dve.wait_ge(i_ev, j + 1)
                own(stt(yt[:, j % 2, :], Z[:, j, :], col("hy_bias", j), yt[:, j % 2, :]))
                if j >= 2:
                    dve.wait_ge(i_h, j - 1)
                VE.tensor_tensor(yv[:, j % 2, :], yt[:, j % 2, :], X0[:, j, :], ALU.mult).then_inc(i_val, 1)
                if j:
                    inv_low(j - 1)
            inv_low(KT - 1)

            split_lo(dve, "hy_out", 0)
            split_lo(dve, "hy_out", 1)
            for n in range(8):
                if n + 2 < 8:
                    split_lo(dve, "hy_out", n + 2)
                dve.wait_ge(o_ev, n + 1)
                VE.tensor_tensor(X[:, n, :], X[:, n, :], hyt[:, n % 2, :], ALU.add).then_inc(n_x, 1)
            reciprocal_root(6)
            split_lo(dve, "up", 0)
            split_lo(dve, "up", 1)
            normed_tiles(6, 4 * KT, H, lambda kt: der("a_ffn2", kt), lambda kt: mod2_col(3, kt))

            dve.wait_ge(n_h, 5 * KT)
            VE.memset(gb[:, :, :, :], 0.0).then_inc(h_cv, 1)

            def up_four(i, last):
                for u in range(4):
                    if not (last and u >= 2):
                        split_lo(dve, "up", u + 2, i)
                    j = u // 2
                    if u % 2 == 0:
                        dve.wait_ge(h_g, i * 2 + (j + 1))
                        dve.wait_ge(h_sl, i * 2 + (FT + j - 1))

                        def wcol(tap):
                            return colt[:, bass.ds(i * 18 + (COL["conv_w"] + 9 * j + tap), 1)]
                        own(VE.tensor_scalar(cva[:, j, :, :], gb[:, j, 0:ROWS, 0:GRID_W], wcol(0),
                                             colt[:, bass.ds(i * 2 + (COL["conv_b"] + j), 1)], ALU.mult, ALU.add))
                        for tap in range(1, 9):
                            dy, dx = tap // 3, tap % 3
                            ins = stt(cva[:, j, :, :], gb[:, j, dy:dy + ROWS, dx:dx + GRID_W], wcol(tap),
                                      cva[:, j, :, :])
                            if tap < 8:
                                own(ins)
                        ins.then_inc(h_cv, 1)
                    else:
                        dve.wait_ge(w_done, i * 4 + (ORD["up"] + u + 1))
                        dve.wait_ge(h_sl, i * 2 + (FT + j + 1))
                        dve.wait_ge(h_lo, i * 2 + (FT + j))
                        VE.tensor_tensor(hv[:, j, :], PS[:, u, :], sl[:, j, :], ALU.mult).then_inc(h_val, 1)
                        dve.wait_ge(h_hi, i * 2 + (FT + j + 1))
                        VE.tensor_tensor(hid[:, 1, i * 2 + j, :], hv[:, j, :], hid[:, 0, i * 2 + j, :].bitcast(F32),
                                         ALU.subtract).then_inc(h_lo, 1)
            with dve.Fori(0, FT // 2 - 1) as i:
                own.enter(i, 16)
                up_four(i, False)
            own.leave(FT // 2 - 1)
            up_four(FT // 2 - 1, True)

            split_lo(dve, "down", 0)
            split_lo(dve, "down", 1)

            def last_four(i, last):
                for u in range(4):
                    if not (last and u >= 2):
                        split_lo(dve, "down", u + 2, i)
                    j = u // 2
                    if u % 2:
                        dve.wait_ge(w_done, i * 4 + (ORD["down"] + u + 1))
                        stt(X[:, i * 2 + j, :], PS[:, j, :],
                            dert[:, bass.ds(i * 2 + (DER["mod2"] + 5 * KT + j), 1)],
                            X[:, i * 2 + j, :]).then_inc(n_x, 1)
            with dve.Fori(0, 3) as i:
                last_four(i, False)
            last_four(3, True)
            reciprocal_root(7)
            for kt in range(KT):
                dve.wait_ge(n_t, 7 * KT + kt + 1)
                VE.tensor_scalar(Y[:, kt, :], tb[:, kt % 2, :], col("g_final", kt), None, ALU.mult).then_inc(n_val, 1)


def tables():
    f32 = np.float32
    m = np.zeros((4, P, P), f32)
    m[0] = 1.0 / D
    i = np.arange(P)
    m[1] = (i[:, None] // HD == i[None, :] // HD) / f32(HD)
    m[2] = i[:, None] == (i[None, :] // HD) * HD + (i[None, :] + HALF) % HD
    m[3] = np.eye(P)
    n_freq = HD // 4
    inv_freq = (f32(10000.0) ** (-np.arange(n_freq, dtype=f32) / f32(n_freq))).astype(f32)
    tok = np.arange(L)
    ang = np.concatenate([(tok // GRID_W).astype(f32)[:, None] * inv_freq, (tok % GRID_W).astype(f32)[:, None] * inv_freq],
                         axis=1).T
    ang = np.tile(ang, (4, 1))
    sign = np.where(i % HD < HALF, -1.0, 1.0).astype(f32)[:, None]
    rope = np.stack([np.cos(ang), np.sin(ang) * sign], 1).astype(f32)
    f, p = np.arange(DIST)[None, :], i[:, None]
    d = f - (L - P) - p
    fc = np.arange(CDIST)[None, :]
    dist = np.concatenate([np.maximum(d, 0), np.maximum(-d, 0), d == 0, fc + P - p, L + P - fc + p], 1).astype(f32)
    t = np.linspace(0.0, 1.0, L, dtype=f32)[:, None]
    w = (f32(TWO_PI) * np.arange(L, dtype=f32)[:, None] / f32(L)).astype(f32)
    bands = np.linspace(1e-4, BANDS - 1, BANDS, dtype=f32)[None, :]
    pos = np.ascontiguousarray(np.concatenate([t, np.cos(bands * w), -np.sin(bands * w)], 1).T.astype(f32))
    deltas = np.linspace(np.log(1e-2) / 1.5, np.log(1e-2) / 0.3, D, dtype=f32)
    dec = np.exp(-t * np.abs(deltas)).astype(f32)
    tokens = [np.arange(256 * mt, 256 * mt + 256)[par::2] for par in range(2) for mt in range(2)]
    decay = np.stack([dec[x] for x in tokens])
    freq, mm = np.arange(256), np.arange(256)
    fwd, inv = np.zeros((P, 4, 2, 256)), np.zeros((P, 4, 2, 256))
    for a in range(4):
        th = TWO_PI * np.outer(2 * mm + a // 2, freq) / (2 * L)
        fm = np.cos(th) if a % 2 == 0 else np.sin(th)
        im = 2.0 * fm
        if a % 2 == 0:
            im[:, 0] = 1.0
        else:
            fm[:, 0] = im[:, 0] = (-1.0) ** mm
        fwd[:, a] = fm.reshape(2, P, 256).transpose(1, 0, 2)
        inv[:, a] = im.T.reshape(2, P, 256).transpose(1, 0, 2) / (2 * L) / D
    return dict(mats=m, rope=rope, dist=dist, posT=pos, decay=decay, fwd=fwd.astype(f32), inv=inv.astype(f32))


def columns(v):
    return v.reshape(-1, P).T


def units(w_, order=None):
    k, n = w_.shape
    u = w_.reshape(k // P, P, n // P, P).transpose(2, 1, 0, 3)
    if order is not None:
        u = u[order]
    return np.ascontiguousarray(u.reshape(len(u), P, k))


def half_units(w_):
    u = units(w_)
    return np.ascontiguousarray(u.reshape(-1, P, 2, U2).transpose(0, 2, 1, 3).reshape(-1, P, U2))


def kernel(**a):
    import concourse.bacc as bacc
    from concourse.bass_utils import run_bass_kernel_spmd

    a = {k: np.asarray(v) for k, v in a.items()}
    heads = np.concatenate([np.arange(HD) + HD * h for t in range(4) for h in (t, 4 + t)])
    w_in = a["w_in"][0]
    w_in = np.concatenate([w_in[:, heads], w_in[:, 512:]], 1)
    w_out = a["w_out"][0]
    w_out = np.concatenate([w_out[heads], w_out[512:]], 0)
    qa, ka, va, qr, kr, vr, gr = 0, 4, 5, 6, 10, 14, 18
    order = [va] + [vr + i for i in range(4)] + [ka] + [kr + i for i in range(4)] + [qa + i for i in range(4)] + \
            [qr + i for i in range(4)] + [gr + i for i in range(4)]
    pair_order = [x for j in range(FT) for x in (j, FT + j)]
    gate_first = [x for j in range(FT) for x in (FT + j, j)]
    hy_order = [x for j in range(KT) for x in (KT + j, 2 * KT + j)] + list(range(KT))
    mod1 = units(a["w_mod"][0])
    weights = dict(
        mod_a=mod1[:16], mod_b=np.concatenate([mod1[16:], units(a["mod_w_2"][0])]), w_in=units(w_in, order),
        w_out=units(w_out), ffn_in=units(a["w_ffn_in"][0], pair_order), ffn_out=half_units(a["w_ffn_out"][0]),
        hy_in=units(a["hy_w_in_2"][0], hy_order), hy_out=units(a["hy_w_out_2"][0]),
        up=units(a["ffn_w_up_2"][0], gate_first), down=half_units(a["ffn_w_down_2"][0]))

    def rep(v):
        return np.broadcast_to(v.reshape(1, -1), (P, v.size))

    def two(v):
        return np.concatenate([v, v]).reshape(P, 1)
    sc_w = a["hy_sc_w_2"][0].reshape(3, 3 * KT, P)[:, hy_order]
    parts = dict(
        g_pre_mix=columns(a["g_pre_mix"][0]), g_post_mix=columns(a["g_post_mix"][0]),
        g_pre_ffn=columns(a["g_pre_ffn"][0]), g_post_ffn=columns(a["g_post_ffn"][0]),
        b_mod=np.repeat(columns(a["b_mod"][0]), 2, 1), b_mod2=columns(a["mod_b_2"][0]),
        g_hy=columns(a["norm_g_2"][0, 0]), g_ffn2=columns(a["norm_g_2"][0, 1]), g_final=columns(a["final_g_2"]),
        hy_b_in=columns(a["hy_b_in_2"][0])[:, hy_order], hy_sc_w=sc_w.transpose(2, 1, 0).reshape(P, -1),
        hy_sc_b=columns(a["hy_sc_b_2"][0])[:, hy_order], hy_bias=columns(a["hy_bias_2"][0]),
        hy_b_out=columns(a["hy_b_out_2"][0]),
        conv_w=a["ffn_conv_w_2"][0].reshape(9, FT, P).transpose(2, 1, 0).reshape(P, -1),
        conv_b=columns(a["ffn_conv_b_2"][0]), q_g=two(a["q_norm_g"][0]), k_g=two(a["k_norm_g"][0]),
        dec_f=rep(a["ret_decay_fwd"][0]), dec_b=rep(a["ret_decay_bwd"][0]), freq=two(a["hy_freq_2"][0]),
        fb1=two(a["hy_f_b1_2"][0]), fb2=two(a["hy_f_b2_2"][0]), fb3=two(a["hy_f_b3_2"][0]),
        eps=np.full((P, 1), EPS, np.float32), not_first=(np.arange(P) > 0).astype(np.float32).reshape(P, 1),
        c=np.stack([columns(a["c"][0]), columns(a["c_ctx"]), columns(a["c_2"][0])], 2).reshape(P, -1))
    cols = np.concatenate([parts[name] for name, _ in COLS], 1).astype(np.float32)
    fw = np.zeros((HYF, 3, HYF), np.float32)
    fw[0:2 * BANDS + 1, 0] = a["hy_f_w1_2"][0]
    fw[:, 1] = a["hy_f_w2_2"][0]
    fw[:, 2] = a["hy_f_w3_2"][0]

    def tiles(x):
        return np.ascontiguousarray(x[0].T.reshape(KT, P, -1).transpose(1, 0, 2))
    arrays = dict(xT=tiles(a["x"]), ctxT=tiles(a["ctx"]), cols=cols, fw=fw, fwout=a["hy_f_wout_2"][0], **tables())
    arrays = {k: np.ascontiguousarray(v) for k, v in arrays.items()}
    nc = bacc.Bacc("TRN2", target_bir_lowering=False, num_devices=1)
    aps = {k: nc.dram_tensor(k, v.shape, F32, kind="ExternalInput").ap() for k, v in arrays.items()}
    waps = {}
    for name, v in weights.items():
        arrays["w_" + name] = np.ascontiguousarray(v)
        waps[name] = nc.dram_tensor("w_" + name, v.shape, F32, kind="ExternalInput").ap()
    out = nc.dram_tensor("out", (P, KT, L), F32, kind="ExternalOutput").ap()
    build(nc, w=waps, out=out, **aps)
    r = run_bass_kernel_spmd(nc, [arrays], core_ids=[0])
    y = np.asarray(r.results[0]["out"])
    return np.ascontiguousarray(y.transpose(1, 0, 2).reshape(D, L).T)[None]
```

```python
from contextlib import ExitStack

import numpy as np

import concourse.bass as bass
from concourse import mybir

F32 = mybir.dt.float32
F32R = mybir.dt.float32r
ALU = mybir.AluOpType
ACT = mybir.ActivationFunctionType

P = 128
D = 1024
KT = D // P
L = 512
LC = 256
LA = L + LC
HD = 64
HALF = HD // 2
NPAIR = 4
FFN = 2816
FT = FFN // P
NCHUNK = 6
MODU = NCHUNK * KT
GRID_W = 64
ROWS = L // GRID_W
HYF = 64
BANDS = 16
EPS = 1e-6
TWO_PI = 2.0 * np.pi
PI_A = 6.28125
PI_B = float(np.float32(np.round((TWO_PI - PI_A) * 2**21) / 2**21))
PI_C = float(np.float32(TWO_PI - PI_A - PI_B))
PI_SAFE = float(np.nextafter(np.float32(np.pi), np.float32(0)))
MAGIC = 1.5 * 2.0**23
DIST = L + 3 * P
CDIST = L + P

COLS = [("g_pre_mix", KT), ("g_post_mix", KT), ("g_pre_ffn", KT), ("g_post_ffn", KT),
        ("b_mod", 2 * MODU), ("b_mod2", MODU), ("g_hy", KT), ("g_ffn2", KT), ("g_final", KT),
        ("hy_b_in", 3 * KT), ("hy_sc_w", 9 * KT), ("hy_sc_b", 3 * KT), ("hy_bias", KT), ("hy_b_out", KT),
        ("conv_w", 9 * FT), ("conv_b", FT), ("q_g", 1), ("k_g", 1), ("dec_f", 8), ("dec_b", 8),
        ("freq", 1), ("fb1", 1), ("fb2", 1), ("fb3", 1), ("eps", 1), ("not_first", 1), ("c", 3 * KT)]
COL = {}
NCOL = 0
for _name, _w in COLS:
    COL[_name] = NCOL
    NCOL += _w
DERS = [("mod", 2 * MODU), ("mod2", MODU), ("a_mix", KT), ("a_ctx", KT), ("p_mix", KT), ("a_ffn", KT),
        ("p_ffn", KT), ("a_hy", KT), ("p_hy", KT), ("a_ffn2", KT), ("silu_c", 3 * KT), ("lg_f", 8), ("lg_b", 8),
        ("fb", 3), ("inv_norm", KT), ("one", 1), ("taps", 18)]
DER = {}
NDER = 0
for _name, _w in DERS:
    DER[_name] = NDER
    NDER += _w

U1 = KT * P
U2 = FFN // 2
FH = FT // 2
PHASES = [("mod_a", 16, U1, False), ("w_in", 22, U1, True), ("mod_b", 2 * MODU - 16, U1, False),
          ("w_out", 8, U1, True), ("ffn_in", 2 * FT, U1, True), ("ffn_out", 16, U2, True),
          ("hy_in", 24, U1, True), ("hy_out", 8, U1, True), ("up", 2 * FT, U1, True), ("down", 16, U2, True)]
RAW = 4
START, ORD, NUNIT, WIDTH = {}, {}, {}, {}
_g, _o = 0, {True: 0, False: 0}
for _name, _n, _w, _s in PHASES:
    START[_name], ORD[_name], NUNIT[_name], WIDTH[_name] = _g, _o[_s], _n, _w
    _g += _n
    _o[_s] += _n
    assert _name == "mod_a" or _s is False or START[_name] % RAW == ORD[_name] % RAW
KIND = [(s, ORD[name] + i) for name, n, w, s in PHASES for i in range(n)]


class Own:

    def __init__(self, eng, sem):
        self.eng, self.sem, self.n, self.i, self.per = eng, sem, 0, None, 0

    def __call__(self, ins):
        ins.then_inc(self.sem, 1)
        self.n += 1
        self.eng.wait_ge(self.sem, self.n if self.i is None else self.base + self.i * self.per + (self.n - self.base))

    def enter(self, i, per):
        self.base, self.i, self.per = self.n, i, per

    def repeat(self, i):
        self.n, self.i = self.base, i

    def leave(self, times):
        assert self.n - self.base == self.per, (self.n - self.base, self.per)
        self.n = self.base + times * self.per
        self.i = None


def build(nc, xT, ctxT, cols, mats, w, rope, dist, posT, fw, fwout, decay, fwd, inv, out):
    def sb(name, at, shape, dt=F32):
        return nc.alloc_sbuf_tensor_at(name, shape, dt, offset=BASE + at)

    with ExitStack() as stack:
        BASE = (nc.sbuf_base + 63) // 64 * 64
        K = 1024
        COLB = 3712
        colt = sb("colt", 0, [P, NCOL])
        o_der = (NCOL * 4 + 63) // 64 * 64
        dert = sb("dert", o_der, [P, NDER])
        assert o_der + NDER * 4 <= COLB
        feat = sb("feat", COLB, [HYF, L])
        o_mat = COLB + 2 * K
        ones = sb("ones", o_mat, [P, P])
        bones = sb("bones", o_mat + 512, [P, P])
        swap = sb("swap", o_mat + 1024, [P, P])
        ident = sb("ident", o_mat + 1536, [P, P])
        o_x = o_mat + 2 * K
        X = sb("X", o_x, [P, KT, L])
        o_raw = o_x + 16 * K
        wraw = sb("wraw", o_raw, [P, RAW, U2])
        o_ws = o_raw + RAW * U2 * 4
        wsp = sb("wsp", o_ws, [P, 2, 2, U2], F32R)
        o_t = o_ws + 4 * U2 * 4
        o_h = o_t + 20 * K
        H = sb("H", o_h, [P, 2, KT, L], F32R)
        Y = sb("Y", o_h, [P, KT, L])
        o_r = o_h + 32 * K
        assert BASE + o_r + 88 * K <= nc.sbuf_usable_end, (BASE + o_r + 88 * K, nc.sbuf_usable_end)
        sqb = sb("sqb", o_t, [P, 2, L])
        rstd = sb("rstd", o_t + 4 * K, [P, L])
        tb = sb("tb", o_t + 6 * K, [P, 4, L])
        acc = sb("acc", o_t + 14 * K, [P, L])
        rtmp = sb("rtmp", o_t + 18 * K, [P, L])
        posb = sb("posb", o_r + 40 * K, [2 * BANDS + 1, L])
        fwb = sb("fwb", o_r + 42 * K, [HYF, 3, HYF])
        fa = sb("fa", o_r + 44 * K, [HYF, L])
        fk = sb("fk", o_r + 46 * K, [HYF, L])
        fh = sb("fh", o_r + 48 * K, [HYF, L])
        Hc = sb("Hc", o_r, [P, 2, KT, LC], F32R)
        Xc = sb("Xc", o_r + 16 * K, [P, KT, LC])
        V = sb("V", o_r + 16 * K, [P, LA // P, 5 * P])
        ropet = sb("ropet", o_r + 31 * K, [P, 2, L])
        KA = sb("KA", o_r + 35 * K, [P, LA])
        KR = sb("KR", o_r + 38 * K, [P, NPAIR, LA])
        QA = sb("QA", o_r + 50 * K, [P, NPAIR, L])
        QR = sb("QR", o_r + 58 * K, [P, NPAIR, L])
        G = sb("G", o_r + 66 * K, [P, NPAIR, L])
        VT = sb("VT", o_t, [P, 2, LA])
        RU = sb("RU", o_t + 6 * K, [P, 2, LA])
        SQ = sb("SQ", o_t + 12 * K, [P, LA])
        RT = sb("RT", o_t + 15 * K, [P, LA])
        RM = sb("RM", o_t + 18 * K, [P, L])
        Pb = sb("Pb", o_r + 74 * K, [P, 2, LA])
        PT = sb("PT", o_r + 80 * K, [P, 2, LA])
        strip = sb("strip", o_r, [P, 2, DIST + CDIST])
        ea = sb("ea", o_r + 12 * K, [P, DIST])
        ec = sb("ec", o_r + 31 * K, [P, CDIST])
        smx = sb("smx", o_r + 86 * K, [P, 2])
        mxr = sb("mxr", o_r + 86 * K + 128, [P, 2])
        rinv = sb("rinv", o_r + 86 * K + 192, [P, 2])
        rsum = sb("rsum", o_r + 86 * K + 64, [P, 2])
        mprod = sb("mprod", o_ws, [P, 2, U1])
        msum = sb("msum", o_ws + 8 * K, [P, 8, P])
        distt = sb("distt", o_t, [P, 3 * DIST + 2 * CDIST])
        pr = sb("pr", o_t + (3 * DIST + 2 * CDIST) * 4, [P, 2, L])
        assert (3 * DIST + 2 * CDIST) * 4 + 4 * K <= 20 * K
        Ym = sb("Ym", o_r, [P, KT, L])
        hid = sb("hid", o_r, [P, 2, FT, L], F32R)
        sl = sb("sl", o_t, [P, 2, L])
        hv = sb("hv", o_t + 4 * K, [P, 2, L])
        PW = GRID_W + 2
        gb = sb("gb", o_t + 8 * K, [P, 2, ROWS + 2, PW])
        cva = sb("cva", o_t + 14 * K, [P, 2, ROWS, GRID_W])
        cvb = sb("cvb", o_t + 18 * K, [P, ROWS, GRID_W])
        cvt = sb("cvt", COLB, [P, ROWS, GRID_W])
        fwdt = sb("fwdt", o_r, [P, 4, 2, 256])
        invt = sb("invt", o_r + 8 * K, [P, 4, 2, 256])
        dect = sb("dect", o_r + 8 * K, [P, 4, 512])
        KS = sb("KS", o_r + 16 * K, [P, 2, 2, 4, 512])
        Z = sb("Z", o_r + 48 * K, [P, KT, L])
        X0 = sb("X0", o_r + 64 * K, [P, KT, L])
        HP = sb("HP", o_r + 48 * K, [P, 4, D])
        HM = sb("HM", o_r + 64 * K, [P, 4, D])
        fwo = sb("fwo", o_r + 80 * K, [HYF, 2 * D])
        fA = sb("fA", o_r + 32 * K, [P, 2, 512])
        fB = sb("fB", o_r + 36 * K, [P, 2, 512])
        aab = sb("aab", o_r + 40 * K, [P, 2, 2, 512])
        kE = sb("kE", o_r + 8 * K, [P, 2, 2, 512])
        absum = sb("absum", o_t + 14 * K, [P, D])
        cb_ = sb("cb_", o_t, [P, 2, L + 2])
        ca = sb("ca", o_t + 5 * K, [P, 2, L])
        x1c = sb("x1c", o_t + 9 * K, [P, L])
        zN = sb("zN", o_h, [P, 4, D])
        zs = sb("zs", o_h + 16 * K, [P, 8, 512])
        zE = sb("zE", o_t, [P, 2, 512])
        zpD = sb("zpD", o_t + 4 * K, [P, 3, 512])
        zpP = sb("zpP", o_t + 10 * K, [P, 3, 512])
        row = sb("row", o_t + 16 * K, [1, 2, 512])
        yt = sb("yt", o_t, [P, 2, L])
        yv = sb("yv", o_t + 4 * K, [P, 2, L])
        hyt = sb("hyt", o_t + 16 * K, [P, 2, L])
        cen = sb("cen", o_t, [P, 2, L])
        gsq = sb("gsq", o_t + 4 * K, [P, 2, L])
        grs = sb("grs", o_t + 8 * K, [P, L])
        gv = sb("gv", o_t + 10 * K, [P, 2, L])

        PS = stack.enter_context(nc.psum_tensor("PS", [P, 8, 512], F32))

        def col(name, i=0, n=1):
            return colt[:, COL[name] + i:COL[name] + i + n]

        def der(name, i=0, n=1):
            return dert[:, DER[name] + i:DER[name] + i + n]

        def sem(name):
            return stack.enter_context(nc.semaphore(name))

        s_small = sem("s_small")
        s_feat = sem("s_feat")
        s_x = sem("s_x")
        s_xc = sem("s_xc")
        s_rope = sem("s_rope")
        s_dist = sem("s_dist")
        s_hyc = sem("s_hyc")
        s_dec = [sem(f"s_dec{i}") for i in range(4)]
        s_inv = sem("s_inv")
        s_out = sem("s_out")
        wload = [sem(f"wload{i}") for i in range(RAW)]
        w_hi = sem("w_hi")
        w_lo = sem("w_lo")
        w_done = sem("w_done")
        mod_done = sem("mod_done")
        m_pr = [sem("m_prD"), sem("m_prP")]
        m_sum = [sem("m_sumD"), sem("m_sumP")]
        s_act = sem("s_act")
        s_dve = sem("s_dve")
        s_pool = sem("s_pool")
        silu_c = sem("silu_c")
        f_mm, f_arg, f_sin = sem("f_mm"), sem("f_arg"), sem("f_sin")
        n_sq, n_acc, n_ss, n_rt = sem("n_sq"), sem("n_acc"), sem("n_ss"), sem("n_rt")
        n_rs, n_hi, n_h, n_x = sem("n_rs"), sem("n_hi"), sem("n_h"), sem("n_x")
        n_t = [sem("n_tD"), sem("n_tP")]
        n_fin = [sem("n_fin0"), sem("n_fin1")]
        n_y = sem("n_y")
        m_cols = sem("m_cols")
        m_gain = sem("m_gain")
        q_ev, q_sw, q_ss, q_rt, q_done, v_tr, v_ev = (sem("q_ev"), sem("q_sw"), sem("q_ss"), sem("q_rt"),
                                                      sem("q_done"), sem("v_tr"), sem("v_ev"))
        a_s, a_mx, a_exp, a_p, a_tr, a_pt, a_pv, a_o = (sem("a_s"), sem("a_mx"), sem("a_exp"), sem("a_p"),
                                                        sem("a_tr"), sem("a_pt"), sem("a_pv"), sem("a_o"))
        r_u, r_e, r_strip, r_s, r_p, r_pv, r_o = (sem("r_u"), sem("r_e"), sem("r_strip"), sem("r_s"), sem("r_p"),
                                                  sem("r_pv"), sem("r_o"))
        a_h = sem("a_h")
        g_c, g_sq, g_var, g_rt, g_y, g_h = (sem("g_c"), sem("g_sq"), sem("g_var"), sem("g_rt"), sem("g_y"),
                                            sem("g_h"))
        g_hi = sem("g_hi")
        h_sl, h_val, h_hi, h_lo, h_g, h_cv = (sem("h_sl"), sem("h_val"), sem("h_hi"), sem("h_lo"), sem("h_g"),
                                              sem("h_cv"))
        h_tp = sem("h_tp")
        h_ct = sem("h_ct")
        h_cp = sem("h_cp")
        k_h, k_ab, k_hp, k_col, k_f, k_e, k_k = (sem("k_h"), sem("k_ab"), sem("k_hp"), sem("k_col"), sem("k_f"),
                                                 sem("k_e"), sem("k_k"))
        y_b, y_c, y_z, z_tr, z_n, z_f, z_e, z_b, z_q, z_y = (
            sem("y_b"), sem("y_c"), sem("y_z"), sem("z_tr"), sem("z_n"), sem("z_f"), sem("z_e"), sem("z_b"),
            sem("z_q"), sem("z_y"))
        i_mm, i_ev, i_val, i_hi, i_h = sem("i_mm"), sem("i_ev"), sem("i_val"), sem("i_hi"), sem("i_h")
        o_ev = sem("o_ev")
        z_p, z_w = sem("z_p"), sem("z_w")
        k_abs, k_sum, k_inv = sem("k_abs"), sem("k_sum"), sem("k_inv")
        m_lg, g_rs, g_val = sem("m_lg"), sem("g_rs"), sem("g_val")
        a_hi = sem("a_hi")

        block = stack.enter_context(nc.Block())

        NCTX = 10
        NV = 5
        NROPE = 13
        DVE_TAPS, POOL_TAPS = (0, 1, 2, 3, 5), (6, 7, 8)
        PE_SUMS = (3, 5)

        def totals(k):
            return len([j for j in range(k + 1) if j not in PE_SUMS])
        NH = {0: 0, 1: KT, 3: 2 * KT, 5: 3 * KT, 6: 4 * KT}
        NX = {2: 0, 4: KT}

        def wait_buffer(eng, t):
            if t >= 4:
                k, kt = (t - 4) // KT, (t - 4) % KT
                eng.wait_ge(n_x if k in NX else n_h, (NX[k] if k in NX else NH[k]) + kt + 1)
        LAG = 2
        STEPS = 32 + LAG

        def ret_steps(s):
            s -= LAG
            return range(s * 3 // 2, (s + 1) * 3 // 2) if s >= 0 else range(0)

        def mod_units(s):
            if not 0 <= s < 32:
                return range(0)
            first = 16 + 2 * s + 2 * ((s + 3) // 4)
            return range(first, first + (4 if s % 4 == 0 else 2))

        @block.sync
        def _(sp):
            def load(name, i, dst_slot, src):
                sp.dma_start(wraw[:, dst_slot, 0:WIDTH[name]], src).then_inc(wload[dst_slot], 16)

            def load_static(name, i):
                g = START[name] + i
                if g >= RAW:
                    split, ordinal = KIND[g - RAW]
                    if split:
                        sp.wait_ge(w_lo, ordinal + 1)
                    elif ordinal < 16:
                        sp.wait_ge(mod_done, ordinal + 1)
                    else:
                        sp.wait_ge(m_pr[ordinal % 2], (ordinal - 16) // 2 + 1)
                load(name, i, g % RAW, w[name][i])

            def load_loop(name, first, times):
                with sp.Fori(0, times) as i:
                    for u in range(RAW):
                        sp.wait_ge(w_lo, i * RAW + (ORD[name] + first + u - RAW + 1))
                        load(name, i, (START[name] + first + u) % RAW, w[name][i * RAW + (first + u)])

            sp.dma_start(colt[:, :], cols).then_inc(s_small, 16)
            sp.dma_start(posb[:, :], posT).then_inc(s_feat, 16)
            sp.dma_start(fwb[:, :, :], fw).then_inc(s_feat, 16)
            for j, m in enumerate((ones, bones, swap, ident)):
                sp.dma_start(m[:, :], mats[j]).then_inc(s_small, 16)
            for i in range(RAW):
                load_static("mod_a", i)
            sp.dma_start(X[:, :, :], xT).then_inc(s_x, 16)
            sp.dma_start(Xc[:, :, :], ctxT).then_inc(s_xc, 16)
            sp.dma_start(ropet[:, :, :], rope).then_inc(s_rope, 16)
            for i in range(RAW, 16):
                load_static("mod_a", i)
            for i in range(22):
                load_static("w_in", i)
            for i in range(RAW):
                load_static("mod_b", i)
            sp.wait_ge(q_done, NROPE)
            sp.wait_ge(v_ev, NV)
            sp.dma_start(distt[:, :], dist).then_inc(s_dist, 16)
            with sp.Fori(1, (2 * MODU - 16) // RAW) as i:
                for u in range(RAW):
                    sp.wait_ge(m_pr[u % 2], i * (RAW // 2) + (u // 2 + 1 - RAW // 2))
                    load("mod_b", i, (START["mod_b"] + u) % RAW, w["mod_b"][i * RAW + u])
            for i in range(8):
                load_static("w_out", i)
            load_loop("ffn_in", 0, 2 * FT // RAW)
            load_loop("ffn_out", 0, 4)
            for i in range(RAW):
                load_static("hy_in", i)
            sp.wait_ge(w_done, ORD["hy_in"])
            sp.dma_start(fwo[:, :], fwout).then_inc(s_hyc, 16)
            for t in range(4):
                sp.dma_start(dect[:, t, :], decay[0, t]).then_inc(s_dec[t], 16)
            sp.dma_start(fwdt[:, :, :, :], fwd).then_inc(s_hyc, 16)
            for t in range(4):
                sp.wait_ge(k_ab, t + 1)
                sp.dma_start(dect[:, t, :], decay[1, t]).then_inc(s_dec[t], 16)
            sp.wait_ge(k_k, 4)
            sp.dma_start(invt[:, :, :, :], inv).then_inc(s_inv, 16)
            load_loop("hy_in", RAW, 5)
            for i in range(8):
                load_static("hy_out", i)
            load_loop("up", 0, 2 * FT // RAW)
            load_loop("down", 0, 4)
            for q in range(2):
                sp.wait_ge(n_fin[0], 3 * (q + 1))
                sp.wait_ge(n_fin[1], q + 1)
                sp.dma_start(out[:, 4 * q:4 * q + 4], Y[:, 4 * q:4 * q + 4, :]).then_inc(s_out, 16)
            sp.wait_ge(s_out, 32)

        def split_hi(act, name, i, r=None):
            o, g, n = ORD[name] + i, START[name] + i, WIDTH[name]
            k = 0 if r is None else r
            act.wait_ge(wload[g % RAW], k * 16 + 16 * (g // RAW + 1))
            if o >= 2:
                act.wait_ge(w_done, k * RAW + (o - 1))
            nc.scalar.activation(wsp[:, o % 2, 0, 0:n], wraw[:, g % RAW, 0:n], ACT.Copy).then_inc(w_hi, 1)

        def split_lo(dve, name, i, r=None):
            o, g, n = ORD[name] + i, START[name] + i, WIDTH[name]
            k = 0 if r is None else r
            dve.wait_ge(w_hi, k * RAW + (o + 1))
            nc.vector.tensor_tensor(wsp[:, o % 2, 1, 0:n], wraw[:, g % RAW, 0:n],
                                    wsp[:, o % 2, 0, 0:n].bitcast(F32), ALU.subtract).then_inc(w_lo, 1)

        def split_matmuls(pe, o, psum, h, kts, wk0, first, last, ready=None):
            mm = None
            for kt in kts:
                wk = kt - wk0
                if ready is not None:
                    pe.wait_ge(ready[0], ready[1] + kt + 1)
                for a, b in ((0, 0), (0, 1), (1, 0)):
                    mm = nc.tensor.matmul(psum, wsp[:, o % 2, a, wk * P:(wk + 1) * P], h[:, b, kt, :],
                                          start=first and kt == kts[0] and (a, b) == (0, 0),
                                          stop=last and kt == kts[-1] and (a, b) == (1, 0))
            return mm

        def mod_multiply(eng, ops, m):
            g, e = START["mod_b"] + m - 16, (m - 16) % 2
            eng.wait_ge(wload[g % RAW], 16 * (g // RAW + 1))
            a = DER["silu_c"] + (0 if m < MODU else 2)
            ops.tensor_tensor(mprod[:, e, :].rearrange("p (k n) -> p k n", n=P),
                              wraw[:, g % RAW, 0:U1].rearrange("p (k n) -> p k n", n=P),
                              dert[:, a:a + 3 * KT - 2:3].unsqueeze(2).to_broadcast([P, KT, P]),
                              ALU.mult).then_inc(m_pr[e], 1)

        @block.tensor
        def _(pe):
            pe.wait_ge(s_feat, 32)
            pe.wait_ge(s_small, 80)
            for l in range(3):
                if l:
                    pe.wait_ge(f_sin, l)
                k = 2 * BANDS + 1 if l == 0 else HYF
                nc.tensor.matmul(PS[0:HYF, 6, :], fwb[0:k, l, :], posb[:, :] if l == 0 else fh[:, :],
                                 start=True, stop=True).then_inc(f_mm, 1)

            def modulation(m):
                pe.wait_ge(wload[m % RAW], 16 * (m // RAW + 1))
                for kt in range(KT):
                    mm = nc.tensor.matmul(PS[:, 7, 2 * m:2 * m + 2], wraw[:, m % RAW, kt * P:(kt + 1) * P],
                                          dert[:, DER["silu_c"] + 3 * kt:DER["silu_c"] + 3 * kt + 2],
                                          start=kt == 0, stop=kt == KT - 1)
                mm.then_inc(mod_done, 1)

            def modulation_total(m):
                pe.wait_ge(m_sum[m % 2], (m - 16) // 2 + 1)
                c = 2 * m if m < MODU else MODU + m
                nc.tensor.matmul(PS[:, 7, c:c + 1], msum[:, m % 8, :], der("one"), start=True,
                                 stop=True).then_inc(mod_done, 1)

            def total(k, bank=6):
                pe.wait_ge(n_acc, KT * (k + 1))
                n = LC if k == 1 else L
                nc.tensor.matmul(PS[:, bank, 0:n], ones[:, :], acc[:, 0:n], start=True, stop=True).then_inc(n_ss, 1)

            def filter_tile(j):
                c, t = j // 4, j % 4
                par, mt = t // 2, t % 2
                if j:
                    pe.wait_ge(k_ab, j)
                for d in range(2):
                    mm = nc.tensor.matmul(PS[:, 4 + d, :], feat[:, mt * 256 + par:(mt + 1) * 256:2],
                                          fwo[:, d * D + c * 512:d * D + c * 512 + 512], start=True, stop=True)
                mm.then_inc(k_h, 1)

            def squares_total(k, kts=range(KT)):
                pe.wait_ge(n_rt, k)
                for kt in kts:
                    q = k * KT + kt
                    pe.wait_ge(n_sq, q + 1)
                    nc.tensor.matmul(PS[:, 6, :], ones[:, :], sqb[:, q % 2, :], start=kt == 0,
                                     stop=kt == KT - 1).then_inc(n_acc, 1)

            pe.wait_ge(silu_c, 1)
            for m in range(8):
                modulation(m)
            pe.wait_ge(f_arg, 3)
            total(0)
            for m in range(8, 16):
                modulation(m)
            pe.wait_ge(n_rt, 1)
            total(1)

            def aux(n):
                if n < NV:
                    pe.wait_ge(q_ev, n + 1)
                    if n == 0:
                        pe.wait_ge(m_cols, 1)
                    else:
                        pe.wait_ge(v_ev, n)
                    for t in range(LA // P):
                        tr = nc.tensor.transpose(PS[:, 6 + t // 4, (t % 4) * P:(t % 4 + 1) * P],
                                                 VT[:, n % 2, t * P:(t + 1) * P], ident[:, :])
                    tr.then_inc(v_tr, 1)
                elif n < NV + NROPE:
                    pe.wait_ge(q_ev, n + 1)
                    pe.wait_ge(v_ev, NV)
                    if n > NV:
                        pe.wait_ge(q_done, n - NV)
                    nc.tensor.matmul(PS[:, 4, :], swap[:, :], RU[:, n % 2, 0:L], start=True, stop=True).then_inc(q_sw, 1)
                    if n == NV or 10 <= n < 14:
                        mm = nc.tensor.matmul(PS[:, 5, :], bones[:, :], SQ[:, 0:L], start=True, stop=True)
                        if n == NV:
                            mm = nc.tensor.matmul(PS[:, 6, 0:LC], bones[:, :], SQ[:, L:LA], start=True, stop=True)
                        mm.then_inc(q_ss, 1)

            for n in range(22):
                pe.wait_ge(w_lo, ORD["w_in"] + n + 1)
                if n >= 2:
                    pe.wait_ge(q_ev, n - 1)
                mm = split_matmuls(pe, ORD["w_in"] + n, PS[:, n % 2, :], H, range(KT), 0, True, True,
                                   (n_h, 0) if n == 0 else None)
                if n < NCTX:
                    mm = split_matmuls(pe, ORD["w_in"] + n, PS[:, 2 + n % 2, 0:LC], Hc, range(KT), 0, True, True,
                                       (n_h, KT) if n == 0 else None)
                mm.then_inc(w_done, 1)
                if n:
                    aux(n - 1)

            def att_scores(s):
                t, lo, qt = s // 8, (s // 4) % 2 * HD, s % 4
                if s == 0:
                    pe.wait_ge(q_ev, 22)
                    pe.wait_ge(q_done, NROPE)
                else:
                    pe.wait_ge(a_exp, s)
                for a, b, bank in ((0, L, 0), (L, LA, 1)):
                    mm = nc.tensor.matmul(PS[:, bank, 0:b - a], QA[lo:lo + HD, t, qt * P:(qt + 1) * P],
                                          KA[lo:lo + HD, a:b], start=True, stop=True)
                mm.then_inc(a_s, 1)

            def att_transposes(s):
                pe.wait_ge(a_p, s + 1)
                if s:
                    pe.wait_ge(a_pt, s)
                for kt in range(LA // P):
                    tr = nc.tensor.transpose(PS[:, 2 + kt // 4, (kt % 4) * P:(kt % 4 + 1) * P],
                                             Pb[:, s % 2, kt * P:(kt + 1) * P], ident[:, :])
                tr.then_inc(a_tr, 1)

            def att_values(s):
                lo, qt = (s // 4) % 2 * HD, s % 4
                pe.wait_ge(a_pt, s + 1)
                if s % 8 == 0 and s:
                    pe.wait_ge(a_o, s // 8)
                for kt in range(LA // P):
                    mm = nc.tensor.matmul(PS[lo:lo + HD, 4, qt * P:(qt + 1) * P], V[:, kt, lo:lo + HD],
                                          PT[:, s % 2, kt * P:(kt + 1) * P], start=kt == 0, stop=kt == LA // P - 1)
                mm.then_inc(a_pv, 1)

            def ret_scores(r):
                h, kt = r // 6, r % 6
                lo = h % 2 * HD
                if r:
                    pe.wait_ge(r_p, r)
                nc.tensor.matmul(PS[:, 5, :], KR[lo:lo + HD, h // 2, kt * P:(kt + 1) * P],
                                 QR[lo:lo + HD, h // 2, :], start=True, stop=True).then_inc(r_s, 1)

            def ret_values(r):
                h, kt = r // 6, r % 6
                lo = h % 2 * HD
                pe.wait_ge(r_p, r + 1)
                if r % 12 == 0 and r:
                    pe.wait_ge(r_o, r // 12)
                nc.tensor.matmul(PS[lo:lo + HD, 6, :], V[:, kt, P + h * HD:P + (h + 1) * HD], pr[:, r % 2, :],
                                 start=kt == 0, stop=kt == 5).then_inc(r_pv, 1)

            for s in range(STEPS):
                rs = ret_steps(s)
                ms = list(mod_units(s - 2))
                if rs:
                    ret_scores(rs[0])
                if s < 32:
                    att_scores(s)
                if 0 < s <= 32:
                    att_transposes(s - 1)
                for m in ms[:2]:
                    modulation_total(m)
                if rs:
                    ret_values(rs[0])
                if len(rs) == 2:
                    ret_scores(rs[1])
                if 0 < s <= 32:
                    att_values(s - 1)
                if len(rs) == 2:
                    ret_values(rs[1])
                for m in ms[2:]:
                    modulation_total(m)

            pe.wait_ge(r_o, 4)
            for t in range(4):
                nc.tensor.matmul(PS[:, t, :], bones[:, :], QR[:, t, :], start=True, stop=True).then_inc(g_c, 1)
            for t in range(4):
                pe.wait_ge(g_sq, t + 1)
                nc.tensor.matmul(PS[:, t, :], bones[:, :], gsq[:, t % 2, :], start=True, stop=True).then_inc(g_var, 1)

            for n in range(8):
                pe.wait_ge(w_lo, ORD["w_out"] + n + 1)
                if n == 0:
                    pe.wait_ge(a_o, 4)
                    pe.wait_ge(g_h, 4)
                if n >= 2:
                    pe.wait_ge(n_y, n - 1)
                split_matmuls(pe, ORD["w_out"] + n, PS[:, n % 2, :], H, range(KT), 0, True, True).then_inc(w_done, 1)
            total(2)
            squares_total(3)

            def pairs(name, normed, free_a, base_a, free_b, base_b):
                def four(i, first):
                    for u in range(4):
                        pe.wait_ge(w_lo, i * 4 + (ORD[name] + u + 1))
                        if not first:
                            free, base = (free_a, base_a) if u % 2 == 0 else (free_b, base_b)
                            pe.wait_ge(free, i * 2 + (base + u // 2 - 1))
                        split_matmuls(pe, ORD[name] + u, PS[:, u, :], H, range(KT), 0, True, True,
                                      (n_h, normed) if first and u == 0 else None).then_inc(w_done, 1)
                four(0, True)
                with pe.Fori(1, FT // 2) as i:
                    four(i, False)

            def down(name, base_h, free, base):
                def four(i, first):
                    for u in range(4):
                        pe.wait_ge(w_lo, i * 4 + (ORD[name] + u + 1))
                        if not first and u % 2 == 0:
                            pe.wait_ge(free, i * 2 + (base + u // 2 - 1))
                        k0 = u % 2 * FH
                        split_matmuls(pe, ORD[name] + u, PS[:, u // 2, :], hid, range(k0, k0 + FH), k0, u % 2 == 0,
                                      u % 2 == 1, (h_lo, base_h) if first and u < 2 else None).then_inc(w_done, 1)
                four(0, True)
                with pe.Fori(1, 4) as i:
                    four(i, False)

            pairs("ffn_in", 2 * KT, h_sl, 0, h_val, 0)
            down("ffn_out", 0, n_y, KT)

            total(4)
            pe.wait_ge(s_hyc, 32)

            def spectrum_part(a, cos_src, sin_src, c, f, b0):
                src = cos_src if a % 2 == 0 else sin_src
                for mt in range(2):
                    mm = nc.tensor.matmul(PS[:, b0 + a, :], fwdt[:, a, mt, f * P:(f + 1) * P],
                                          src[:, (a // 2) * 2 + mt, c * 512:(c + 1) * 512], start=mt == 0,
                                          stop=mt == 1)
                if cos_src is not sin_src and a == 1 and f == 0:
                    for mt in range(2):
                        mm = nc.tensor.matmul(PS[0:1, b0 + a, :], fwdt[:, a, mt, 0:1],
                                              cos_src[:, mt, c * 512:(c + 1) * 512], start=mt == 0, stop=mt == 1)
                return mm

            def spectrum(cos_src, sin_src, c, f, b0):
                for a in range(4):
                    mm = spectrum_part(a, cos_src, sin_src, c, f, b0)
                return mm

            filter_tile(0)
            filter_tile(1)
            squares_total(5, range(0, 2))
            filter_tile(2)
            squares_total(5, range(2, 5))
            filter_tile(3)
            squares_total(5, range(5, KT))
            filter_tile(4)
            pe.wait_ge(k_hp, 4)
            for a in range(4):
                mm = spectrum_part(a, HP, HM, 0, 0, 0)
                if a < 3:
                    filter_tile(5 + a)
            mm.then_inc(k_f, 1)
            for k in range(1, 4):
                if k == 1:
                    pe.wait_ge(n_rt, 6)
                    pe.wait_ge(k_ab, 8)
                else:
                    pe.wait_ge(k_hp, 8)
                    pe.wait_ge(k_k, k - 1)
                spectrum(HP, HM, k // 2, k % 2, 4 * (k % 2)).then_inc(k_f, 1)
            pe.wait_ge(k_sum, 8)
            pe.wait_ge(k_k, 3)
            for j in range(KT):
                mm = nc.tensor.matmul(PS[:, 0, j:j + 1], absum[:, j * P:(j + 1) * P], ones[:, 0:1],
                                      start=True, stop=True)
            mm.then_inc(k_col, 1)

            def hy_four(i, first):
                for u in range(4):
                    pe.wait_ge(w_lo, i * 4 + (ORD["hy_in"] + u + 1))
                    if first and u == 0:
                        pe.wait_ge(k_inv, 1)
                    if not (first and u < 2):
                        pe.wait_ge(y_b, i * 4 + (u - 1))
                    split_matmuls(pe, ORD["hy_in"] + u, PS[:, u % 2, :], H, range(KT), 0, True, True,
                                  (n_h, 3 * KT) if first and u == 0 else None).then_inc(w_done, 1)
            hy_four(0, True)
            with pe.Fori(1, 6) as i:
                hy_four(i, False)

            pe.wait_ge(y_z, KT)
            pe.wait_ge(y_b, 24)
            for g in range(8):
                par, mt, c = g // 4, g // 2 % 2, g % 2
                if g >= 4:
                    pe.wait_ge(z_n, g - 3)
                for j in range(4):
                    tr = nc.tensor.transpose(PS[:, g % 4, j * P:(j + 1) * P],
                                             Z[:, 4 * c + j, mt * 256 + par:(mt + 1) * 256:2], ident[:, :])
                tr.then_inc(z_tr, 1)
            pe.wait_ge(z_n, 8)
            for k in range(4):
                if k >= 2:
                    pe.wait_ge(z_b, k - 1)
                spectrum(zN, zN, k // 2, k % 2, 4 * (k % 2)).then_inc(z_f, 1)
            pe.wait_ge(s_inv, 16)
            pe.wait_ge(z_y, 4)
            for j in range(KT):
                if j >= 4:
                    pe.wait_ge(i_ev, j - 3)
                for par in range(2):
                    for n in range(4):
                        a, f = 2 * par + n // 2, n % 2
                        mm = nc.tensor.matmul(PS[:, j % 4, par * 256:(par + 1) * 256],
                                              KS[:, j // 4, f, a, (j % 4) * P:(j % 4 + 1) * P], invt[:, a, f, :],
                                              start=n == 0, stop=n == 3)
                mm.then_inc(i_mm, 1)
            for n in range(8):
                pe.wait_ge(w_lo, ORD["hy_out"] + n + 1)
                if n >= 2:
                    pe.wait_ge(o_ev, n - 1)
                split_matmuls(pe, ORD["hy_out"] + n, PS[:, n % 2, :], H, range(KT), 0, True, True,
                              (i_h, 0) if n == 0 else None).then_inc(w_done, 1)
            total(6)
            pairs("up", 4 * KT, h_ct, 0, h_val, FT)
            down("down", FT, n_x, 3 * KT)
            total(7)

        @block.scalar
        def _(act):
            own = Own(act, s_act)
            SC = nc.scalar

            def root(k):
                if k in PE_SUMS:
                    act.wait_ge(n_acc, KT * (k + 1))
                else:
                    act.wait_ge(n_ss, totals(k))
                if k:
                    act.wait_ge(n_rs, k)
                n = LC if k == 1 else L
                SC.activation(rtmp[:, 0:n], PS[:, 6, 0:n], ACT.Sqrt, bias=col("eps")).then_inc(n_rt, 1)

            def square(q, src, n=L):
                if q >= 2:
                    act.wait_ge(n_acc, q - 1)
                SC.activation(sqb[:, q % 2, 0:n], src, ACT.Square).then_inc(n_sq, 1)

            def high(k, kt, dst, shift, n=L):
                act.wait_ge(n_t[kt % 2], (k * KT + kt) // 2 + 1)
                SC.activation(dst, tb[:, (k * KT + kt) % 4, 0:n], ACT.Identity, bias=shift).then_inc(n_hi, 1)

            def mod_col(chunk, kt, which=0):
                a = DER["mod"] + 2 * (KT * chunk + kt) + which
                return dert[:, a:a + 1]

            def mod2_col(chunk, kt):
                return der("mod2", KT * chunk + kt)

            act.wait_ge(s_small, 80)
            SC.activation(der("silu_c", 0, 3 * KT), col("c", 0, 3 * KT), ACT.Silu).then_inc(silu_c, 1)
            SC.activation(der("lg_f", 0, 8), col("dec_f", 0, 8), ACT.Exp).then_inc(m_lg, 1)
            SC.activation(der("lg_b", 0, 8), col("dec_b", 0, 8), ACT.Exp).then_inc(m_lg, 1)
            for l in range(3):
                act.wait_ge(f_arg, l + 1)
                if l:
                    act.wait_ge(f_mm, l + 1)
                SC.activation((fh if l < 2 else feat)[:, :], fa[:, :], ACT.Sin).then_inc(f_sin, 1)
            act.wait_ge(s_x, 16)
            for kt in range(KT):
                square(kt, X[:, kt, :])
            root(0)
            act.wait_ge(s_xc, 16)
            for kt in range(KT):
                square(KT + kt, Xc[:, kt, :], LC)
            root(1)
            split_hi(act, "w_in", 0)
            split_hi(act, "w_in", 1)
            for kt in range(KT):
                high(0, kt, H[:, 0, kt, :], mod_col(0, kt))
            for kt in range(KT):
                high(1, kt, Hc[:, 0, kt, :], mod_col(0, kt, 1), LC)

            def normed_head(n):
                return n == NV or 10 <= n < 14

            for n in range(22):
                act.wait_ge(w_done, ORD["w_in"] + n + 1)
                if n + 2 < 22:
                    split_hi(act, "w_in", n + 2)
                lat, ctx = PS[:, n % 2, :], PS[:, 2 + n % 2, 0:LC]
                if n == 0:
                    act.wait_ge(n_h, 2 * KT)
                m = n - 1
                if normed_head(m):
                    act.wait_ge(q_ss, 1 if m == NV else m - 8)
                    if m == NV:
                        own(SC.activation(RT[:, L:LA], PS[:, 6, 0:LC], ACT.Sqrt, bias=col("eps")))
                    else:
                        act.wait_ge(q_done, m - NV)
                    SC.activation(RT[:, 0:L], PS[:, 5, :], ACT.Sqrt, bias=col("eps")).then_inc(q_rt, 1)
                if n < NV:
                    if n >= 2:
                        act.wait_ge(v_tr, n - 1)
                    own(SC.activation(VT[:, n % 2, 0:L], lat, ACT.Copy))
                    SC.activation(VT[:, n % 2, L:LA], ctx, ACT.Copy).then_inc(q_ev, 1)
                    continue
                if n < 18 and n - NV >= 2:
                    act.wait_ge(q_done, n - NV - 1)
                if normed_head(n):
                    g = col("k_g") if n == NV else col("q_g")
                    own(SC.activation(SQ[:, 0:L], lat, ACT.Square))
                    if n == NV:
                        own(SC.activation(SQ[:, L:LA], ctx, ACT.Square))
                        own(SC.activation(RU[:, n % 2, L:LA], ctx, ACT.Copy, scale=g))
                    SC.activation(RU[:, n % 2, 0:L], lat, ACT.Copy, scale=g).then_inc(q_ev, 1)
                elif n < 10:
                    own(SC.activation(KR[:, n - 6, L:LA], ctx, ACT.Copy, scale=HD**-0.5))
                    SC.activation(RU[:, n % 2, 0:L], lat, ACT.Copy, scale=HD**-0.5).then_inc(q_ev, 1)
                elif n < 18:
                    SC.activation(RU[:, n % 2, 0:L], lat, ACT.Copy).then_inc(q_ev, 1)
                else:
                    SC.activation(G[:, n - 18, :], lat, ACT.Silu).then_inc(q_ev, 1)

            def exp_strip(h):
                act.wait_ge(r_u, h + 1)
                if h >= 2:
                    act.wait_ge(r_p, 6 * (h - 1))
                if h:
                    act.wait_ge(r_strip, h)
                own(SC.activation(ea[:, :], ea[:, :], ACT.Exp))
                own(SC.activation(strip[:, h % 2, DIST:], distt[:, 3 * DIST:3 * DIST + CDIST], ACT.Exp,
                                  scale=der("lg_f", h)))
                SC.activation(ec[:, :], distt[:, 3 * DIST + CDIST:], ACT.Exp, scale=der("lg_b", h)).then_inc(r_e, 1)

            def att_out(t):
                act.wait_ge(a_pv, 8 * (t + 1))
                SC.activation(H[:, 0, t, :], PS[:, 4, :], ACT.Copy).then_inc(a_hi, 1)

            def ret_out(t):
                act.wait_ge(r_pv, 12 * (t + 1))
                SC.activation(QR[:, t, :], PS[:, 6, :], ACT.Copy).then_inc(r_o, 1)

            for s in range(STEPS):
                if s < 32:
                    act.wait_ge(a_mx, s + 1)
                    if s >= 2:
                        act.wait_ge(a_tr, s - 1)
                        act.wait_ge(a_p, s - 1)
                    SC.activation(Pb[:, s % 2, :], PS[:, 0:2, :].rearrange("p a b -> p (a b)")[:, 0:LA], ACT.Exp,
                                  bias=smx[:, s % 2:s % 2 + 1], scale=HD**-0.5,
                                  accum_out=rsum[:, s % 2:s % 2 + 1]).then_inc(a_exp, 1)
                if s >= LAG and (s - LAG) % 8 == 0 and s > LAG:
                    ret_out((s - LAG) // 8 - 1)
                if 0 < s <= 32:
                    act.wait_ge(a_tr, s)
                    if s >= 3:
                        act.wait_ge(a_pv, s - 2)
                    SC.activation(PT[:, (s - 1) % 2, :], PS[:, 2:4, :].rearrange("p a b -> p (a b)")[:, 0:LA],
                                  ACT.Copy).then_inc(a_pt, 1)
                if s == 0:
                    exp_strip(0)
                elif s % 4 == 0 and s // 4 < 8:
                    exp_strip(s // 4)
                if s and s % 8 == 0:
                    att_out(s // 8 - 1)
            ret_out(3)

            def gn_square(t):
                act.wait_ge(g_y, t + 1)
                if t >= 2:
                    act.wait_ge(g_var, t - 1)
                SC.activation(gsq[:, t % 2, :], cen[:, t % 2, :], ACT.Square).then_inc(g_sq, 1)
            gn_square(0)
            gn_square(1)
            act.wait_ge(mod_done, 2 * MODU)
            split_hi(act, "w_out", 0)
            split_hi(act, "w_out", 1)
            for t in range(4):
                act.wait_ge(g_var, t + 1)
                if t:
                    act.wait_ge(g_rs, t)
                SC.activation(rtmp[:, :], PS[:, t, :], ACT.Sqrt, bias=col("eps")).then_inc(g_rt, 1)
                act.wait_ge(g_val, t + 1)
                SC.activation(H[:, 0, 4 + t, :], gv[:, t % 2, :], ACT.Copy).then_inc(g_hi, 1)
                if t + 2 < 4:
                    gn_square(t + 2)

            for n in range(8):
                act.wait_ge(w_done, ORD["w_out"] + n + 1)
                if n + 2 < 8:
                    split_hi(act, "w_out", n + 2)
                if n == 0:
                    act.wait_ge(g_h, 4)
                square(2 * KT + n, PS[:, n % 2, :])
                SC.activation(Ym[:, n, :], PS[:, n % 2, :], ACT.Copy).then_inc(n_y, 1)
            root(2)
            for kt in range(KT):
                act.wait_ge(n_x, kt + 1)
                square(3 * KT + kt, X[:, kt, :])
            root(3)
            split_hi(act, "ffn_in", 0)
            split_hi(act, "ffn_in", 1)
            for kt in range(KT):
                high(3, kt, H[:, 0, kt, :], mod_col(3, kt))

            def ffn_four(i, first, last):
                for u in range(4):
                    act.wait_ge(w_done, i * 4 + (ORD["ffn_in"] + u + 1))
                    if not (last and u >= 2):
                        split_hi(act, "ffn_in", u + 2, i)
                    j = u // 2
                    if u % 2 == 0:
                        if not first or u == 2:
                            act.wait_ge(h_val, i * 2 + j)
                        SC.activation(sl[:, j, :], PS[:, u, :], ACT.Silu).then_inc(h_sl, 1)
                    else:
                        act.wait_ge(h_val, i * 2 + (j + 1))
                        SC.activation(hid[:, 0, i * 2 + j, :], hv[:, j, :], ACT.Copy).then_inc(h_hi, 1)
            ffn_four(0, True, False)
            with act.Fori(1, FT // 2 - 1) as i:
                ffn_four(i, False, False)
            ffn_four(FT // 2 - 1, False, True)

            split_hi(act, "ffn_out", 0)
            split_hi(act, "ffn_out", 1)

            def down_four(i, last):
                for u in range(4):
                    act.wait_ge(w_done, i * 4 + (ORD["ffn_out"] + u + 1))
                    if not (last and u >= 2):
                        split_hi(act, "ffn_out", u + 2, i)
                    j = u // 2
                    if u % 2:
                        act.wait_ge(n_acc, i * 2 + (4 * KT + j - 1))
                        SC.activation(sqb[:, j, :], PS[:, j, :], ACT.Square).then_inc(n_sq, 1)
                        SC.activation(Y[:, i * 2 + j, :], PS[:, j, :], ACT.Copy).then_inc(n_y, 1)
            act.wait_ge(h_lo, FT)
            with act.Fori(0, 3) as i:
                down_four(i, False)
            down_four(3, True)
            root(4)

            def squares(kts):
                for kt in kts:
                    act.wait_ge(n_x, KT + kt + 1)
                    square(5 * KT + kt, X[:, kt, :])

            def absolute(j):
                act.wait_ge(k_hp, j + 1)
                if j >= 2:
                    act.wait_ge(k_sum, j - 1)
                own(SC.activation(aab[:, j % 2, 0, :], fA[:, j % 2, :], ACT.Abs))
                SC.activation(aab[:, j % 2, 1, :], fB[:, j % 2, :], ACT.Abs).then_inc(k_abs, 1)

            squares(range(0, 2))
            absolute(0)
            squares(range(2, 5))
            absolute(1)
            squares(range(5, KT))
            root(5)
            absolute(2)
            absolute(3)
            split_hi(act, "hy_in", 0)
            split_hi(act, "hy_in", 1)
            for j in range(4, 8):
                absolute(j)
                for kt in (2 * j - 8, 2 * j - 7):
                    high(5, kt, H[:, 0, kt, :], mod2_col(0, kt))
            act.wait_ge(k_ab, 8)
            for k in range(4):
                act.wait_ge(k_f, k + 1)
                if k >= 2:
                    act.wait_ge(k_k, k - 1)
                own(SC.activation(kE[:, k % 2, 0, :], PS[:, 4 * (k % 2), :], ACT.Copy))
                SC.activation(kE[:, k % 2, 1, :], PS[:, 4 * (k % 2) + 1, :], ACT.Copy).then_inc(k_e, 1)

            act.wait_ge(y_c, 1)

            def hy_four(i, first, last):
                for u in range(4):
                    act.wait_ge(w_done, i * 4 + (ORD["hy_in"] + u + 1))
                    if not (last and u >= 2):
                        split_hi(act, "hy_in", u + 2, i)
                    if not first or u >= 2:
                        act.wait_ge(y_c, i * 4 + u)
                    SC.activation(cb_[:, u % 2, 1:L + 1], PS[:, u % 2, :], ACT.Identity,
                                  bias=colt[:, bass.ds(i * 4 + (COL["hy_b_in"] + u), 1)]).then_inc(y_b, 1)
            hy_four(0, True, False)
            with act.Fori(1, 5) as i:
                hy_four(i, False, False)
            hy_four(5, False, True)
            for g in range(8):
                par, mt, c = g // 4, g // 2 % 2, g % 2
                act.wait_ge(z_tr, g + 1)
                SC.activation(zN[:, par * 2 + mt, c * 512:(c + 1) * 512], PS[:, g % 4, :], ACT.Copy).then_inc(z_n, 1)
            act.wait_ge(y_c, 25)
            for k in range(4):
                act.wait_ge(z_f, k + 1)
                if k:
                    act.wait_ge(z_b, k)
                b = 4 * (k % 2)
                own(SC.activation(zE[:, 0, :], PS[:, b, :], ACT.Copy))
                SC.activation(zE[:, 1, :], PS[:, b + 1, :], ACT.Copy).then_inc(z_e, 1)

            def inv_high(j):
                act.wait_ge(i_val, j + 1)
                SC.activation(H[:, 0, j, :], yv[:, j % 2, :], ACT.Copy).then_inc(i_hi, 1)
            act.wait_ge(z_y, 4)
            for j in range(KT):
                act.wait_ge(i_mm, j + 1)
                if j >= 2:
                    act.wait_ge(i_val, j - 1)
                SC.activation(yt[:, j % 2, :].rearrange("p (m r) -> p r m", r=2),
                              PS[:, j % 4, :].rearrange("p (r m) -> p r m", r=2), ACT.Copy,
                              scale=der("inv_norm", j)).then_inc(i_ev, 1)
                if j:
                    inv_high(j - 1)
            inv_high(KT - 1)

            split_hi(act, "hy_out", 0)
            split_hi(act, "hy_out", 1)
            for n in range(8):
                act.wait_ge(w_done, ORD["hy_out"] + n + 1)
                if n + 2 < 8:
                    split_hi(act, "hy_out", n + 2)
                if n >= 2:
                    act.wait_ge(n_x, 2 * KT + n - 1)
                SC.activation(hyt[:, n % 2, :], PS[:, n % 2, :], ACT.Identity, bias=der("p_hy", n),
                              scale=dert[:, DER["mod2"] + 2 * KT + n:DER["mod2"] + 2 * KT + n + 1]).then_inc(o_ev, 1)
                if n:
                    act.wait_ge(n_x, 2 * KT + n)
                    square(6 * KT + n - 1, X[:, n - 1, :])
            act.wait_ge(n_x, 3 * KT)
            square(7 * KT - 1, X[:, KT - 1, :])
            root(6)
            split_hi(act, "up", 0)
            split_hi(act, "up", 1)
            for kt in range(KT):
                high(6, kt, H[:, 0, kt, :], mod2_col(3, kt))

            act.wait_ge(h_cv, 1)

            def up_high(i, j):
                act.wait_ge(h_val, i * 2 + (FT + j + 1))
                SC.activation(hid[:, 0, i * 2 + j, :], hv[:, j % 2, :], ACT.Copy).then_inc(h_hi, 1)

            def up_four(i, first, last):
                for u in range(4):
                    act.wait_ge(w_done, i * 4 + (ORD["up"] + u + 1))
                    if not (last and u >= 2):
                        split_hi(act, "up", u + 2, i)
                    j = u // 2
                    if u % 2 == 0:
                        if not (first and u == 0):
                            act.wait_ge(h_cv, i * 2 + j)
                        SC.activation(gb[:, j, 1:ROWS + 1, 1:GRID_W + 1],
                                      PS[:, u, :].rearrange("p (a b) -> p a b", b=GRID_W), ACT.Copy).then_inc(h_g, 1)
                        SC.activation(der("taps", 9 * j, 9), colt[:, bass.ds(i * 18 + (COL["conv_w"] + 9 * j), 9)],
                                      ACT.Copy).then_inc(h_tp, 1)
                        SC.activation(cva[:, j, :, :].rearrange("p a b -> p (a b)"), PS[:, u, :], ACT.Copy,
                                      scale=colt[:, bass.ds(i * 18 + (COL["conv_w"] + 9 * j + 4), 1)]).then_inc(h_ct, 1)
                        if not (first and u == 0):
                            up_high(i, j - 1)
                    else:
                        act.wait_ge(h_cv, i * 2 + (j + 2))
                        act.wait_ge(h_val, i * 2 + (FT + j - 1))
                        SC.activation(sl[:, j, :], cva[:, j, :, :].rearrange("p a b -> p (a b)"), ACT.Silu,
                                      bias=colt[:, bass.ds(i * 2 + (COL["conv_b"] + j), 1)]).then_inc(h_sl, 1)
            up_four(0, True, False)
            with act.Fori(1, FT // 2 - 1) as i:
                up_four(i, False, False)
            up_four(FT // 2 - 1, False, True)
            up_high(FT // 2 - 1, 1)

            split_hi(act, "down", 0)
            split_hi(act, "down", 1)
            act.wait_ge(h_lo, 2 * FT)

            def last_four(i, last):
                for u in range(4):
                    act.wait_ge(w_done, i * 4 + (ORD["down"] + u + 1))
                    if not (last and u >= 2):
                        split_hi(act, "down", u + 2, i)
                    j = u // 2
                    if u % 2:
                        act.wait_ge(n_x, i * 2 + (3 * KT + j + 1))
                        act.wait_ge(n_acc, i * 2 + (7 * KT + j - 1))
                        SC.activation(sqb[:, j, :], X[:, i * 2 + j, :], ACT.Square).then_inc(n_sq, 1)
            with act.Fori(0, 3) as i:
                last_four(i, False)
            last_four(3, True)
            root(7)

        @block.gpsimd
        def _(pool):
            own = Own(pool, s_pool)
            PL = nc.gpsimd

            def sums(k, n=L, kts=range(KT)):
                for kt in kts:
                    q = k * KT + kt
                    pool.wait_ge(n_sq, q + 1)
                    if kt == 0:
                        if k:
                            pool.wait_ge(n_ss, totals(k - 1))
                        PL.tensor_copy(acc[:, 0:n], sqb[:, q % 2, 0:n]).then_inc(n_acc, 1)
                    else:
                        pool.wait_ge(n_acc, q)
                        PL.tensor_tensor(acc[:, 0:n], acc[:, 0:n], sqb[:, q % 2, 0:n], ALU.add).then_inc(n_acc, 1)

            def scaled(k, src, gain, n=L, kts=range(KT)):
                pool.wait_ge(n_rs, k + 1)
                for kt in [kt for kt in kts if kt % 2]:
                    t = k * KT + kt
                    wait_buffer(pool, t)
                    own(PL.tensor_tensor(tb[:, t % 4, 0:n], src[:, kt, 0:n], rstd[:, 0:n], ALU.mult))
                    PL.tensor_scalar(tb[:, t % 4, 0:n], tb[:, t % 4, 0:n], der(gain, kt), None,
                                     ALU.mult).then_inc(n_t[1], 1)

            sums(0)
            sums(1, LC)
            pool.wait_ge(m_gain, 1)
            scaled(0, X, "a_mix")
            scaled(1, Xc, "a_ctx", LC)
            def abs_sum(j):
                c, t, ab = j // 4, j % 4, aab[:, j % 2, :, :]
                cs = slice(c * 512, (c + 1) * 512)
                pool.wait_ge(k_abs, j + 1)
                if t == 0:
                    PL.tensor_tensor(absum[:, cs], ab[:, 0, :], ab[:, 1, :], ALU.add).then_inc(k_sum, 1)
                else:
                    pool.wait_ge(k_sum, j)
                    own(PL.tensor_tensor(absum[:, cs], absum[:, cs], ab[:, 0, :], ALU.add))
                    PL.tensor_tensor(absum[:, cs], absum[:, cs], ab[:, 1, :], ALU.add).then_inc(k_sum, 1)

            def strip_sums(h):
                pool.wait_ge(r_e, h + 1)
                own(PL.tensor_tensor(strip[:, h % 2, 0:DIST], ea[:, :], distt[:, 2 * DIST:3 * DIST], ALU.add))
                PL.tensor_tensor(strip[:, h % 2, DIST:], strip[:, h % 2, DIST:], ec[:, :], ALU.add).then_inc(r_strip, 1)

            def mod_product(m):
                mod_multiply(pool, PL, m)
                pool.wait_ge(m_pr[1], (m - 17) // 2 + 1)
                pm = mprod[:, 1, :]
                own(PL.tensor_tensor(pm[:, 0:512], pm[:, 0:512], pm[:, 512:1024], ALU.add))
                own(PL.tensor_tensor(pm[:, 0:256], pm[:, 0:256], pm[:, 256:512], ALU.add))
                if m >= 24:
                    pool.wait_ge(mod_done, m - 7)
                PL.tensor_tensor(msum[:, m % 8, :], pm[:, 0:128], pm[:, 128:256], ALU.add).then_inc(m_sum[1], 1)
                pool.wait_ge(m_sum[1], (m - 17) // 2 + 1)

            pool.wait_ge(w_done, ORD["w_in"] + 22)
            for s in range(32):
                if s % 4 == 0:
                    strip_sums(s // 4)
                for m in mod_units(s)[1::2]:
                    mod_product(m)
            sums(2)
            pool.wait_ge(m_gain, 2)
            scaled(2, Ym, "p_mix")
            scaled(3, X, "a_ffn")
            sums(4)
            scaled(4, Y, "p_ffn")
            for j in range(4):
                abs_sum(j)
            scaled(5, X, "a_hy", L, range(0, 4))
            abs_sum(4)
            scaled(5, X, "a_hy", L, range(4, KT))
            for j in range(5, 8):
                abs_sum(j)
            for k in range(4):
                pool.wait_ge(z_b, k + 1)
                c, f, z0 = k // 2, k % 2, 4 * (k % 2)
                kk = KS[:, c, f, :, :]
                if k:
                    pool.wait_ge(z_w, k)
                for d in range(2):
                    zr, zi, kr, ki = zs[:, z0 + 2 * d, :], zs[:, z0 + 2 * d + 1, :], kk[:, 2 * d, :], kk[:, 2 * d + 1, :]
                    own(PL.tensor_tensor(zpP[:, d, :], zr, ki, ALU.mult))
                    own(PL.tensor_tensor(zpP[:, 2, :], zi, kr, ALU.mult))
                    last = PL.tensor_tensor(zpP[:, d, :], zpP[:, d, :], zpP[:, 2, :], ALU.add)
                    if d == 0:
                        own(last)
                last.then_inc(z_q, 1)
                pool.wait_ge(z_q, k + 1)
                pool.wait_ge(z_p, k + 1)
                own(PL.tensor_tensor(kk[:, 1, :], zpP[:, 0, :], zpP[:, 1, :], ALU.add))
                PL.tensor_tensor(kk[:, 3, :], zpP[:, 0, :], zpP[:, 1, :], ALU.subtract).then_inc(z_w, 1)
            sums(6)
            scaled(6, X, "a_ffn2")

            def up_two(i):
                for j in range(2):
                    pool.wait_ge(h_g, i * 2 + (j + 1))
                    pool.wait_ge(h_tp, i * 2 + (j + 1))
                    pool.wait_ge(h_cv, i * 2 + (j + 1))
                    for n, tap in enumerate(POOL_TAPS):
                        dy, dx = tap // 3, tap % 3
                        src = gb[:, j, dy:dy + ROWS, dx:dx + GRID_W]
                        wcol = der("taps", 9 * j + tap)
                        own(PL.tensor_tensor((cvt if n else cvb)[:, :, :], src,
                                             wcol.unsqueeze(2).to_broadcast([P, ROWS, GRID_W]), ALU.mult))
                        if n:
                            ins = PL.tensor_tensor(cvb[:, :, :], cvb[:, :, :], cvt[:, :, :], ALU.add)
                        if 0 < n < len(POOL_TAPS) - 1:
                            own(ins)
                    ins.then_inc(h_cp, 1)
            with pool.Fori(0, FT // 2) as i:
                own.enter(i, 4 * (len(POOL_TAPS) - 1))
                up_two(i)
            own.leave(FT // 2)
            sums(7)
            pool.wait_ge(n_rs, 8)
            for kt in (3, 7):
                own(PL.tensor_tensor(Y[:, kt, :], X[:, kt, :], rstd[:, :], ALU.mult))
                PL.tensor_scalar(Y[:, kt, :], Y[:, kt, :], col("g_final", kt), None, ALU.mult).then_inc(n_fin[1], 1)

        @block.vector
        def _(dve):
            own = Own(dve, s_dve)
            VE = nc.vector

            def stt(o, a, s, b, op0=ALU.mult, op1=ALU.add):
                return VE.scalar_tensor_tensor(out=o, in0=a, scalar=s, in1=b, op0=op0, op1=op1)

            def reciprocal_root(k):
                dve.wait_ge(n_rt, k + 1)
                n = LC if k == 1 else L
                VE.reciprocal(rstd[:, 0:n], rtmp[:, 0:n]).then_inc(n_rs, 1)

            def scaled(k, src, gain, kts, n=L):
                for kt in kts:
                    if kt == 0:
                        dve.wait_ge(n_rs, k + 1)
                    if kt < KT:
                        wait_buffer(dve, k * KT + kt)
                        stt(tb[:, kt % 4, 0:n], src[:, kt, 0:n], der(gain, kt), rstd[:, 0:n], ALU.mult,
                            ALU.mult).then_inc(n_t[0], 1)

            def low(k, c, kt, h, shift, n=L):
                dve.wait_ge(n_hi, c + 1)
                stt(h[:, 1, kt, :], tb[:, kt % 4, 0:n], shift, h[:, 0, kt, :].bitcast(F32), ALU.add,
                    ALU.subtract).then_inc(n_h, 1)

            def lows(k, c0, h, shift, src, gain, kts=range(KT), n=L):
                for kt in kts:
                    low(k, c0 + kt, kt, h, shift(kt), n)
                    if kt % 2:
                        scaled(k, src, gain, [kt + 3], n)

            def residuals(k, src, gain, kts=range(KT)):
                for kt in kts:
                    dve.wait_ge(n_t[kt % 2], (k * KT + kt) // 2 + 1)
                    VE.tensor_tensor(X[:, kt, :], X[:, kt, :], tb[:, kt % 4, :], ALU.add).then_inc(n_x, 1)
                    if kt % 2:
                        scaled(k, src, gain, [kt + 3])

            own(VE.memset(der("one"), 1.0))
            dve.wait_ge(s_small, 80)
            for l in range(3):
                dve.wait_ge(f_mm, l + 1)
                if l:
                    dve.wait_ge(f_sin, l)
                b = ("fb1", "fb2", "fb3")[l]
                own(VE.tensor_scalar(fa[:, :], PS[0:HYF, 6, :], colt[0:HYF, COL[b]:COL[b] + 1],
                                     colt[0:HYF, COL["freq"]:COL["freq"] + 1], ALU.add, ALU.mult))
                own(VE.tensor_scalar(fk[:, :], fa[:, :], float(1 / TWO_PI), MAGIC, ALU.mult, ALU.add))
                own(VE.tensor_scalar(fk[:, :], fk[:, :], MAGIC, None, ALU.subtract))
                for part in (PI_A, PI_B, PI_C):
                    own(stt(fa[:, :], fk[:, :], -part, fa[:, :]))
                VE.tensor_scalar(fa[:, :], fa[:, :], PI_SAFE, -PI_SAFE, ALU.min, ALU.max).then_inc(f_arg, 1)

            dve.wait_ge(m_lg, 2)
            for name in ("lg_f", "lg_b"):
                own(VE.tensor_scalar(der(name, 0, 8), der(name, 0, 8), -1.0, None, ALU.mult))

            def mod_pair(chunk, which):
                a = DER["mod"] + 2 * KT * chunk + which
                return dert[:, a:a + 2 * KT - 1:2]

            def mod_col(chunk, kt, which=0):
                a = DER["mod"] + 2 * (KT * chunk + kt) + which
                return dert[:, a:a + 1]

            def mod2_col(chunk, kt):
                return der("mod2", KT * chunk + kt)

            reciprocal_root(0)
            dve.wait_ge(mod_done, 16)
            VE.tensor_tensor(der("mod", 0, 32), PS[:, 7, 0:32], col("b_mod", 0, 32), ALU.add).then_inc(m_cols, 1)
            dve.wait_ge(m_cols, 1)
            own(stt(der("a_mix", 0, KT), mod_pair(1, 0), 1.0, col("g_pre_mix", 0, KT), ALU.add, ALU.mult))
            stt(der("a_ctx", 0, KT), mod_pair(1, 1), 1.0, col("g_pre_mix", 0, KT), ALU.add,
                ALU.mult).then_inc(m_gain, 1)
            dve.wait_ge(m_gain, 1)
            scaled(0, X, "a_mix", (0, 2))
            lows(0, 0, H, lambda kt: mod_col(0, kt), X, "a_mix")
            reciprocal_root(1)
            split_lo(dve, "w_in", 0)
            scaled(1, Xc, "a_ctx", (0, 2), LC)
            split_lo(dve, "w_in", 1)
            lows(1, KT, Hc, lambda kt: mod_col(0, kt, 1), Xc, "a_ctx", n=LC)

            dve.wait_ge(s_rope, 16)
            for n in range(22):
                if n + 2 < 22:
                    split_lo(dve, "w_in", n + 2)
                m = n - 1
                if 0 <= m < NV:
                    dve.wait_ge(v_tr, m + 1)
                    VE.tensor_copy(V[:, :, m * P:(m + 1) * P],
                                   PS[:, 6:8, :].rearrange("p a b -> p (a b)")[:, 0:LA].rearrange(
                                       "p (t d) -> p t d", d=P)).then_inc(v_ev, 1)
                elif NV <= m < NV + NROPE:
                    normed_q = m == NV or 10 <= m < 14
                    dst = (KA[:, 0:L] if m == NV else KR[:, m - 6, 0:L] if m < 10 else QA[:, m - 10, :] if m < 14
                           else QR[:, m - 14, :])
                    dve.wait_ge(q_sw, m - NV + 1)
                    if m > NV:
                        dve.wait_ge(q_done, m - NV)
                    own(VE.tensor_tensor(RM[:, :], RU[:, m % 2, 0:L], ropet[:, 0, :], ALU.mult))
                    own(VE.tensor_tensor(dst, PS[:, 4, :], ropet[:, 1, :], ALU.mult))
                    if not normed_q:
                        VE.tensor_tensor(dst, dst, RM[:, :], ALU.add).then_inc(q_done, 1)
                        continue
                    own(VE.tensor_tensor(dst, dst, RM[:, :], ALU.add))
                    dve.wait_ge(q_rt, 1 if m == NV else m - 8)
                    w_ = LA if m == NV else L
                    own(VE.reciprocal(RT[:, 0:w_], RT[:, 0:w_]))
                    if m == NV:
                        own(VE.tensor_tensor(KA[:, L:LA], RU[:, m % 2, L:LA], RT[:, L:LA], ALU.mult))
                    VE.tensor_tensor(dst, dst, RT[:, 0:L], ALU.mult).then_inc(q_done, 1)

            def decay_arg(h):
                if h:
                    dve.wait_ge(r_strip, h)
                own(VE.tensor_scalar(ea[:, :], distt[:, DIST:2 * DIST], der("lg_b", h), None, ALU.mult))
                stt(ea[:, :], distt[:, 0:DIST], der("lg_f", h), ea[:, :]).then_inc(r_u, 1)

            def ret_decay(r):
                h, kt = r // 6, r % 6
                a = L - P - P * kt if kt < 4 else DIST + P * (5 - kt)
                dve.wait_ge(r_s, r + 1)
                dve.wait_ge(r_strip, h + 1)
                if r >= 2:
                    dve.wait_ge(r_pv, r - 1)
                VE.tensor_tensor(pr[:, r % 2, :], PS[:, 5, :], strip[:, h % 2, a:a + L], ALU.mult).then_inc(r_p, 1)

            def mod_product(m):
                mod_multiply(dve, VE, m)

            def mod_sum(m):
                dve.wait_ge(m_pr[0], (m - 16) // 2 + 1)
                if m >= 24:
                    dve.wait_ge(mod_done, m - 7)
                VE.tensor_reduce(msum[:, m % 8, :], mprod[:, 0, :].rearrange("p (k n) -> p n k", n=P),
                                 mybir.AxisListType.X, ALU.add).then_inc(m_sum[0], 1)
                dve.wait_ge(m_sum[0], (m - 16) // 2 + 1)

            for s in range(STEPS):
                rs = ret_steps(s)
                ms = list(mod_units(s))[::2]
                if rs:
                    ret_decay(rs[0])
                if s < 32:
                    dve.wait_ge(a_s, s + 1)
                    own(VE.tensor_reduce(mxr[:, s % 2:s % 2 + 1],
                                         PS[:, 0:2, :].rearrange("p a b -> p (a b)")[:, 0:LA],
                                         mybir.AxisListType.X, ALU.max))
                    if s >= 2:
                        dve.wait_ge(a_exp, s - 1)
                    VE.tensor_scalar(smx[:, s % 2:s % 2 + 1], mxr[:, s % 2:s % 2 + 1], -HD**-0.5, None,
                                     ALU.mult).then_inc(a_mx, 1)
                if s == 0:
                    dve.wait_ge(s_dist, 16)
                    decay_arg(0)
                    dve.wait_ge(w_done, ORD["w_in"] + 22)
                if ms:
                    mod_product(ms[0])
                if len(rs) == 2:
                    ret_decay(rs[1])
                if s < 32:
                    dve.wait_ge(a_exp, s + 1)
                    own(VE.reciprocal(rinv[:, s % 2:s % 2 + 1], rsum[:, s % 2:s % 2 + 1]))
                    VE.tensor_scalar(Pb[:, s % 2, :], Pb[:, s % 2, :], rinv[:, s % 2:s % 2 + 1], None,
                                     ALU.mult).then_inc(a_p, 1)
                if ms:
                    mod_sum(ms[0])
                for m in ms[1:]:
                    mod_product(m)
                    mod_sum(m)
                if s % 4 == 2 and s // 4 < 7:
                    decay_arg(s // 4 + 1)
                if s and s % 8 == 0:
                    dve.wait_ge(a_hi, s // 8)
                    VE.tensor_tensor(H[:, 1, s // 8 - 1, :], PS[:, 4, :], H[:, 0, s // 8 - 1, :].bitcast(F32),
                                     ALU.subtract).then_inc(a_o, 1)

            def gn_centre(t):
                dve.wait_ge(g_c, t + 1)
                if t >= 2:
                    dve.wait_ge(g_h, t - 1)
                VE.tensor_tensor(cen[:, t % 2, :], QR[:, t, :], PS[:, t, :], ALU.subtract).then_inc(g_y, 1)
            gn_centre(0)
            gn_centre(1)
            dve.wait_ge(mod_done, 2 * MODU)
            own(VE.tensor_tensor(dert[:, DER["mod"] + 32:DER["mod"] + 95:2], PS[:, 7, 32:95:2],
                                 colt[:, COL["b_mod"] + 32:COL["b_mod"] + 95:2], ALU.add))
            own(VE.tensor_tensor(der("mod2", 0, MODU), PS[:, 7, 96:96 + MODU], col("b_mod2", 0, MODU), ALU.add))
            own(VE.tensor_tensor(der("p_mix", 0, KT), mod_pair(2, 0), col("g_post_mix", 0, KT), ALU.mult))
            own(stt(der("a_ffn", 0, KT), mod_pair(4, 0), 1.0, col("g_pre_ffn", 0, KT), ALU.add, ALU.mult))
            own(VE.tensor_tensor(der("p_ffn", 0, KT), mod_pair(5, 0), col("g_post_ffn", 0, KT), ALU.mult))
            own(stt(der("a_hy", 0, KT), der("mod2", KT, KT), 1.0, col("g_hy", 0, KT), ALU.add, ALU.mult))
            own(VE.tensor_tensor(der("p_hy", 0, KT), der("mod2", 2 * KT, KT), col("hy_b_out", 0, KT), ALU.mult))
            stt(der("a_ffn2", 0, KT), der("mod2", 4 * KT, KT), 1.0, col("g_ffn2", 0, KT), ALU.add,
                ALU.mult).then_inc(m_gain, 1)
            for t in range(4):
                dve.wait_ge(g_rt, t + 1)
                VE.reciprocal(grs[:, :], rtmp[:, :]).then_inc(g_rs, 1)
                own(VE.tensor_tensor(gv[:, t % 2, :], cen[:, t % 2, :], G[:, t, :], ALU.mult))
                dve.wait_ge(g_rs, t + 1)
                VE.tensor_tensor(gv[:, t % 2, :], gv[:, t % 2, :], grs[:, :], ALU.mult).then_inc(g_val, 1)
                dve.wait_ge(g_hi, t + 1)
                VE.tensor_tensor(H[:, 1, 4 + t, :], gv[:, t % 2, :], H[:, 0, 4 + t, :].bitcast(F32),
                                 ALU.subtract).then_inc(g_h, 1)
                if t == 0:
                    split_lo(dve, "w_out", 0)
                    split_lo(dve, "w_out", 1)
                if t + 2 < 4:
                    gn_centre(t + 2)

            for n in range(2, 8):
                split_lo(dve, "w_out", n)
            reciprocal_root(2)
            scaled(2, Ym, "p_mix", (0, 2))
            residuals(2, Ym, "p_mix")
            reciprocal_root(3)
            scaled(3, X, "a_ffn", (0, 2))
            split_lo(dve, "ffn_in", 0)
            lows(3, 2 * KT, H, lambda kt: mod_col(3, kt), X, "a_ffn", range(0, 4))
            split_lo(dve, "ffn_in", 1)
            lows(3, 2 * KT, H, lambda kt: mod_col(3, kt), X, "a_ffn", range(4, KT))

            def ffn_four(i, first, last):
                for u in range(4):
                    if not (last and u >= 2):
                        split_lo(dve, "ffn_in", u + 2, i)
                    j = u // 2
                    if u % 2:
                        dve.wait_ge(w_done, i * 4 + (ORD["ffn_in"] + u + 1))
                        dve.wait_ge(h_sl, i * 2 + (j + 1))
                        if not first or u == 3:
                            dve.wait_ge(h_lo, i * 2 + j)
                        VE.tensor_tensor(hv[:, j, :], PS[:, u, :], sl[:, j, :], ALU.mult).then_inc(h_val, 1)
                        dve.wait_ge(h_hi, i * 2 + (j + 1))
                        VE.tensor_tensor(hid[:, 1, i * 2 + j, :], hv[:, j, :], hid[:, 0, i * 2 + j, :].bitcast(F32),
                                         ALU.subtract).then_inc(h_lo, 1)
            ffn_four(0, True, False)
            with dve.Fori(1, FT // 2 - 1) as i:
                ffn_four(i, False, False)
            ffn_four(FT // 2 - 1, False, True)
            for n in range(2):
                split_lo(dve, "ffn_out", n)
            with dve.Fori(0, 3) as i:
                for u in range(4):
                    split_lo(dve, "ffn_out", u + 2, i)
            for n in range(14, 16):
                split_lo(dve, "ffn_out", n)

            def filters(j):
                c, t = j // 4, j % 4
                cs = slice(c * 512, (c + 1) * 512)
                dve.wait_ge(s_dec[t], 16 * (c + 1))
                dve.wait_ge(k_h, j + 1)
                if j >= 2:
                    dve.wait_ge(k_hp, j - 1)
                    dve.wait_ge(k_abs, j - 1)
                own(VE.tensor_tensor(fA[:, j % 2, :], PS[:, 4, :], dect[:, t, :], ALU.mult))
                VE.tensor_tensor(fB[:, j % 2, :], PS[:, 5, :], dect[:, t, :], ALU.mult).then_inc(k_ab, 1)
                dve.wait_ge(k_ab, j + 1)
                if t == 0:
                    own(VE.memset(fB[0:1, j % 2, :], 0.0))
                own(VE.tensor_tensor(HP[:, t, cs], fA[:, j % 2, :], fB[:, j % 2, :], ALU.add))
                VE.tensor_tensor(HM[:, t, cs], fA[:, j % 2, :], fB[:, j % 2, :], ALU.subtract).then_inc(k_hp, 1)

            def lows_5(kts):
                lows(5, 3 * KT, H, lambda kt: mod2_col(0, kt), X, "a_hy", kts)

            filters(0)
            reciprocal_root(4)
            scaled(4, Y, "p_ffn", (0, 2))
            for j, kts in ((1, range(0, 2)), (2, range(2, 5)), (3, range(5, KT))):
                residuals(4, Y, "p_ffn", kts)
                filters(j)
            filters(4)
            reciprocal_root(5)
            split_lo(dve, "hy_in", 0)
            split_lo(dve, "hy_in", 1)
            scaled(5, X, "a_hy", (0, 2))
            filters(5)
            lows_5(range(0, 2))
            filters(6)
            lows_5(range(2, 4))
            filters(7)
            lows_5(range(4, KT))
            for k in range(4):
                c, f, b = k // 2, k % 2, 4 * (k % 2) + 2
                dve.wait_ge(k_e, k + 1)
                if k == 2:
                    dve.wait_ge(k_sum, 8)
                ke = kE[:, k % 2, :, :]
                for part in range(2):
                    own(VE.tensor_tensor(KS[:, c, f, part, :], ke[:, part, :], PS[:, b + part, :], ALU.add))
                own(VE.tensor_tensor(KS[:, c, f, 2, :], ke[:, 0, :], PS[:, b, :], ALU.subtract))
                VE.tensor_tensor(KS[:, c, f, 3, :], ke[:, 1, :], PS[:, b + 1, :], ALU.subtract).then_inc(k_k, 1)
            dve.wait_ge(k_col, 1)
            VE.reciprocal(der("inv_norm", 0, KT), PS[:, 0, 0:KT]).then_inc(k_inv, 1)

            dve.wait_ge(n_h, 4 * KT)
            VE.memset(cb_[:, :, 0:L + 2:L + 1], 0.0).then_inc(y_c, 1)

            def hy_four(i, gated, last):
                for u in range(4):
                    if not (last and u >= 2):
                        split_lo(dve, "hy_in", u + 2, i)
                    dve.wait_ge(y_b, i * 4 + (u + 1))
                    j = u // 2

                    def hcol(name, per, tap):
                        return colt[:, bass.ds(i * (4 * per) + (COL[name] + per * u + tap), 1)]
                    if gated:
                        dst = x1c[:, :] if u % 2 == 0 else ca[:, 1, :]
                    else:
                        dst = X0[:, i * 4 + (u - 16), :]
                    own(VE.tensor_scalar(ca[:, 0, :], cb_[:, u % 2, 1:L + 1], hcol("hy_sc_w", 3, 1),
                                         hcol("hy_sc_b", 1, 0), ALU.mult, ALU.add))
                    own(stt(ca[:, 0, :], cb_[:, u % 2, 0:L], hcol("hy_sc_w", 3, 0), ca[:, 0, :]))
                    stt(dst, cb_[:, u % 2, 2:L + 2], hcol("hy_sc_w", 3, 2), ca[:, 0, :]).then_inc(y_c, 1)
                    dve.wait_ge(y_c, i * 4 + (u + 2))
                    if gated and u % 2:
                        VE.tensor_tensor(Z[:, i * 2 + j, :], x1c[:, :], ca[:, 1, :], ALU.mult).then_inc(y_z, 1)
                        dve.wait_ge(y_z, i * 2 + (j + 1))
            with dve.Fori(0, 4) as i:
                own.enter(i, 8)
                hy_four(i, True, False)
            own.leave(4)
            hy_four(4, False, False)
            hy_four(5, False, True)

            for k in range(4):
                c, f, z0, b = k // 2, k % 2, 4 * (k % 2), 4 * (k % 2)
                kk = KS[:, c, f, :, :]
                dve.wait_ge(z_e, k + 1)
                if k >= 2:
                    dve.wait_ge(z_q, k - 1)
                for part in range(2):
                    own(VE.tensor_tensor(zs[:, z0 + part, :], zE[:, part, :], PS[:, b + 2 + part, :], ALU.add))
                own(VE.tensor_tensor(zs[:, z0 + 2, :], zE[:, 0, :], PS[:, b + 2, :], ALU.subtract))
                VE.tensor_tensor(zs[:, z0 + 3, :], zE[:, 1, :], PS[:, b + 3, :], ALU.subtract).then_inc(z_b, 1)
                dve.wait_ge(z_b, k + 1)
                for d in range(2):
                    zr, zi, kr, ki = zs[:, z0 + 2 * d, :], zs[:, z0 + 2 * d + 1, :], kk[:, 2 * d, :], kk[:, 2 * d + 1, :]
                    own(VE.tensor_tensor(zpD[:, d, :], zr, kr, ALU.mult))
                    own(stt(zpD[:, 2, :], zi, 1.0 if f else col("not_first"), ki, ALU.mult, ALU.mult))
                    last = VE.tensor_tensor(zpD[:, d, :], zpD[:, d, :], zpD[:, 2, :], ALU.subtract)
                    if d == 0 or f == 0:
                        own(last)
                if f == 0:
                    S, W, S_, W_ = zs[0:1, z0 + 1, :], zs[0:1, z0 + 3, :], kk[0:1, 1, :], kk[0:1, 3, :]
                    own(VE.tensor_tensor(row[:, 0, :], S, W_, ALU.mult))
                    own(VE.tensor_tensor(row[:, 1, :], W, S_, ALU.mult))
                    own(VE.tensor_tensor(row[:, 0, :], row[:, 0, :], row[:, 1, :], ALU.add))
                    own(VE.tensor_tensor(row[:, 1, :], S, S_, ALU.mult))
                    own(VE.tensor_tensor(zpD[0:1, 2, :], W, W_, ALU.mult))
                    last = VE.tensor_tensor(row[:, 1, :], row[:, 1, :], zpD[0:1, 2, :], ALU.subtract)
                last.then_inc(z_p, 1)
                dve.wait_ge(z_p, k + 1)
                dve.wait_ge(z_q, k + 1)
                own(VE.tensor_tensor(kk[:, 0, :], zpD[:, 0, :], zpD[:, 1, :], ALU.add))
                last = VE.tensor_tensor(kk[:, 2, :], zpD[:, 0, :], zpD[:, 1, :], ALU.subtract)
                if f == 0:
                    own(last)
                    dve.wait_ge(z_w, k + 1)
                    own(VE.tensor_copy(kk[0:1, 1, :], row[:, 0, :]))
                    last = VE.tensor_copy(kk[0:1, 3, :], row[:, 1, :])
                else:
                    own(last)
                    dve.wait_ge(z_w, k + 1)
                    last = VE.tensor_copy(row[:, 0, 0:1], row[:, 1, 0:1])
                last.then_inc(z_y, 1)
                dve.wait_ge(z_y, k + 1)

            def inv_low(j):
                dve.wait_ge(i_hi, j + 1)
                VE.tensor_tensor(H[:, 1, j, :], yv[:, j % 2, :], H[:, 0, j, :].bitcast(F32),
                                 ALU.subtract).then_inc(i_h, 1)
            for j in range(KT):
                dve.wait_ge(i_ev, j + 1)
                own(stt(yt[:, j % 2, :], Z[:, j, :], col("hy_bias", j), yt[:, j % 2, :]))
                if j >= 2:
                    dve.wait_ge(i_h, j - 1)
                VE.tensor_tensor(yv[:, j % 2, :], yt[:, j % 2, :], X0[:, j, :], ALU.mult).then_inc(i_val, 1)
                if j:
                    inv_low(j - 1)
            inv_low(KT - 1)

            split_lo(dve, "hy_out", 0)
            split_lo(dve, "hy_out", 1)
            for n in range(8):
                if n + 2 < 8:
                    split_lo(dve, "hy_out", n + 2)
                dve.wait_ge(o_ev, n + 1)
                VE.tensor_tensor(X[:, n, :], X[:, n, :], hyt[:, n % 2, :], ALU.add).then_inc(n_x, 1)
            reciprocal_root(6)
            scaled(6, X, "a_ffn2", (0, 2))
            split_lo(dve, "up", 0)
            split_lo(dve, "up", 1)
            lows(6, 4 * KT, H, lambda kt: mod2_col(3, kt), X, "a_ffn2")

            dve.wait_ge(n_h, 5 * KT)
            VE.memset(gb[:, :, :, :], 0.0).then_inc(h_cv, 1)

            def up_low(i, j):
                dve.wait_ge(h_hi, i * 2 + (FT + j + 1))
                VE.tensor_tensor(hid[:, 1, i * 2 + j, :], hv[:, j % 2, :], hid[:, 0, i * 2 + j, :].bitcast(F32),
                                 ALU.subtract).then_inc(h_lo, 1)

            def up_four(i, first, last):
                for u in range(4):
                    if not (last and u >= 2):
                        split_lo(dve, "up", u + 2, i)
                    j = u // 2
                    if u % 2 == 0:
                        dve.wait_ge(h_g, i * 2 + (j + 1))
                        dve.wait_ge(h_tp, i * 2 + (j + 1))
                        dve.wait_ge(h_ct, i * 2 + (j + 1))
                        for tap in DVE_TAPS:
                            dy, dx = tap // 3, tap % 3
                            own(stt(cva[:, j, :, :], gb[:, j, dy:dy + ROWS, dx:dx + GRID_W],
                                    der("taps", 9 * j + tap), cva[:, j, :, :]))
                        if not (first and u == 0):
                            up_low(i, j - 1)
                    else:
                        dve.wait_ge(h_cp, i * 2 + (j + 1))
                        VE.tensor_tensor(cva[:, j, :, :], cva[:, j, :, :], cvb[:, :, :], ALU.add).then_inc(h_cv, 1)
                        dve.wait_ge(w_done, i * 4 + (ORD["up"] + u + 1))
                        dve.wait_ge(h_sl, i * 2 + (FT + j + 1))
                        dve.wait_ge(h_lo, i * 2 + (FT + j - 1))
                        VE.tensor_tensor(hv[:, j, :], PS[:, u, :], sl[:, j, :], ALU.mult).then_inc(h_val, 1)
            own.enter(0, 2 * len(DVE_TAPS))
            up_four(0, True, False)
            with dve.Fori(1, FT // 2 - 1) as i:
                own.repeat(i)
                up_four(i, False, False)
            own.leave(FT // 2 - 1)
            up_four(FT // 2 - 1, False, True)
            up_low(FT // 2 - 1, 1)

            split_lo(dve, "down", 0)
            split_lo(dve, "down", 1)

            def last_four(i, last):
                for u in range(4):
                    if not (last and u >= 2):
                        split_lo(dve, "down", u + 2, i)
                    j = u // 2
                    if u % 2:
                        dve.wait_ge(w_done, i * 4 + (ORD["down"] + u + 1))
                        stt(X[:, i * 2 + j, :], PS[:, j, :],
                            dert[:, bass.ds(i * 2 + (DER["mod2"] + 5 * KT + j), 1)],
                            X[:, i * 2 + j, :]).then_inc(n_x, 1)
            with dve.Fori(0, 3) as i:
                last_four(i, False)
            last_four(3, True)
            reciprocal_root(7)
            dve.wait_ge(n_rs, 8)
            for kt in (0, 1, 2, 4, 5, 6):
                stt(Y[:, kt, :], X[:, kt, :], col("g_final", kt), rstd[:, :], ALU.mult, ALU.mult).then_inc(n_fin[0], 1)
def tables():
    f32 = np.float32
    m = np.zeros((4, P, P), f32)
    m[0] = 1.0 / D
    i = np.arange(P)
    m[1] = (i[:, None] // HD == i[None, :] // HD) / f32(HD)
    m[2] = i[:, None] == (i[None, :] // HD) * HD + (i[None, :] + HALF) % HD
    m[3] = np.eye(P)
    n_freq = HD // 4
    inv_freq = (f32(10000.0) ** (-np.arange(n_freq, dtype=f32) / f32(n_freq))).astype(f32)
    tok = np.arange(L)
    ang = np.concatenate([(tok // GRID_W).astype(f32)[:, None] * inv_freq, (tok % GRID_W).astype(f32)[:, None] * inv_freq],
                         axis=1).T
    ang = np.tile(ang, (4, 1))
    sign = np.where(i % HD < HALF, -1.0, 1.0).astype(f32)[:, None]
    rope = np.stack([np.cos(ang), np.sin(ang) * sign], 1).astype(f32)
    f, p = np.arange(DIST)[None, :], i[:, None]
    d = f - (L - P) - p
    fc = np.arange(CDIST)[None, :]
    dist = np.concatenate([np.maximum(d, 0), np.maximum(-d, 0), d == 0, fc + P - p, L + P - fc + p], 1).astype(f32)
    t = np.linspace(0.0, 1.0, L, dtype=f32)[:, None]
    w = (f32(TWO_PI) * np.arange(L, dtype=f32)[:, None] / f32(L)).astype(f32)
    bands = np.linspace(1e-4, BANDS - 1, BANDS, dtype=f32)[None, :]
    pos = np.ascontiguousarray(np.concatenate([t, np.cos(bands * w), -np.sin(bands * w)], 1).T.astype(f32))
    deltas = np.linspace(np.log(1e-2) / 1.5, np.log(1e-2) / 0.3, D, dtype=f32)
    dec = np.exp(-t * np.abs(deltas)).astype(f32)
    tokens = [np.arange(256 * mt, 256 * mt + 256)[par::2] for par in range(2) for mt in range(2)]
    decay = np.stack([dec[x] for x in tokens]).reshape(4, P, 2, D // 2).transpose(2, 0, 1, 3)
    decay = np.ascontiguousarray(decay)
    freq, mm = np.arange(256), np.arange(256)
    fwd, inv = np.zeros((P, 4, 2, 256)), np.zeros((P, 4, 2, 256))
    for a in range(4):
        th = TWO_PI * np.outer(2 * mm + a // 2, freq) / (2 * L)
        fm = np.cos(th) if a % 2 == 0 else np.sin(th)
        im = 2.0 * fm
        if a % 2 == 0:
            im[:, 0] = 1.0
        else:
            fm[:, 0] = im[:, 0] = (-1.0) ** mm
        fwd[:, a] = fm.reshape(2, P, 256).transpose(1, 0, 2)
        inv[:, a] = im.T.reshape(2, P, 256).transpose(1, 0, 2) / (2 * L) / D
    return dict(mats=m, rope=rope, dist=dist, posT=pos, decay=decay, fwd=fwd.astype(f32), inv=inv.astype(f32))


def columns(v):
    return v.reshape(-1, P).T


def units(w_, order=None):
    k, n = w_.shape
    u = w_.reshape(k // P, P, n // P, P).transpose(2, 1, 0, 3)
    if order is not None:
        u = u[order]
    return np.ascontiguousarray(u.reshape(len(u), P, k))


def half_units(w_):
    u = units(w_)
    return np.ascontiguousarray(u.reshape(-1, P, 2, U2).transpose(0, 2, 1, 3).reshape(-1, P, U2))


def kernel(**a):
    import concourse.bacc as bacc
    from concourse.bass_utils import run_bass_kernel_spmd

    a = {k: np.asarray(v) for k, v in a.items()}
    heads = np.concatenate([np.arange(HD) + HD * h for t in range(4) for h in (t, 4 + t)])
    w_in = a["w_in"][0]
    w_in = np.concatenate([w_in[:, heads], w_in[:, 512:]], 1)
    w_out = a["w_out"][0]
    w_out = np.concatenate([w_out[heads], w_out[512:]], 0)
    qa, ka, va, qr, kr, vr, gr = 0, 4, 5, 6, 10, 14, 18
    order = [va] + [vr + i for i in range(4)] + [ka] + [kr + i for i in range(4)] + [qa + i for i in range(4)] + \
            [qr + i for i in range(4)] + [gr + i for i in range(4)]
    pair_order = [x for j in range(FT) for x in (j, FT + j)]
    gate_first = [x for j in range(FT) for x in (FT + j, j)]
    hy_order = [x for j in range(KT) for x in (KT + j, 2 * KT + j)] + list(range(KT))
    mod1 = units(a["w_mod"][0])
    weights = dict(
        mod_a=mod1[:16], mod_b=np.concatenate([mod1[16:], units(a["mod_w_2"][0])]), w_in=units(w_in, order),
        w_out=units(w_out), ffn_in=units(a["w_ffn_in"][0], pair_order), ffn_out=half_units(a["w_ffn_out"][0]),
        hy_in=units(a["hy_w_in_2"][0], hy_order), hy_out=units(a["hy_w_out_2"][0]),
        up=units(a["ffn_w_up_2"][0], gate_first), down=half_units(a["ffn_w_down_2"][0]))

    def rep(v):
        return np.broadcast_to(v.reshape(1, -1), (P, v.size))

    def two(v):
        return np.concatenate([v, v]).reshape(P, 1)
    sc_w = a["hy_sc_w_2"][0].reshape(3, 3 * KT, P)[:, hy_order]
    parts = dict(
        g_pre_mix=columns(a["g_pre_mix"][0]), g_post_mix=columns(a["g_post_mix"][0]),
        g_pre_ffn=columns(a["g_pre_ffn"][0]), g_post_ffn=columns(a["g_post_ffn"][0]),
        b_mod=np.repeat(columns(a["b_mod"][0]), 2, 1), b_mod2=columns(a["mod_b_2"][0]),
        g_hy=columns(a["norm_g_2"][0, 0]), g_ffn2=columns(a["norm_g_2"][0, 1]), g_final=columns(a["final_g_2"]),
        hy_b_in=columns(a["hy_b_in_2"][0])[:, hy_order], hy_sc_w=sc_w.transpose(2, 1, 0).reshape(P, -1),
        hy_sc_b=columns(a["hy_sc_b_2"][0])[:, hy_order], hy_bias=columns(a["hy_bias_2"][0]),
        hy_b_out=columns(a["hy_b_out_2"][0]),
        conv_w=a["ffn_conv_w_2"][0].reshape(9, FT, P).transpose(2, 1, 0).reshape(P, -1),
        conv_b=columns(a["ffn_conv_b_2"][0]), q_g=two(a["q_norm_g"][0]), k_g=two(a["k_norm_g"][0]),
        dec_f=rep(a["ret_decay_fwd"][0]), dec_b=rep(a["ret_decay_bwd"][0]), freq=two(a["hy_freq_2"][0]),
        fb1=two(a["hy_f_b1_2"][0]), fb2=two(a["hy_f_b2_2"][0]), fb3=two(a["hy_f_b3_2"][0]),
        eps=np.full((P, 1), EPS, np.float32), not_first=(np.arange(P) > 0).astype(np.float32).reshape(P, 1),
        c=np.stack([columns(a["c"][0]), columns(a["c_ctx"]), columns(a["c_2"][0])], 2).reshape(P, -1))
    cols = np.concatenate([parts[name] for name, _ in COLS], 1).astype(np.float32)
    fw = np.zeros((HYF, 3, HYF), np.float32)
    fw[0:2 * BANDS + 1, 0] = a["hy_f_w1_2"][0]
    fw[:, 1] = a["hy_f_w2_2"][0]
    fw[:, 2] = a["hy_f_w3_2"][0]

    def tiles(x):
        return np.ascontiguousarray(x[0].T.reshape(KT, P, -1).transpose(1, 0, 2))
    arrays = dict(xT=tiles(a["x"]), ctxT=tiles(a["ctx"]), cols=cols, fw=fw, fwout=a["hy_f_wout_2"][0], **tables())
    arrays = {k: np.ascontiguousarray(v) for k, v in arrays.items()}
    nc = bacc.Bacc("TRN2", target_bir_lowering=False, num_devices=1)
    aps = {k: nc.dram_tensor(k, v.shape, F32, kind="ExternalInput").ap() for k, v in arrays.items()}
    waps = {}
    for name, v in weights.items():
        arrays["w_" + name] = np.ascontiguousarray(v)
        waps[name] = nc.dram_tensor("w_" + name, v.shape, F32, kind="ExternalInput").ap()
    out = nc.dram_tensor("out", (P, KT, L), F32, kind="ExternalOutput").ap()
    build(nc, w=waps, out=out, **aps)
    r = run_bass_kernel_spmd(nc, [arrays], core_ids=[0])
    y = np.asarray(r.results[0]["out"])
    return np.ascontiguousarray(y.transpose(1, 0, 2).reshape(D, L).T)[None]
```

```python
from contextlib import ExitStack

import numpy as np

import concourse.bass as bass
from concourse import mybir

F32 = mybir.dt.float32
F32R = mybir.dt.float32r
ALU = mybir.AluOpType
ACT = mybir.ActivationFunctionType

P = 128
D = 1024
KT = D // P
L = 512
LC = 256
LA = L + LC
HD = 64
HALF = HD // 2
NPAIR = 4
FFN = 2816
FT = FFN // P
NCHUNK = 6
MODU = NCHUNK * KT
GRID_W = 64
ROWS = L // GRID_W
HYF = 64
BANDS = 16
EPS = 1e-6
TWO_PI = 2.0 * np.pi
PI_A = 6.28125
PI_B = float(np.float32(np.round((TWO_PI - PI_A) * 2**21) / 2**21))
PI_C = float(np.float32(TWO_PI - PI_A - PI_B))
PI_SAFE = float(np.nextafter(np.float32(np.pi), np.float32(0)))
MAGIC = 1.5 * 2.0**23
DIST = L + 3 * P
CDIST = L + P

COLS = [("g_pre_mix", KT), ("g_post_mix", KT), ("g_pre_ffn", KT), ("g_post_ffn", KT),
        ("b_mod", 2 * MODU), ("b_mod2", MODU), ("g_hy", KT), ("g_ffn2", KT), ("g_final", KT),
        ("hy_b_in", 3 * KT), ("hy_sc_w", 9 * KT), ("hy_sc_b", 3 * KT), ("hy_bias", KT), ("hy_b_out", KT),
        ("conv_w", 9 * FT), ("conv_b", FT), ("q_g", 1), ("k_g", 1), ("dec_f", 8), ("dec_b", 8),
        ("freq", 1), ("fb1", 1), ("fb2", 1), ("fb3", 1), ("eps", 1), ("not_first", 1), ("c", 3 * KT)]
COL = {}
NCOL = 0
for _name, _w in COLS:
    COL[_name] = NCOL
    NCOL += _w
DERS = [("mod", 2 * MODU), ("mod2", MODU), ("a_mix", KT), ("a_ctx", KT), ("p_mix", KT), ("a_ffn", KT),
        ("p_ffn", KT), ("a_hy", KT), ("p_hy", KT), ("a_ffn2", KT), ("silu_c", 3 * KT), ("lg_f", 8), ("lg_b", 8),
        ("fb", 3), ("inv_norm", KT), ("one", 1), ("taps", 18)]
DER = {}
NDER = 0
for _name, _w in DERS:
    DER[_name] = NDER
    NDER += _w

U1 = KT * P
U2 = FFN // 2
FH = FT // 2
PHASES = [("mod_a", 16, U1, False), ("w_in", 22, U1, True), ("mod_b", 2 * MODU - 16, U1, False),
          ("w_out", 8, U1, True), ("ffn_in", 2 * FT, U1, True), ("ffn_out", 16, U2, True),
          ("hy_in", 24, U1, True), ("hy_out", 8, U1, True), ("up", 2 * FT, U1, True), ("down", 16, U2, True)]
RAW = 4
START, ORD, NUNIT, WIDTH = {}, {}, {}, {}
_g, _o = 0, {True: 0, False: 0}
for _name, _n, _w, _s in PHASES:
    START[_name], ORD[_name], NUNIT[_name], WIDTH[_name] = _g, _o[_s], _n, _w
    _g += _n
    _o[_s] += _n
    assert _name == "mod_a" or _s is False or START[_name] % RAW == ORD[_name] % RAW
KIND = [(s, ORD[name] + i) for name, n, w, s in PHASES for i in range(n)]


class Own:

    def __init__(self, eng, sem):
        self.eng, self.sem, self.n, self.i, self.per = eng, sem, 0, None, 0

    def __call__(self, ins):
        ins.then_inc(self.sem, 1)
        self.n += 1
        self.eng.wait_ge(self.sem, self.n if self.i is None else self.base + self.i * self.per + (self.n - self.base))

    def enter(self, i, per):
        self.base, self.i, self.per = self.n, i, per

    def repeat(self, i):
        self.n, self.i = self.base, i

    def leave(self, times):
        assert self.n - self.base == self.per, (self.n - self.base, self.per)
        self.n = self.base + times * self.per
        self.i = None


def build(nc, xT, ctxT, cols, mats, w, rope, dist, posT, fw, fwout, decay, fwd, inv, out):
    def sb(name, at, shape, dt=F32):
        return nc.alloc_sbuf_tensor_at(name, shape, dt, offset=BASE + at)

    with ExitStack() as stack:
        BASE = (nc.sbuf_base + 63) // 64 * 64
        K = 1024
        COLB = 3712
        colt = sb("colt", 0, [P, NCOL])
        o_der = (NCOL * 4 + 63) // 64 * 64
        dert = sb("dert", o_der, [P, NDER])
        assert o_der + NDER * 4 <= COLB
        feat = sb("feat", COLB, [HYF, L])
        o_mat = COLB + 2 * K
        ones = sb("ones", o_mat, [P, P])
        bones = sb("bones", o_mat + 512, [P, P])
        swap = sb("swap", o_mat + 1024, [P, P])
        ident = sb("ident", o_mat + 1536, [P, P])
        o_x = o_mat + 2 * K
        X = sb("X", o_x, [P, KT, L])
        o_raw = o_x + 16 * K
        wraw = sb("wraw", o_raw, [P, RAW, U2])
        o_ws = o_raw + RAW * U2 * 4
        wsp = sb("wsp", o_ws, [P, 2, 2, U2], F32R)
        o_t = o_ws + 4 * U2 * 4
        o_h = o_t + 20 * K
        H = sb("H", o_h, [P, 2, KT, L], F32R)
        Y = sb("Y", o_h, [P, KT, L])
        o_r = o_h + 32 * K
        assert BASE + o_r + 88 * K <= nc.sbuf_usable_end, (BASE + o_r + 88 * K, nc.sbuf_usable_end)
        sqb = sb("sqb", o_t, [P, 2, L])
        rstd = sb("rstd", o_t + 4 * K, [P, L])
        rstdc = sb("rstdc", o_t + 16 * K, [P, LC])
        accc = sb("accc", o_t + 17 * K, [P, LC])
        tb = sb("tb", o_t + 6 * K, [P, 4, L])
        acc = sb("acc", o_t + 14 * K, [P, L])
        rtmp = sb("rtmp", o_t + 18 * K, [P, L])
        posb = sb("posb", o_r + 40 * K, [2 * BANDS + 1, L])
        fwb = sb("fwb", o_r + 42 * K, [HYF, 3, HYF])
        fa = sb("fa", o_r + 44 * K, [HYF, L])
        fk = sb("fk", o_r + 46 * K, [HYF, L])
        fh = sb("fh", o_r + 48 * K, [HYF, L])
        Hc = sb("Hc", o_r, [P, 2, KT, LC], F32R)
        Xc = sb("Xc", o_r + 16 * K, [P, KT, LC])
        V = sb("V", o_r + 16 * K, [P, LA // P, 5 * P])
        ropet = sb("ropet", o_r + 31 * K, [P, 2, L])
        KA = sb("KA", o_r + 35 * K, [P, LA])
        KR = sb("KR", o_r + 38 * K, [P, NPAIR, LA])
        QA = sb("QA", o_r + 50 * K, [P, NPAIR, L])
        QR = sb("QR", o_r + 58 * K, [P, NPAIR, L])
        G = sb("G", o_r + 66 * K, [P, NPAIR, L])
        VT = sb("VT", o_t, [P, 2, LA])
        RU = sb("RU", o_t + 6 * K, [P, 2, LA])
        SQ = sb("SQ", o_t + 12 * K, [P, LA])
        RT = sb("RT", o_t + 15 * K, [P, LA])
        RM = sb("RM", o_t + 18 * K, [P, L])
        Pb = sb("Pb", o_r + 74 * K, [P, 2, LA])
        PT = sb("PT", o_r + 80 * K, [P, 2, LA])
        strip = sb("strip", o_r, [P, 2, DIST + CDIST])
        ea = sb("ea", o_r + 12 * K, [P, DIST])
        ec = sb("ec", o_r + 31 * K, [P, CDIST])
        smx = sb("smx", o_r + 86 * K, [P, 2])
        mxr = sb("mxr", o_r + 86 * K + 128, [P, 2])
        rinv = sb("rinv", o_r + 86 * K + 192, [P, 2])
        rsum = sb("rsum", o_r + 86 * K + 64, [P, 2])
        mprod = sb("mprod", o_ws, [P, 2, U1])
        msum = sb("msum", o_ws + 8 * K, [P, 8, P])
        aprod = sb("aprod", o_r + 50 * K, [P, 2, U1])
        asum = sb("asum", o_r + 58 * K, [P, 12, P])
        distt = sb("distt", o_t, [P, 3 * DIST + 2 * CDIST])
        pr = sb("pr", o_t + (3 * DIST + 2 * CDIST) * 4, [P, 2, L])
        assert (3 * DIST + 2 * CDIST) * 4 + 4 * K <= 20 * K
        Ym = sb("Ym", o_r, [P, KT, L])
        hid = sb("hid", o_r, [P, 2, FT, L], F32R)
        sl = sb("sl", o_t, [P, 2, L])
        hv = sb("hv", o_t + 4 * K, [P, 2, L])
        PW = GRID_W + 2
        gb = sb("gb", o_t + 8 * K, [P, 2, ROWS + 2, PW])
        cva = sb("cva", o_t + 14 * K, [P, 2, ROWS, GRID_W])
        cvb = sb("cvb", o_t + 18 * K, [P, ROWS, GRID_W])
        cvt = sb("cvt", COLB, [P, ROWS, GRID_W])
        fwdt = sb("fwdt", o_r, [P, 4, 2, 256])
        invt = sb("invt", o_r + 8 * K, [P, 4, 2, 256])
        dect = sb("dect", o_r + 8 * K, [P, 4, 512])
        KS = sb("KS", o_r + 16 * K, [P, 2, 2, 4, 512])
        Z = sb("Z", o_r + 48 * K, [P, KT, L])
        X0 = sb("X0", o_r + 64 * K, [P, KT, L])
        HP = sb("HP", o_r + 48 * K, [P, 4, D])
        HM = sb("HM", o_r + 64 * K, [P, 4, D])
        fwo = sb("fwo", o_r + 80 * K, [HYF, 2 * D])
        fA = sb("fA", o_r + 32 * K, [P, 2, 512])
        fB = sb("fB", o_r + 36 * K, [P, 2, 512])
        aab = sb("aab", o_r + 40 * K, [P, 2, 2, 512])
        kE = sb("kE", o_r + 8 * K, [P, 2, 2, 512])
        absum = sb("absum", o_t + 14 * K, [P, D])
        cb_ = sb("cb_", o_t, [P, 2, L + 2])
        ca = sb("ca", o_t + 5 * K, [P, 2, L])
        x1c = sb("x1c", o_t + 9 * K, [P, L])
        zN = sb("zN", o_h, [P, 4, D])
        zs = sb("zs", o_h + 16 * K, [P, 8, 512])
        zE = sb("zE", o_t, [P, 2, 512])
        zpD = sb("zpD", o_t + 4 * K, [P, 4, 512])
        zpP = sb("zpP", o_t + 12 * K, [P, 4, 512])
        row = sb("row", o_r + 80 * K, [1, 2, 512])
        yt = sb("yt", o_t, [P, 2, L])
        yv = sb("yv", o_t + 4 * K, [P, 2, L])
        hyt = sb("hyt", o_t + 16 * K, [P, 2, L])
        centre = sb("centre", o_r + 74 * K, [P, P])
        gsq = sb("gsq", o_r + 50 * K, [P, NPAIR, L])

        PS = stack.enter_context(nc.psum_tensor("PS", [P, 8, 512], F32))

        def col(name, i=0, n=1):
            return colt[:, COL[name] + i:COL[name] + i + n]

        def der(name, i=0, n=1):
            return dert[:, DER[name] + i:DER[name] + i + n]

        def sem(name):
            return stack.enter_context(nc.semaphore(name))

        s_small = sem("s_small")
        s_feat = sem("s_feat")
        s_x = sem("s_x")
        s_xc = sem("s_xc")
        s_rope = sem("s_rope")
        s_dist = sem("s_dist")
        s_hyc = sem("s_hyc")
        s_fwd = sem("s_fwd")
        s_dec = [sem(f"s_dec{i}") for i in range(4)]
        s_inv = sem("s_inv")
        s_out = sem("s_out")
        wload = [sem(f"wload{i}") for i in range(RAW)]
        w_hi = sem("w_hi")
        w_lo = sem("w_lo")
        w_done = sem("w_done")
        a_pr = [sem("a_prD"), sem("a_prP")]
        a_sum = [sem("a_sumD"), sem("a_sumP")]
        mod_done = sem("mod_done")
        m_pr = [sem("m_prD"), sem("m_prP")]
        m_sum = [sem("m_sumD"), sem("m_sumP")]
        s_act = sem("s_act")
        s_dve = sem("s_dve")
        s_pool = sem("s_pool")
        silu_c = sem("silu_c")
        f_mm, f_arg, f_sin = sem("f_mm"), sem("f_arg"), sem("f_sin")
        n_sq, n_acc, n_ss, n_rt = sem("n_sq"), sem("n_acc"), sem("n_ss"), sem("n_rt")
        n_rs, n_hi, n_h, n_x = sem("n_rs"), sem("n_hi"), sem("n_h"), sem("n_x")
        n_t = [sem("n_tD"), sem("n_tP")]
        n_fin = [sem("n_fin0"), sem("n_fin1")]
        n_y = sem("n_y")
        m_cols = sem("m_cols")
        m_gain = sem("m_gain")
        q_ev, q_sw, q_ss, q_rt, q_done, v_tr, v_ev = (sem("q_ev"), sem("q_sw"), sem("q_ss"), sem("q_rt"),
                                                      sem("q_done"), sem("v_tr"), sem("v_ev"))
        a_s, a_mx, a_exp, a_p, a_tr, a_pt, a_pv, a_o = (sem("a_s"), sem("a_mx"), sem("a_exp"), sem("a_p"),
                                                        sem("a_tr"), sem("a_pt"), sem("a_pv"), sem("a_o"))
        r_u, r_e, r_strip, r_s, r_p, r_pv, r_o = (sem("r_u"), sem("r_e"), sem("r_strip"), sem("r_s"), sem("r_p"),
                                                  sem("r_pv"), sem("r_o"))
        a_h = sem("a_h")
        g_sq, g_var, g_ln, g_h = sem("g_sq"), sem("g_var"), sem("g_ln"), sem("g_h")
        g_hi = sem("g_hi")
        h_sl, h_val, h_hi, h_lo, h_g, h_cv = (sem("h_sl"), sem("h_val"), sem("h_hi"), sem("h_lo"), sem("h_g"),
                                              sem("h_cv"))
        h_tp = sem("h_tp")
        h_ct = sem("h_ct")
        h_cp = sem("h_cp")
        k_h, k_ab, k_hp, k_col, k_f, k_e, k_k = (sem("k_h"), sem("k_ab"), sem("k_hp"), sem("k_col"), sem("k_f"),
                                                 sem("k_e"), sem("k_k"))
        y_b, y_c, y_z, z_tr, z_n, z_f, z_e, z_b, z_q, z_y = (
            sem("y_b"), sem("y_c"), sem("y_z"), sem("z_tr"), sem("z_n"), sem("z_f"), sem("z_e"), sem("z_b"),
            sem("z_q"), sem("z_y"))
        i_mm, i_ev, i_val, i_hi, i_h = sem("i_mm"), sem("i_ev"), sem("i_val"), sem("i_hi"), sem("i_h")
        o_ev = sem("o_ev")
        z_p, z_w = sem("z_p"), sem("z_w")
        k_abs, k_sum, k_inv = sem("k_abs"), sem("k_sum"), sem("k_inv")
        m_lg, g_rs, g_val, g_gate = sem("m_lg"), sem("g_rs"), sem("g_val"), sem("g_gate")
        a_hi = sem("a_hi")

        block = stack.enter_context(nc.Block())

        NCTX = 10
        NV = 5
        NROPE = 13
        DVE_TAPS, POOL_TAPS = (0, 1, 2, 3, 5), (6, 7, 8)
        PE_SUMS = (3, 5)

        def totals(k):
            return len([j for j in range(k + 1) if j not in PE_SUMS])
        NH = {0: 0, 1: KT, 3: 2 * KT, 5: 3 * KT, 6: 4 * KT}
        NX = {2: 0, 4: KT}

        def last_tile(eng, k):
            eng.wait_ge(n_x if k in NX else n_h, (NX[k] if k in NX else NH[k]) + KT)

        def root_of(k):
            return rstdc[:, :] if k == 1 else rstd[:, :]

        def wait_tile(eng, k, kt):
            if kt % 4 == 3:
                eng.wait_ge(n_t[1], 2 * k + kt // 4 + 1)
            else:
                eng.wait_ge(n_t[0], 6 * k + kt - kt // 4 + 1)

        def acc_of(k):
            return accc[:, :] if k == 1 else acc[:, :]

        def wait_buffer(eng, t):
            if t >= 4:
                k, kt = (t - 4) // KT, (t - 4) % KT
                eng.wait_ge(n_x if k in NX else n_h, (NX[k] if k in NX else NH[k]) + kt + 1)
        LAG = 2
        STEPS = 32 + LAG

        GN_BANK = (1, 2, 3, 6)

        def ret_steps(s):
            s -= LAG
            return range(s * 3 // 2, (s + 1) * 3 // 2) if s >= 0 else range(0)

        def mod_units(s):
            if not 0 <= s < 32:
                return range(0)
            first = 16 + 2 * s + 2 * ((s + 3) // 4)
            return range(first, first + (4 if s % 4 == 0 else 2))

        OFF_PE = (1, 4, 6, 9, 11, 14)
        ON_PE = [m for m in range(16) if m not in OFF_PE]
        MOD_A = len(ON_PE) + 2 * len(OFF_PE)

        @block.sync
        def _(sp):
            def load(name, i, dst_slot, src):
                sp.dma_start(wraw[:, dst_slot, 0:WIDTH[name]], src).then_inc(wload[dst_slot], 16)

            def load_static(name, i):
                g = START[name] + i
                if g >= RAW:
                    split, ordinal = KIND[g - RAW]
                    if split:
                        sp.wait_ge(w_lo, ordinal + 1)
                    elif ordinal in OFF_PE:
                        k = OFF_PE.index(ordinal)
                        sp.wait_ge(a_pr[0], k + 1 if k < 3 else 2 * k - 1)
                        if k < 3:
                            sp.wait_ge(a_pr[1], k + 1)
                    elif ordinal < 16:
                        sp.wait_ge(mod_done, ON_PE.index(ordinal) + 1)
                    else:
                        sp.wait_ge(m_pr[ordinal % 2], (ordinal - 16) // 2 + 1)
                load(name, i, g % RAW, w[name][i])

            def load_loop(name, first, times):
                with sp.Fori(0, times) as i:
                    for u in range(RAW):
                        sp.wait_ge(w_lo, i * RAW + (ORD[name] + first + u - RAW + 1))
                        load(name, i, (START[name] + first + u) % RAW, w[name][i * RAW + (first + u)])

            sp.dma_start(colt[:, :], cols).then_inc(s_small, 16)
            sp.dma_start(posb[:, :], posT).then_inc(s_feat, 16)
            sp.dma_start(fwb[:, :, :], fw).then_inc(s_feat, 16)
            for j, m in enumerate((ones, bones, swap, ident)):
                sp.dma_start(m[:, :], mats[j]).then_inc(s_small, 16)
            for i in range(RAW):
                load_static("mod_a", i)
            for i in range(RAW, 16):
                if i < RAW + 2:
                    k0 = (i - RAW) * (KT // 2)
                    sp.dma_start(X[:, k0:k0 + KT // 2, :], xT[:, k0:k0 + KT // 2]).then_inc(s_x, 16)
                if i == 8:
                    sp.dma_start(Xc[:, :, :], ctxT).then_inc(s_xc, 16)
                load_static("mod_a", i)
            for i in range(22):
                load_static("w_in", i)
                if i == 0:
                    sp.dma_start(ropet[:, :, :], rope).then_inc(s_rope, 16)
            for i in range(RAW):
                load_static("mod_b", i)
            sp.wait_ge(q_done, NROPE)
            sp.wait_ge(v_ev, NV)
            sp.dma_start(distt[:, :], dist).then_inc(s_dist, 16)
            with sp.Fori(1, (2 * MODU - 16) // RAW) as i:
                for u in range(RAW):
                    sp.wait_ge(m_pr[u % 2], i * (RAW // 2) + (u // 2 + 1 - RAW // 2))
                    load("mod_b", i, (START["mod_b"] + u) % RAW, w["mod_b"][i * RAW + u])
            for i in range(8):
                load_static("w_out", i)
            load_loop("ffn_in", 0, 2 * FT // RAW)
            load_loop("ffn_out", 0, 4)
            for i in range(RAW):
                load_static("hy_in", i)
            sp.wait_ge(w_done, ORD["hy_in"])
            sp.dma_start(fwo[:, :], fwout).then_inc(s_hyc, 16)
            for t in range(4):
                sp.dma_start(dect[:, t, :], decay[0, t]).then_inc(s_dec[t], 16)
            sp.dma_start(fwdt[:, :, :, :], fwd).then_inc(s_fwd, 16)
            for t in range(4):
                sp.wait_ge(k_ab, t + 1)
                sp.dma_start(dect[:, t, :], decay[1, t]).then_inc(s_dec[t], 16)
            sp.wait_ge(k_k, 4)
            sp.dma_start(invt[:, :, :, :], inv).then_inc(s_inv, 16)
            load_loop("hy_in", RAW, 5)
            for i in range(8):
                load_static("hy_out", i)
            load_loop("up", 0, 2 * FT // RAW)
            load_loop("down", 0, 4)
            for q in range(2):
                sp.wait_ge(n_fin[0], 3 * (q + 1))
                sp.wait_ge(n_fin[1], q + 1)
                sp.dma_start(out[:, 4 * q:4 * q + 4], Y[:, 4 * q:4 * q + 4, :]).then_inc(s_out, 16)
            sp.wait_ge(s_out, 32)

        def split_hi(act, name, i, r=None):
            o, g, n = ORD[name] + i, START[name] + i, WIDTH[name]
            k = 0 if r is None else r
            act.wait_ge(wload[g % RAW], k * 16 + 16 * (g // RAW + 1))
            if o >= 2:
                act.wait_ge(w_done, k * RAW + (o - 1))
            nc.scalar.activation(wsp[:, o % 2, 0, 0:n], wraw[:, g % RAW, 0:n], ACT.Copy).then_inc(w_hi, 1)

        def split_lo(dve, name, i, r=None):
            o, g, n = ORD[name] + i, START[name] + i, WIDTH[name]
            k = 0 if r is None else r
            dve.wait_ge(w_hi, k * RAW + (o + 1))
            nc.vector.tensor_tensor(wsp[:, o % 2, 1, 0:n], wraw[:, g % RAW, 0:n],
                                    wsp[:, o % 2, 0, 0:n].bitcast(F32), ALU.subtract).then_inc(w_lo, 1)

        def split_matmuls(pe, o, psum, h, kts, wk0, first, last, ready=None):
            mm = None
            for kt in kts:
                wk = kt - wk0
                if ready is not None and ready[1] + kt >= 0:
                    pe.wait_ge(ready[0], ready[1] + kt + 1)
                for a, b in ((0, 0), (0, 1), (1, 0)):
                    mm = nc.tensor.matmul(psum, wsp[:, o % 2, a, wk * P:(wk + 1) * P], h[:, b, kt, :],
                                          start=first and kt == kts[0] and (a, b) == (0, 0),
                                          stop=last and kt == kts[-1] and (a, b) == (1, 0))
            return mm

        def mod_a_multiply(eng, ops, e, i, which):
            m = OFF_PE[i]
            eng.wait_ge(wload[m % RAW], 16 * (m // RAW + 1))
            a = DER["silu_c"] + which
            ops.tensor_tensor(aprod[:, e, :].rearrange("p (k n) -> p k n", n=P),
                              wraw[:, m % RAW, 0:U1].rearrange("p (k n) -> p k n", n=P),
                              dert[:, a:a + 3 * KT - 2:3].unsqueeze(2).to_broadcast([P, KT, P]),
                              ALU.mult).then_inc(a_pr[e], 1)

        def mod_multiply(eng, ops, m):
            g, e = START["mod_b"] + m - 16, (m - 16) % 2
            eng.wait_ge(wload[g % RAW], 16 * (g // RAW + 1))
            a = DER["silu_c"] + (0 if m < MODU else 2)
            ops.tensor_tensor(mprod[:, e, :].rearrange("p (k n) -> p k n", n=P),
                              wraw[:, g % RAW, 0:U1].rearrange("p (k n) -> p k n", n=P),
                              dert[:, a:a + 3 * KT - 2:3].unsqueeze(2).to_broadcast([P, KT, P]),
                              ALU.mult).then_inc(m_pr[e], 1)

        @block.tensor
        def _(pe):
            def filter_layer(l):
                if l:
                    pe.wait_ge(f_sin, l)
                k = 2 * BANDS + 1 if l == 0 else HYF
                nc.tensor.matmul(PS[0:HYF, 6, :], fwb[0:k, l, :], posb[:, :] if l == 0 else fh[:, :],
                                 start=True, stop=True).then_inc(f_mm, 1)

            def modulation(m):
                pe.wait_ge(wload[m % RAW], 16 * (m // RAW + 1))
                for kt in range(KT):
                    mm = nc.tensor.matmul(PS[:, 7, 2 * m:2 * m + 2], wraw[:, m % RAW, kt * P:(kt + 1) * P],
                                          dert[:, DER["silu_c"] + 3 * kt:DER["silu_c"] + 3 * kt + 2],
                                          start=kt == 0, stop=kt == KT - 1)
                mm.then_inc(mod_done, 1)

            def modulation_total(m):
                pe.wait_ge(m_sum[m % 2], (m - 16) // 2 + 1)
                c = 2 * m if m < MODU else MODU + m
                nc.tensor.matmul(PS[:, 7, c:c + 1], msum[:, m % 8, :], der("one"), start=True,
                                 stop=True).then_inc(mod_done, 1)

            def total(k):
                pe.wait_ge(n_acc, KT * (k + 1))
                n = LC if k == 1 else L
                nc.tensor.matmul(PS[:, 5 if k == 1 else 6, 0:n], ones[:, :], acc_of(k), start=True, stop=True).then_inc(n_ss, 1)

            def filter_tile(j):
                c, t = j // 4, j % 4
                par, mt = t // 2, t % 2
                if j:
                    pe.wait_ge(k_ab, j)
                for d in range(2):
                    mm = nc.tensor.matmul(PS[:, 4 + d, :], feat[:, mt * 256 + par:(mt + 1) * 256:2],
                                          fwo[:, d * D + c * 512:d * D + c * 512 + 512], start=True, stop=True)
                mm.then_inc(k_h, 1)

            def squares_total(k, kts=range(KT)):
                pe.wait_ge(n_rt, k)
                for kt in kts:
                    q = k * KT + kt
                    pe.wait_ge(n_sq, q + 1)
                    nc.tensor.matmul(PS[:, 6, :], ones[:, :], sqb[:, q % 2, :], start=kt == 0,
                                     stop=kt == KT - 1).then_inc(n_acc, 1)

            pe.wait_ge(s_feat, 32)
            pe.wait_ge(s_small, 80)
            filter_layer(0)
            pe.wait_ge(silu_c, 1)
            for n, m in enumerate(ON_PE):
                modulation(m)
                if n in (2, 5):
                    filter_layer((n + 1) // 3)
            pe.wait_ge(f_arg, 3)
            total(0)
            total(1)
            for which in range(2):
                for i in range(len(OFF_PE)):
                    pe.wait_ge(a_sum[0 if which == 0 or i >= 3 else 1],
                               i + 1 if i < 3 else 2 * i - 2 + which)
                    c = 2 * OFF_PE[i] + which
                    nc.tensor.matmul(PS[:, 7, c:c + 1], asum[:, 2 * i + which, :], der("one"), start=True,
                                     stop=True).then_inc(mod_done, 1)
            def aux(n):
                if n < NV:
                    pe.wait_ge(q_ev, n + 1)
                    if n == 0:
                        pe.wait_ge(m_cols, 1)
                    else:
                        pe.wait_ge(v_ev, n)
                    for t in range(LA // P):
                        dst = PS[:, 6 + t // 4, (t % 4) * P:(t % 4 + 1) * P]
                        if n == 0:
                            tr = nc.tensor.transpose(dst, VT[:, n % 2, t * P:(t + 1) * P], ident[:, :])
                        else:
                            tr = nc.tensor.matmul(dst, VT[:, n % 2, t * P:(t + 1) * P], centre[:, :], start=True,
                                                  stop=True)
                    tr.then_inc(v_tr, 1)
                elif n < NV + NROPE:
                    pe.wait_ge(q_ev, n + 1)
                    pe.wait_ge(v_ev, NV)
                    if n > NV:
                        pe.wait_ge(q_done, n - NV)
                    nc.tensor.matmul(PS[:, 4, :], swap[:, :], RU[:, n % 2, 0:L], start=True, stop=True).then_inc(q_sw, 1)
                    if n == NV or 10 <= n < 14:
                        mm = nc.tensor.matmul(PS[:, 5, :], bones[:, :], SQ[:, 0:L], start=True, stop=True)
                        if n == NV:
                            mm = nc.tensor.matmul(PS[:, 6, 0:LC], bones[:, :], SQ[:, L:LA], start=True, stop=True)
                        mm.then_inc(q_ss, 1)

            for n in range(22):
                pe.wait_ge(w_lo, ORD["w_in"] + n + 1)
                if n >= 2:
                    pe.wait_ge(q_ev, n - 1)
                mm = split_matmuls(pe, ORD["w_in"] + n, PS[:, n % 2, :], H, range(KT), 0, True, True,
                                   (n_h, 0) if n == 0 else None)
                if n < NCTX:
                    mm = split_matmuls(pe, ORD["w_in"] + n, PS[:, 2 + n % 2, 0:LC], Hc, range(KT), 0, True, True,
                                       (n_h, KT) if n == 0 else None)
                mm.then_inc(w_done, 1)
                if n:
                    aux(n - 1)

            def att_scores(s):
                t, lo, qt = s // 8, (s // 4) % 2 * HD, s % 4
                if s == 0:
                    pe.wait_ge(q_ev, 22)
                    pe.wait_ge(q_done, NROPE)
                else:
                    pe.wait_ge(a_exp, s)
                for a, b, bank in ((0, L, 0), (L, LA, 1)):
                    mm = nc.tensor.matmul(PS[:, bank, 0:b - a], QA[lo:lo + HD, t, qt * P:(qt + 1) * P],
                                          KA[lo:lo + HD, a:b], start=True, stop=True)
                mm.then_inc(a_s, 1)

            def att_transposes(s):
                pe.wait_ge(a_p, s + 1)
                if s:
                    pe.wait_ge(a_pt, s)
                for kt in range(LA // P):
                    tr = nc.tensor.transpose(PS[:, 2 + kt // 4, (kt % 4) * P:(kt % 4 + 1) * P],
                                             Pb[:, s % 2, kt * P:(kt + 1) * P], ident[:, :])
                tr.then_inc(a_tr, 1)

            def att_values(s):
                lo, qt = (s // 4) % 2 * HD, s % 4
                pe.wait_ge(a_pt, s + 1)
                if s % 8 == 0 and s:
                    pe.wait_ge(a_o, s // 8)
                for kt in range(LA // P):
                    mm = nc.tensor.matmul(PS[lo:lo + HD, 4, qt * P:(qt + 1) * P], V[:, kt, lo:lo + HD],
                                          PT[:, s % 2, kt * P:(kt + 1) * P], start=kt == 0, stop=kt == LA // P - 1)
                mm.then_inc(a_pv, 1)

            def ret_scores(r):
                h, kt = r // 6, r % 6
                lo = h % 2 * HD
                if r:
                    pe.wait_ge(r_p, r)
                nc.tensor.matmul(PS[:, 5, :], KR[lo:lo + HD, h // 2, kt * P:(kt + 1) * P],
                                 QR[lo:lo + HD, h // 2, :], start=True, stop=True).then_inc(r_s, 1)

            def ret_values(r):
                h, kt = r // 6, r % 6
                lo = h % 2 * HD
                pe.wait_ge(r_p, r + 1)
                if r % 12 == 0 and r:
                    pe.wait_ge(r_o, r // 12)
                nc.tensor.matmul(PS[lo:lo + HD, 6, :], V[:, kt, P + h * HD:P + (h + 1) * HD], pr[:, r % 2, :],
                                 start=kt == 0, stop=kt == 5).then_inc(r_pv, 1)

            def gn_variance(t):
                pe.wait_ge(g_sq, t + 1)
                nc.tensor.matmul(PS[:, GN_BANK[t], :], bones[:, :], gsq[:, t, :], start=True, stop=True).then_inc(g_var, 1)

            def ret_pair(r):
                ret_scores(r)
                if r:
                    ret_values(r - 1)

            for s in range(STEPS):
                rs = ret_steps(s)
                if rs:
                    ret_pair(rs[0])
                if s < 32:
                    att_scores(s)
                if 0 < s <= 32:
                    att_transposes(s - 1)
                for m in mod_units(s - 2):
                    modulation_total(m)
                if s == 33:
                    pe.wait_ge(a_exp, 32)
                    gn_variance(0)
                if len(rs) == 2:
                    ret_pair(rs[1])
                if s == 33:
                    pe.wait_ge(a_pt, 32)
                    gn_variance(1)
                if 0 < s <= 32:
                    att_values(s - 1)
            ret_values(47)
            gn_variance(2)

            pe.wait_ge(a_o, 4)
            for n in range(2):
                pe.wait_ge(w_lo, ORD["w_out"] + n + 1)
                if n == 1:
                    pe.wait_ge(g_ln, 1)
                split_matmuls(pe, ORD["w_out"] + n, PS[:, n, :], H, range(0, 4), 0, True, False)
                if n == 0:
                    pe.wait_ge(r_o, 4)
                    gn_variance(3)
            for n in range(2):
                split_matmuls(pe, ORD["w_out"] + n, PS[:, n, :], H, range(4, KT - 1), 0, False, False, (g_h, -4))
            for n in range(8):
                if n < 2:
                    mm = split_matmuls(pe, ORD["w_out"] + n, PS[:, n, :], H, range(KT - 1, KT), 0, False, True,
                                       (g_h, -4))
                else:
                    pe.wait_ge(w_lo, ORD["w_out"] + n + 1)
                    pe.wait_ge(n_y, n - 1)
                    mm = split_matmuls(pe, ORD["w_out"] + n, PS[:, n % 2, :], H, range(KT), 0, True, True)
                mm.then_inc(w_done, 1)
            total(2)
            squares_total(3)

            def pairs(name, normed, free_a, base_a, free_b, base_b):
                def four(i, first):
                    for u in range(4):
                        pe.wait_ge(w_lo, i * 4 + (ORD[name] + u + 1))
                        if not first:
                            free, base = (free_a, base_a) if u % 2 == 0 else (free_b, base_b)
                            pe.wait_ge(free, i * 2 + (base + u // 2 - 1))
                        split_matmuls(pe, ORD[name] + u, PS[:, u, :], H, range(KT), 0, True, True,
                                      (n_h, normed) if first and u == 0 else None).then_inc(w_done, 1)
                four(0, True)
                with pe.Fori(1, FT // 2) as i:
                    four(i, False)

            def down(name, base_h, free, base):
                def four(i, first):
                    for u in range(4):
                        pe.wait_ge(w_lo, i * 4 + (ORD[name] + u + 1))
                        if not first and u % 2 == 0:
                            pe.wait_ge(free, i * 2 + (base + u // 2 - 1))
                        k0 = u % 2 * FH
                        split_matmuls(pe, ORD[name] + u, PS[:, u // 2, :], hid, range(k0, k0 + FH), k0, u % 2 == 0,
                                      u % 2 == 1, (h_lo, base_h) if first and u < 2 else None).then_inc(w_done, 1)
                four(0, True)
                with pe.Fori(1, 4) as i:
                    four(i, False)

            pairs("ffn_in", 2 * KT, h_sl, 0, h_val, 0)
            down("ffn_out", 0, n_y, KT)

            total(4)
            pe.wait_ge(s_hyc, 16)

            def spectrum_part(a, cos_src, sin_src, c, f, b0):
                src = cos_src if a % 2 == 0 else sin_src
                for mt in range(2):
                    mm = nc.tensor.matmul(PS[:, b0 + a, :], fwdt[:, a, mt, f * P:(f + 1) * P],
                                          src[:, (a // 2) * 2 + mt, c * 512:(c + 1) * 512], start=mt == 0,
                                          stop=mt == 1)
                if cos_src is not sin_src and a == 1 and f == 0:
                    for mt in range(2):
                        mm = nc.tensor.matmul(PS[0:1, b0 + a, :], fwdt[:, a, mt, 0:1],
                                              cos_src[:, mt, c * 512:(c + 1) * 512], start=mt == 0, stop=mt == 1)
                return mm

            def spectrum(cos_src, sin_src, c, f, b0):
                for a in range(4):
                    mm = spectrum_part(a, cos_src, sin_src, c, f, b0)
                return mm

            filter_tile(0)
            filter_tile(1)
            squares_total(5, range(0, 2))
            filter_tile(2)
            squares_total(5, range(2, 5))
            filter_tile(3)
            squares_total(5, range(5, KT))
            filter_tile(4)
            pe.wait_ge(s_fwd, 16)
            pe.wait_ge(k_hp, 4)
            for a in range(4):
                mm = spectrum_part(a, HP, HM, 0, 0, 0)
                if a < 3:
                    filter_tile(5 + a)
            mm.then_inc(k_f, 1)
            for k in range(1, 4):
                if k == 1:
                    pe.wait_ge(n_rt, 6)
                    pe.wait_ge(k_ab, 8)
                else:
                    pe.wait_ge(k_hp, 8)
                    pe.wait_ge(k_k, k - 1)
                spectrum(HP, HM, k // 2, k % 2, 4 * (k % 2)).then_inc(k_f, 1)
            pe.wait_ge(k_sum, 8)
            pe.wait_ge(k_k, 3)
            for j in range(KT):
                mm = nc.tensor.matmul(PS[:, 0, j:j + 1], absum[:, j * P:(j + 1) * P], ones[:, 0:1],
                                      start=True, stop=True)
            mm.then_inc(k_col, 1)

            def hy_four(i, first):
                for u in range(4):
                    pe.wait_ge(w_lo, i * 4 + (ORD["hy_in"] + u + 1))
                    if first and u == 0:
                        pe.wait_ge(k_inv, 1)
                    if not (first and u < 2):
                        pe.wait_ge(y_b, i * 4 + (u - 1))
                    split_matmuls(pe, ORD["hy_in"] + u, PS[:, u % 2, :], H, range(KT), 0, True, True,
                                  (n_h, 3 * KT) if first and u == 0 else None).then_inc(w_done, 1)
            hy_four(0, True)
            with pe.Fori(1, 6) as i:
                hy_four(i, False)

            pe.wait_ge(y_z, KT)
            pe.wait_ge(y_b, 24)
            for g in range(8):
                par, mt, c = g // 4, g // 2 % 2, g % 2
                if g >= 4:
                    pe.wait_ge(z_n, g - 3)
                for j in range(4):
                    tr = nc.tensor.transpose(PS[:, g % 4, j * P:(j + 1) * P],
                                             Z[:, 4 * c + j, mt * 256 + par:(mt + 1) * 256:2], ident[:, :])
                tr.then_inc(z_tr, 1)
            pe.wait_ge(z_n, 8)
            for k in range(4):
                if k >= 2:
                    pe.wait_ge(z_b, k - 1)
                spectrum(zN, zN, k // 2, k % 2, 4 * (k % 2)).then_inc(z_f, 1)
            pe.wait_ge(s_inv, 16)
            for j in range(KT):
                if j % 4 == 0:
                    pe.wait_ge(z_y, j // 2 + 2)
                    pe.wait_ge(z_b, j // 4 + 3)
                for par in range(2):
                    for n in range(4):
                        a, f = 2 * par + n // 2, n % 2
                        mm = nc.tensor.matmul(PS[:, j, par * 256:(par + 1) * 256],
                                              KS[:, j // 4, f, a, (j % 4) * P:(j % 4 + 1) * P], invt[:, a, f, :],
                                              start=n == 0, stop=n == 3)
                mm.then_inc(i_mm, 1)
            for n in range(8):
                pe.wait_ge(w_lo, ORD["hy_out"] + n + 1)
                if n >= 2:
                    pe.wait_ge(o_ev, n - 1)
                split_matmuls(pe, ORD["hy_out"] + n, PS[:, n % 2, :], H, range(KT), 0, True, True,
                              (i_h, 0) if n == 0 else None).then_inc(w_done, 1)
            total(6)
            pairs("up", 4 * KT, h_ct, 0, h_val, FT)
            down("down", FT, n_x, 3 * KT)
            total(7)

        @block.scalar
        def _(act):
            own = Own(act, s_act)
            SC = nc.scalar

            def root(k):
                if k in PE_SUMS:
                    act.wait_ge(n_acc, KT * (k + 1))
                else:
                    act.wait_ge(n_ss, totals(k))
                if k >= 2:
                    last_tile(act, k - 1)
                SC.activation(rtmp[:, :], PS[:, 6, :], ACT.Ln, bias=col("eps")).then_inc(n_rt, 1)
                act.wait_ge(n_rt, k + 1)
                SC.activation(rstd[:, :], rtmp[:, :], ACT.Exp, scale=-0.5).then_inc(n_rs, 1)

            def square(q, src, n=L):
                if q >= 2:
                    act.wait_ge(n_acc, q - 1)
                SC.activation(sqb[:, q % 2, 0:n], src, ACT.Square).then_inc(n_sq, 1)

            def high(k, kt, dst, shift, n=L):
                wait_tile(act, k, kt)
                SC.activation(dst, tb[:, (k * KT + kt) % 4, 0:n], ACT.Identity, bias=shift).then_inc(n_hi, 1)

            def mod_col(chunk, kt, which=0):
                a = DER["mod"] + 2 * (KT * chunk + kt) + which
                return dert[:, a:a + 1]

            def mod2_col(chunk, kt):
                return der("mod2", KT * chunk + kt)

            act.wait_ge(s_small, 80)
            SC.activation(der("silu_c", 0, 3 * KT), col("c", 0, 3 * KT), ACT.Silu).then_inc(silu_c, 1)
            SC.activation(der("lg_f", 0, 8), col("dec_f", 0, 8), ACT.Exp).then_inc(m_lg, 1)
            SC.activation(der("lg_b", 0, 8), col("dec_b", 0, 8), ACT.Exp).then_inc(m_lg, 1)
            for l in range(3):
                act.wait_ge(f_arg, l + 1)
                if l:
                    act.wait_ge(f_mm, l + 1)
                SC.activation((fh if l < 2 else feat)[:, :], fa[:, :], ACT.Sin).then_inc(f_sin, 1)
            act.wait_ge(s_x, 32)
            for kt in range(KT):
                square(kt, X[:, kt, :])
            act.wait_ge(s_xc, 16)
            for kt in range(KT):
                square(KT + kt, Xc[:, kt, :], LC)
            act.wait_ge(n_ss, 1)
            SC.activation(rtmp[:, :], PS[:, 6, :], ACT.Ln, bias=col("eps")).then_inc(n_rt, 1)
            act.wait_ge(n_ss, 2)
            SC.activation(accc[:, :], PS[:, 5, 0:LC], ACT.Ln, bias=col("eps")).then_inc(n_rt, 1)
            act.wait_ge(n_rt, 1)
            act.wait_ge(n_rt, 2)
            SC.activation(rstd[:, :], rtmp[:, :], ACT.Exp, scale=-0.5).then_inc(n_rs, 1)
            SC.activation(rstdc[:, :], accc[:, :], ACT.Exp, scale=-0.5).then_inc(n_rs, 1)
            split_hi(act, "w_in", 0)
            split_hi(act, "w_in", 1)
            for kt in range(KT):
                high(0, kt, H[:, 0, kt, :], mod_col(0, kt))
            for kt in range(KT):
                high(1, kt, Hc[:, 0, kt, :], mod_col(0, kt, 1), LC)

            def normed_head(n):
                return n == NV or 10 <= n < 14

            for n in range(22):
                act.wait_ge(w_done, ORD["w_in"] + n + 1)
                if n + 2 < 22:
                    split_hi(act, "w_in", n + 2)
                lat, ctx = PS[:, n % 2, :], PS[:, 2 + n % 2, 0:LC]
                if n == 0:
                    act.wait_ge(n_h, 2 * KT)
                m = n - 1
                if normed_head(m):
                    act.wait_ge(q_ss, 1 if m == NV else m - 8)
                    if m == NV:
                        own(SC.activation(RT[:, L:LA], PS[:, 6, 0:LC], ACT.Sqrt, bias=col("eps")))
                    else:
                        act.wait_ge(q_done, m - NV)
                    SC.activation(RT[:, 0:L], PS[:, 5, :], ACT.Sqrt, bias=col("eps")).then_inc(q_rt, 1)
                if n < NV:
                    if n >= 2:
                        act.wait_ge(v_tr, n - 1)
                    own(SC.activation(VT[:, n % 2, 0:L], lat, ACT.Copy))
                    SC.activation(VT[:, n % 2, L:LA], ctx, ACT.Copy).then_inc(q_ev, 1)
                    continue
                if n < 18 and n - NV >= 2:
                    act.wait_ge(q_done, n - NV - 1)
                if normed_head(n):
                    g = col("k_g") if n == NV else col("q_g")
                    own(SC.activation(SQ[:, 0:L], lat, ACT.Square))
                    if n == NV:
                        own(SC.activation(SQ[:, L:LA], ctx, ACT.Square))
                        own(SC.activation(RU[:, n % 2, L:LA], ctx, ACT.Copy, scale=g))
                    SC.activation(RU[:, n % 2, 0:L], lat, ACT.Copy, scale=g).then_inc(q_ev, 1)
                elif n < 10:
                    own(SC.activation(KR[:, n - 6, L:LA], ctx, ACT.Copy, scale=HD**-0.5))
                    SC.activation(RU[:, n % 2, 0:L], lat, ACT.Copy, scale=HD**-0.5).then_inc(q_ev, 1)
                elif n < 18:
                    SC.activation(RU[:, n % 2, 0:L], lat, ACT.Copy).then_inc(q_ev, 1)
                else:
                    SC.activation(G[:, n - 18, :], lat, ACT.Silu).then_inc(q_ev, 1)

            def exp_strip(h):
                act.wait_ge(r_u, h + 1)
                if h >= 2:
                    act.wait_ge(r_p, 6 * (h - 1))
                if h:
                    act.wait_ge(r_strip, h)
                own(SC.activation(ea[:, :], ea[:, :], ACT.Exp))
                own(SC.activation(strip[:, h % 2, DIST:], distt[:, 3 * DIST:3 * DIST + CDIST], ACT.Exp,
                                  scale=der("lg_f", h)))
                SC.activation(ec[:, :], distt[:, 3 * DIST + CDIST:], ACT.Exp, scale=der("lg_b", h)).then_inc(r_e, 1)

            def att_out(t):
                act.wait_ge(a_pv, 8 * (t + 1))
                SC.activation(H[:, 0, t, :], PS[:, 4, :], ACT.Copy).then_inc(a_hi, 1)

            def ret_out(t):
                act.wait_ge(r_pv, 12 * (t + 1))
                act.wait_ge(a_s, min(32, 8 * (t + 1)))
                SC.activation(gsq[:, t, :], PS[:, 6, :], ACT.Square).then_inc(g_sq, 1)
                SC.activation(QR[:, t, :], PS[:, 6, :], ACT.Copy).then_inc(r_o, 1)

            def gn_log(t):
                act.wait_ge(g_var, t + 1)
                SC.activation(gsq[:, t, :], PS[:, GN_BANK[t], :], ACT.Ln, bias=col("eps")).then_inc(g_ln, 1)

            def gn_root(t):
                act.wait_ge(g_ln, t + 1)
                SC.activation(gsq[:, t, :], gsq[:, t, :], ACT.Exp, scale=-0.5).then_inc(g_rs, 1)

            def gn_high(t):
                act.wait_ge(g_val, t + 1)
                SC.activation(H[:, 0, 4 + t, :], G[:, t, :], ACT.Copy).then_inc(g_hi, 1)

            for s in range(STEPS):
                if s < 32:
                    act.wait_ge(a_mx, s + 1)
                    if s >= 2:
                        act.wait_ge(a_tr, s - 1)
                        act.wait_ge(a_p, s - 1)
                    SC.activation(Pb[:, s % 2, :], PS[:, 0:2, :].rearrange("p a b -> p (a b)")[:, 0:LA], ACT.Exp,
                                  bias=smx[:, s % 2:s % 2 + 1], scale=HD**-0.5,
                                  accum_out=rsum[:, s % 2:s % 2 + 1]).then_inc(a_exp, 1)
                if 0 < s <= 32:
                    act.wait_ge(a_tr, s)
                    if s >= 3:
                        act.wait_ge(a_pv, s - 2)
                    SC.activation(PT[:, (s - 1) % 2, :], PS[:, 2:4, :].rearrange("p a b -> p (a b)")[:, 0:LA],
                                  ACT.Copy).then_inc(a_pt, 1)
                if s >= LAG and (s - LAG) % 8 == 0 and s > LAG:
                    ret_out((s - LAG) // 8 - 1)
                if s == 0:
                    exp_strip(0)
                elif s % 4 == 0 and s // 4 < 8:
                    exp_strip(s // 4)
                if s and s % 8 == 0:
                    att_out(s // 8 - 1)
                if s == 33:
                    act.wait_ge(mod_done, MOD_A + 2 * MODU - 16)
                    split_hi(act, "w_out", 0)
                    split_hi(act, "w_out", 1)
                    gn_log(0)
                    gn_log(1)
            ret_out(3)
            gn_log(2)
            for t in range(3):
                gn_root(t)
            for t in range(3):
                gn_high(t)
            gn_log(3)
            gn_root(3)
            gn_high(3)

            for n in range(8):
                act.wait_ge(w_done, ORD["w_out"] + n + 1)
                if n + 2 < 8:
                    split_hi(act, "w_out", n + 2)
                square(2 * KT + n, PS[:, n % 2, :])
                SC.activation(Ym[:, n, :], PS[:, n % 2, :], ACT.Copy).then_inc(n_y, 1)
            split_hi(act, "ffn_in", 0)
            root(2)
            for kt in range(KT):
                act.wait_ge(n_x, kt + 1)
                square(3 * KT + kt, X[:, kt, :])
            root(3)
            split_hi(act, "ffn_in", 1)
            for kt in range(KT):
                high(3, kt, H[:, 0, kt, :], mod_col(3, kt))

            def ffn_four(i, first, last):
                for u in range(4):
                    act.wait_ge(w_done, i * 4 + (ORD["ffn_in"] + u + 1))
                    if not (last and u >= 2):
                        split_hi(act, "ffn_in", u + 2, i)
                    else:
                        split_hi(act, "ffn_out", u - 2)
                    j = u // 2
                    if u % 2 == 0:
                        if not first or u == 2:
                            act.wait_ge(h_val, i * 2 + j)
                        SC.activation(sl[:, j, :], PS[:, u, :], ACT.Silu).then_inc(h_sl, 1)
                    else:
                        act.wait_ge(h_val, i * 2 + (j + 1))
                        SC.activation(hid[:, 0, i * 2 + j, :], hv[:, j, :], ACT.Copy).then_inc(h_hi, 1)
            ffn_four(0, True, False)
            with act.Fori(1, FT // 2 - 1) as i:
                ffn_four(i, False, False)
            ffn_four(FT // 2 - 1, False, True)


            def down_four(i, last):
                for u in range(4):
                    act.wait_ge(w_done, i * 4 + (ORD["ffn_out"] + u + 1))
                    if not (last and u >= 2):
                        split_hi(act, "ffn_out", u + 2, i)
                    j = u // 2
                    if u % 2:
                        act.wait_ge(n_acc, i * 2 + (4 * KT + j - 1))
                        SC.activation(sqb[:, j, :], PS[:, j, :], ACT.Square).then_inc(n_sq, 1)
                        SC.activation(Y[:, i * 2 + j, :], PS[:, j, :], ACT.Copy).then_inc(n_y, 1)
            act.wait_ge(h_lo, FT)
            with act.Fori(0, 3) as i:
                down_four(i, False)
            down_four(3, True)
            split_hi(act, "hy_in", 0)
            root(4)

            def squares(kts):
                for kt in kts:
                    act.wait_ge(n_x, KT + kt + 1)
                    square(5 * KT + kt, X[:, kt, :])

            def absolute(j):
                act.wait_ge(k_hp, j + 1)
                if j >= 2:
                    act.wait_ge(k_sum, j - 1)
                own(SC.activation(aab[:, j % 2, 0, :], fA[:, j % 2, :], ACT.Abs))
                SC.activation(aab[:, j % 2, 1, :], fB[:, j % 2, :], ACT.Abs).then_inc(k_abs, 1)

            squares(range(0, 2))
            absolute(0)
            squares(range(2, 5))
            absolute(1)
            squares(range(5, KT))
            root(5)
            absolute(2)
            absolute(3)
            split_hi(act, "hy_in", 1)
            for j in range(4, 8):
                absolute(j)
                for kt in (2 * j - 8, 2 * j - 7):
                    high(5, kt, H[:, 0, kt, :], mod2_col(0, kt))
            act.wait_ge(k_ab, 8)
            for k in range(4):
                act.wait_ge(k_f, k + 1)
                if k >= 2:
                    act.wait_ge(k_k, k - 1)
                own(SC.activation(kE[:, k % 2, 0, :], PS[:, 4 * (k % 2), :], ACT.Copy))
                SC.activation(kE[:, k % 2, 1, :], PS[:, 4 * (k % 2) + 1, :], ACT.Copy).then_inc(k_e, 1)

            act.wait_ge(y_c, 1)

            def hy_four(i, first, last):
                for u in range(4):
                    act.wait_ge(w_done, i * 4 + (ORD["hy_in"] + u + 1))
                    if not (last and u >= 2):
                        split_hi(act, "hy_in", u + 2, i)
                    if not first or u >= 2:
                        act.wait_ge(y_c, i * 4 + u)
                    SC.activation(cb_[:, u % 2, 1:L + 1], PS[:, u % 2, :], ACT.Identity,
                                  bias=colt[:, bass.ds(i * 4 + (COL["hy_b_in"] + u), 1)]).then_inc(y_b, 1)
            hy_four(0, True, False)
            with act.Fori(1, 5) as i:
                hy_four(i, False, False)
            hy_four(5, False, True)
            for g in range(8):
                par, mt, c = g // 4, g // 2 % 2, g % 2
                act.wait_ge(z_tr, g + 1)
                SC.activation(zN[:, par * 2 + mt, c * 512:(c + 1) * 512], PS[:, g % 4, :], ACT.Copy).then_inc(z_n, 1)
            act.wait_ge(y_c, 25)
            for k in range(4):
                act.wait_ge(z_f, k + 1)
                if k:
                    act.wait_ge(z_b, k)
                b = 4 * (k % 2)
                own(SC.activation(zE[:, 0, :], PS[:, b, :], ACT.Copy))
                SC.activation(zE[:, 1, :], PS[:, b + 1, :], ACT.Copy).then_inc(z_e, 1)

            def inv_high(j):
                act.wait_ge(i_val, j + 1)
                SC.activation(H[:, 0, j, :], yv[:, j % 2, :], ACT.Copy).then_inc(i_hi, 1)
            act.wait_ge(z_y, 4)
            for j in range(KT):
                act.wait_ge(i_mm, j + 1)
                if j >= 2:
                    act.wait_ge(i_val, j - 1)
                SC.activation(yt[:, j % 2, :].rearrange("p (m r) -> p r m", r=2),
                              PS[:, j, :].rearrange("p (r m) -> p r m", r=2), ACT.Copy,
                              scale=der("inv_norm", j)).then_inc(i_ev, 1)
                if j:
                    inv_high(j - 1)
            inv_high(KT - 1)

            split_hi(act, "hy_out", 0)
            split_hi(act, "hy_out", 1)
            for n in range(8):
                act.wait_ge(w_done, ORD["hy_out"] + n + 1)
                if n + 2 < 8:
                    split_hi(act, "hy_out", n + 2)
                if n >= 2:
                    act.wait_ge(n_x, 2 * KT + n - 1)
                SC.activation(hyt[:, n % 2, :], PS[:, n % 2, :], ACT.Identity, bias=der("p_hy", n),
                              scale=dert[:, DER["mod2"] + 2 * KT + n:DER["mod2"] + 2 * KT + n + 1]).then_inc(o_ev, 1)
                if n:
                    act.wait_ge(n_x, 2 * KT + n)
                    square(6 * KT + n - 1, X[:, n - 1, :])
            act.wait_ge(n_x, 3 * KT)
            square(7 * KT - 1, X[:, KT - 1, :])
            split_hi(act, "up", 0)
            root(6)
            split_hi(act, "up", 1)
            for kt in range(KT):
                high(6, kt, H[:, 0, kt, :], mod2_col(3, kt))

            act.wait_ge(h_cv, 1)

            def up_high(i, j):
                act.wait_ge(h_val, i * 2 + (FT + j + 1))
                SC.activation(hid[:, 0, i * 2 + j, :], hv[:, j % 2, :], ACT.Copy).then_inc(h_hi, 1)

            def up_four(i, first, last):
                for u in range(4):
                    act.wait_ge(w_done, i * 4 + (ORD["up"] + u + 1))
                    if not (last and u >= 2):
                        split_hi(act, "up", u + 2, i)
                    else:
                        split_hi(act, "down", u - 2)
                    j = u // 2
                    if u % 2 == 0:
                        if not (first and u == 0):
                            act.wait_ge(h_cv, i * 2 + j)
                        SC.activation(gb[:, j, 1:ROWS + 1, 1:GRID_W + 1],
                                      PS[:, u, :].rearrange("p (a b) -> p a b", b=GRID_W), ACT.Copy).then_inc(h_g, 1)
                        SC.activation(der("taps", 9 * j, 9), colt[:, bass.ds(i * 18 + (COL["conv_w"] + 9 * j), 9)],
                                      ACT.Copy).then_inc(h_tp, 1)
                        SC.activation(cva[:, j, :, :].rearrange("p a b -> p (a b)"), PS[:, u, :], ACT.Copy,
                                      scale=colt[:, bass.ds(i * 18 + (COL["conv_w"] + 9 * j + 4), 1)]).then_inc(h_ct, 1)
                        if not (first and u == 0):
                            up_high(i, j - 1)
                    else:
                        act.wait_ge(h_cv, i * 2 + (j + 2))
                        act.wait_ge(h_val, i * 2 + (FT + j - 1))
                        SC.activation(sl[:, j, :], cva[:, j, :, :].rearrange("p a b -> p (a b)"), ACT.Silu,
                                      bias=colt[:, bass.ds(i * 2 + (COL["conv_b"] + j), 1)]).then_inc(h_sl, 1)
            up_four(0, True, False)
            with act.Fori(1, FT // 2 - 1) as i:
                up_four(i, False, False)
            up_four(FT // 2 - 1, False, True)
            up_high(FT // 2 - 1, 1)

            act.wait_ge(h_lo, 2 * FT)

            def last_four(i, last):
                for u in range(4):
                    act.wait_ge(w_done, i * 4 + (ORD["down"] + u + 1))
                    if not (last and u >= 2):
                        split_hi(act, "down", u + 2, i)
                    j = u // 2
                    if u % 2:
                        act.wait_ge(n_x, i * 2 + (3 * KT + j + 1))
                        act.wait_ge(n_acc, i * 2 + (7 * KT + j - 1))
                        SC.activation(sqb[:, j, :], X[:, i * 2 + j, :], ACT.Square).then_inc(n_sq, 1)
            with act.Fori(0, 3) as i:
                last_four(i, False)
            last_four(3, True)
            root(7)

        @block.gpsimd
        def _(pool):
            own = Own(pool, s_pool)
            PL = nc.gpsimd

            def sums(k, n=L, kts=range(KT)):
                for kt in kts:
                    q = k * KT + kt
                    pool.wait_ge(n_sq, q + 1)
                    if kt == 0:
                        if k >= 2:
                            pool.wait_ge(n_ss, totals(k - 1))
                        PL.tensor_copy(acc_of(k), sqb[:, q % 2, 0:n]).then_inc(n_acc, 1)
                    else:
                        pool.wait_ge(n_acc, q)
                        PL.tensor_tensor(acc_of(k), acc_of(k), sqb[:, q % 2, 0:n], ALU.add).then_inc(n_acc, 1)

            def scaled(k, src, gain, n=L, kts=range(KT)):
                pool.wait_ge(n_rs, k + 1)
                for kt in [kt for kt in kts if kt % 4 == 3]:
                    t = k * KT + kt
                    wait_buffer(pool, t)
                    own(PL.tensor_tensor(tb[:, t % 4, 0:n], src[:, kt, 0:n], root_of(k), ALU.mult))
                    PL.tensor_scalar(tb[:, t % 4, 0:n], tb[:, t % 4, 0:n], der(gain, kt), None,
                                     ALU.mult).then_inc(n_t[1], 1)

            def mod_a_product(i):
                if i:
                    pool.wait_ge(a_sum[1], i)
                mod_a_multiply(pool, PL, 1, i, 1)
                pool.wait_ge(a_pr[1], i + 1)
                pm = aprod[:, 1, :]
                own(PL.tensor_tensor(pm[:, 0:512], pm[:, 0:512], pm[:, 512:1024], ALU.add))
                own(PL.tensor_tensor(pm[:, 0:256], pm[:, 0:256], pm[:, 256:512], ALU.add))
                PL.tensor_tensor(asum[:, 2 * i + 1, :], pm[:, 0:128], pm[:, 128:256], ALU.add).then_inc(a_sum[1], 1)

            pool.wait_ge(silu_c, 1)
            for i in range(3):
                mod_a_product(i)
            sums(0)
            sums(1, LC)
            pool.wait_ge(m_gain, 1)
            scaled(0, X, "a_mix")
            scaled(1, Xc, "a_ctx", LC)
            def abs_sum(j):
                c, t, ab = j // 4, j % 4, aab[:, j % 2, :, :]
                cs = slice(c * 512, (c + 1) * 512)
                pool.wait_ge(k_abs, j + 1)
                if t == 0:
                    PL.tensor_tensor(absum[:, cs], ab[:, 0, :], ab[:, 1, :], ALU.add).then_inc(k_sum, 1)
                else:
                    pool.wait_ge(k_sum, j)
                    own(PL.tensor_tensor(absum[:, cs], absum[:, cs], ab[:, 0, :], ALU.add))
                    PL.tensor_tensor(absum[:, cs], absum[:, cs], ab[:, 1, :], ALU.add).then_inc(k_sum, 1)

            def strip_sums(h):
                pool.wait_ge(r_e, h + 1)
                own(PL.tensor_tensor(strip[:, h % 2, 0:DIST], ea[:, :], distt[:, 2 * DIST:3 * DIST], ALU.add))
                PL.tensor_tensor(strip[:, h % 2, DIST:], strip[:, h % 2, DIST:], ec[:, :], ALU.add).then_inc(r_strip, 1)

            def mod_product(m):
                mod_multiply(pool, PL, m)
                pool.wait_ge(m_pr[1], (m - 17) // 2 + 1)
                pm = mprod[:, 1, :]
                own(PL.tensor_tensor(pm[:, 0:512], pm[:, 0:512], pm[:, 512:1024], ALU.add))
                own(PL.tensor_tensor(pm[:, 0:256], pm[:, 0:256], pm[:, 256:512], ALU.add))
                if m >= 24:
                    pool.wait_ge(mod_done, MOD_A + m - 23)
                PL.tensor_tensor(msum[:, m % 8, :], pm[:, 0:128], pm[:, 128:256], ALU.add).then_inc(m_sum[1], 1)
                pool.wait_ge(m_sum[1], (m - 17) // 2 + 1)

            pool.wait_ge(w_done, ORD["w_in"] + 22)
            for s in range(32):
                if s % 4 == 0:
                    strip_sums(s // 4)
                for m in mod_units(s)[1::2]:
                    mod_product(m)
            sums(2)
            pool.wait_ge(m_gain, 2)
            scaled(2, Ym, "p_mix")
            scaled(3, X, "a_ffn")
            sums(4)
            scaled(4, Y, "p_ffn")
            for j in range(4):
                abs_sum(j)
            scaled(5, X, "a_hy", L, range(0, 4))
            abs_sum(4)
            scaled(5, X, "a_hy", L, range(4, KT))
            for j in range(5, 8):
                abs_sum(j)
            for k in range(4):
                pool.wait_ge(z_b, k + 1)
                c, f, z0 = k // 2, k % 2, 4 * (k % 2)
                kk = KS[:, c, f, :, :]
                if k:
                    pool.wait_ge(z_w, k)
                for d in range(2):
                    PL.tensor_tensor(zpP[:, d, :], zs[:, z0 + 2 * d, :], kk[:, 2 * d + 1, :], ALU.mult)
                    last = PL.tensor_tensor(zpP[:, 2 + d, :], zs[:, z0 + 2 * d + 1, :], kk[:, 2 * d, :], ALU.mult)
                own(last)
                for d in range(2):
                    last = PL.tensor_tensor(zpP[:, d, :], zpP[:, d, :], zpP[:, 2 + d, :], ALU.add)
                last.then_inc(z_q, 1)
                pool.wait_ge(z_q, k + 1)
                pool.wait_ge(z_p, k + 1)
                PL.tensor_tensor(kk[:, 1, :], zpP[:, 0, :], zpP[:, 1, :], ALU.add)
                PL.tensor_tensor(kk[:, 3, :], zpP[:, 0, :], zpP[:, 1, :], ALU.subtract).then_inc(z_w, 1)
            sums(6)
            scaled(6, X, "a_ffn2")

            def up_two(i):
                for j in range(2):
                    pool.wait_ge(h_g, i * 2 + (j + 1))
                    pool.wait_ge(h_tp, i * 2 + (j + 1))
                    pool.wait_ge(h_cv, i * 2 + (j + 1))
                    for n, tap in enumerate(POOL_TAPS):
                        dy, dx = tap // 3, tap % 3
                        src = gb[:, j, dy:dy + ROWS, dx:dx + GRID_W]
                        wcol = der("taps", 9 * j + tap)
                        own(PL.tensor_tensor((cvt if n else cvb)[:, :, :], src,
                                             wcol.unsqueeze(2).to_broadcast([P, ROWS, GRID_W]), ALU.mult))
                        if n:
                            ins = PL.tensor_tensor(cvb[:, :, :], cvb[:, :, :], cvt[:, :, :], ALU.add)
                        if 0 < n < len(POOL_TAPS) - 1:
                            own(ins)
                    ins.then_inc(h_cp, 1)
            with pool.Fori(0, FT // 2) as i:
                own.enter(i, 4 * (len(POOL_TAPS) - 1))
                up_two(i)
            own.leave(FT // 2)
            sums(7)
            pool.wait_ge(n_rs, 8)
            for kt in (3, 7):
                own(PL.tensor_tensor(Y[:, kt, :], X[:, kt, :], rstd[:, :], ALU.mult))
                PL.tensor_scalar(Y[:, kt, :], Y[:, kt, :], col("g_final", kt), None, ALU.mult).then_inc(n_fin[1], 1)

        @block.vector
        def _(dve):
            own = Own(dve, s_dve)
            VE = nc.vector

            def stt(o, a, s, b, op0=ALU.mult, op1=ALU.add):
                return VE.scalar_tensor_tensor(out=o, in0=a, scalar=s, in1=b, op0=op0, op1=op1)

            def scaled(k, src, gain, kts, n=L):
                for kt in kts:
                    if kt == 0:
                        dve.wait_ge(n_rs, k + 1)
                    if kt < KT and kt % 4 < 3:
                        wait_buffer(dve, k * KT + kt)
                        stt(tb[:, kt % 4, 0:n], src[:, kt, 0:n], der(gain, kt), root_of(k), ALU.mult,
                            ALU.mult).then_inc(n_t[0], 1)

            def low(k, c, kt, h, shift, n=L):
                dve.wait_ge(n_hi, c + 1)
                stt(h[:, 1, kt, :], tb[:, kt % 4, 0:n], shift, h[:, 0, kt, :].bitcast(F32), ALU.add,
                    ALU.subtract).then_inc(n_h, 1)

            def lows(k, c0, h, shift, src, gain, kts=range(KT), n=L):
                for kt in kts:
                    low(k, c0 + kt, kt, h, shift(kt), n)
                    if kt:
                        scaled(k, src, gain, [kt + 3], n)

            def residuals(k, src, gain, kts=range(KT)):
                for kt in kts:
                    wait_tile(dve, k, kt)
                    VE.tensor_tensor(X[:, kt, :], X[:, kt, :], tb[:, kt % 4, :], ALU.add).then_inc(n_x, 1)
                    if kt:
                        scaled(k, src, gain, [kt + 3])

            own(VE.memset(der("one"), 1.0))
            count = [0]

            def mod_a_product(i, which):
                if count[0]:
                    dve.wait_ge(a_sum[0], count[0])
                count[0] += 1
                mod_a_multiply(dve, VE, 0, i, which)
                dve.wait_ge(a_pr[0], count[0])
                VE.tensor_reduce(asum[:, 2 * i + which, :], aprod[:, 0, :].rearrange("p (k n) -> p n k", n=P),
                                 mybir.AxisListType.X, ALU.add).then_inc(a_sum[0], 1)

            dve.wait_ge(s_small, 80)
            dve.wait_ge(silu_c, 1)
            for l in range(3):
                mod_a_product(l, 0)
                dve.wait_ge(f_mm, l + 1)
                if l:
                    dve.wait_ge(f_sin, l)
                b = ("fb1", "fb2", "fb3")[l]
                own(VE.tensor_scalar(fa[:, :], PS[0:HYF, 6, :], colt[0:HYF, COL[b]:COL[b] + 1],
                                     colt[0:HYF, COL["freq"]:COL["freq"] + 1], ALU.add, ALU.mult))
                own(VE.tensor_scalar(fk[:, :], fa[:, :], float(1 / TWO_PI), MAGIC, ALU.mult, ALU.add))
                own(VE.tensor_scalar(fk[:, :], fk[:, :], MAGIC, None, ALU.subtract))
                for part in (PI_A, PI_B, PI_C):
                    own(stt(fa[:, :], fk[:, :], -part, fa[:, :]))
                VE.tensor_scalar(fa[:, :], fa[:, :], PI_SAFE, -PI_SAFE, ALU.min, ALU.max).then_inc(f_arg, 1)

            for i in range(3, len(OFF_PE)):
                for which in range(2):
                    mod_a_product(i, which)
            own(VE.tensor_tensor(centre[:, :], ident[:, :], bones[:, :], ALU.subtract))
            dve.wait_ge(m_lg, 2)
            for name in ("lg_f", "lg_b"):
                own(VE.tensor_scalar(der(name, 0, 8), der(name, 0, 8), -1.0, None, ALU.mult))

            def mod_pair(chunk, which):
                a = DER["mod"] + 2 * KT * chunk + which
                return dert[:, a:a + 2 * KT - 1:2]

            def mod_col(chunk, kt, which=0):
                a = DER["mod"] + 2 * (KT * chunk + kt) + which
                return dert[:, a:a + 1]

            def mod2_col(chunk, kt):
                return der("mod2", KT * chunk + kt)

            dve.wait_ge(mod_done, MOD_A)
            VE.tensor_tensor(der("mod", 0, 32), PS[:, 7, 0:32], col("b_mod", 0, 32), ALU.add).then_inc(m_cols, 1)
            dve.wait_ge(m_cols, 1)
            own(stt(der("a_mix", 0, KT), mod_pair(1, 0), 1.0, col("g_pre_mix", 0, KT), ALU.add, ALU.mult))
            stt(der("a_ctx", 0, KT), mod_pair(1, 1), 1.0, col("g_pre_mix", 0, KT), ALU.add,
                ALU.mult).then_inc(m_gain, 1)
            dve.wait_ge(m_gain, 1)
            scaled(0, X, "a_mix", (0, 1, 2))
            split_lo(dve, "w_in", 0)
            lows(0, 0, H, lambda kt: mod_col(0, kt), X, "a_mix")
            scaled(1, Xc, "a_ctx", (0, 1, 2), LC)
            split_lo(dve, "w_in", 1)
            lows(1, KT, Hc, lambda kt: mod_col(0, kt, 1), Xc, "a_ctx", n=LC)

            dve.wait_ge(s_rope, 16)
            for n in range(22):
                if n + 2 < 22:
                    split_lo(dve, "w_in", n + 2)
                m = n - 1
                if 0 <= m < NV:
                    dve.wait_ge(v_tr, m + 1)
                    VE.tensor_copy(V[:, :, m * P:(m + 1) * P],
                                   PS[:, 6:8, :].rearrange("p a b -> p (a b)")[:, 0:LA].rearrange(
                                       "p (t d) -> p t d", d=P)).then_inc(v_ev, 1)
                elif NV <= m < NV + NROPE:
                    normed_q = m == NV or 10 <= m < 14
                    dst = (KA[:, 0:L] if m == NV else KR[:, m - 6, 0:L] if m < 10 else QA[:, m - 10, :] if m < 14
                           else QR[:, m - 14, :])
                    dve.wait_ge(q_sw, m - NV + 1)
                    if m > NV:
                        dve.wait_ge(q_done, m - NV)
                    VE.tensor_tensor(RM[:, :], RU[:, m % 2, 0:L], ropet[:, 0, :], ALU.mult)
                    own(VE.tensor_tensor(dst, PS[:, 4, :], ropet[:, 1, :], ALU.mult))
                    if not normed_q:
                        VE.tensor_tensor(dst, dst, RM[:, :], ALU.add).then_inc(q_done, 1)
                        continue
                    own(VE.tensor_tensor(dst, dst, RM[:, :], ALU.add))
                    dve.wait_ge(q_rt, 1 if m == NV else m - 8)
                    w_ = LA if m == NV else L
                    own(VE.reciprocal(RT[:, 0:w_], RT[:, 0:w_]))
                    if m == NV:
                        own(VE.tensor_tensor(KA[:, L:LA], RU[:, m % 2, L:LA], RT[:, L:LA], ALU.mult))
                    VE.tensor_tensor(dst, dst, RT[:, 0:L], ALU.mult).then_inc(q_done, 1)

            def decay_arg(h):
                if h:
                    dve.wait_ge(r_strip, h)
                own(VE.tensor_scalar(ea[:, :], distt[:, DIST:2 * DIST], der("lg_b", h), None, ALU.mult))
                stt(ea[:, :], distt[:, 0:DIST], der("lg_f", h), ea[:, :]).then_inc(r_u, 1)

            def ret_decay(r):
                h, kt = r // 6, r % 6
                a = L - P - P * kt if kt < 4 else DIST + P * (5 - kt)
                dve.wait_ge(r_s, r + 1)
                dve.wait_ge(r_strip, h + 1)
                if r >= 2:
                    dve.wait_ge(r_pv, r - 1)
                VE.tensor_tensor(pr[:, r % 2, :], PS[:, 5, :], strip[:, h % 2, a:a + L], ALU.mult).then_inc(r_p, 1)

            def mod_product(m):
                mod_multiply(dve, VE, m)

            def mod_sum(m):
                dve.wait_ge(m_pr[0], (m - 16) // 2 + 1)
                if m >= 24:
                    dve.wait_ge(mod_done, MOD_A + m - 23)
                VE.tensor_reduce(msum[:, m % 8, :], mprod[:, 0, :].rearrange("p (k n) -> p n k", n=P),
                                 mybir.AxisListType.X, ALU.add).then_inc(m_sum[0], 1)
                dve.wait_ge(m_sum[0], (m - 16) // 2 + 1)

            def gn_gate(t):
                dve.wait_ge(r_o, t + 1)
                VE.tensor_tensor(G[:, t, :], G[:, t, :], QR[:, t, :], ALU.mult).then_inc(g_gate, 1)

            def gn_scale(t):
                dve.wait_ge(g_gate, t + 1)
                dve.wait_ge(g_rs, t + 1)
                VE.tensor_tensor(G[:, t, :], G[:, t, :], gsq[:, t, :], ALU.mult).then_inc(g_val, 1)

            def gn_low(t):
                dve.wait_ge(g_hi, t + 1)
                VE.tensor_tensor(H[:, 1, 4 + t, :], G[:, t, :], H[:, 0, 4 + t, :].bitcast(F32),
                                 ALU.subtract).then_inc(g_h, 1)

            for s in range(STEPS):
                rs = ret_steps(s)
                ms = list(mod_units(s))[::2]
                if rs:
                    ret_decay(rs[0])
                if s < 32:
                    dve.wait_ge(a_s, s + 1)
                    own(VE.tensor_reduce(mxr[:, s % 2:s % 2 + 1],
                                         PS[:, 0:2, :].rearrange("p a b -> p (a b)")[:, 0:LA],
                                         mybir.AxisListType.X, ALU.max))
                    if s >= 2:
                        dve.wait_ge(a_exp, s - 1)
                    VE.tensor_scalar(smx[:, s % 2:s % 2 + 1], mxr[:, s % 2:s % 2 + 1], -HD**-0.5, None,
                                     ALU.mult).then_inc(a_mx, 1)
                if s == 0:
                    dve.wait_ge(s_dist, 16)
                    decay_arg(0)
                    dve.wait_ge(w_done, ORD["w_in"] + 22)
                if ms:
                    mod_product(ms[0])
                if len(rs) == 2:
                    ret_decay(rs[1])
                if s < 32:
                    dve.wait_ge(a_exp, s + 1)
                    own(VE.reciprocal(rinv[:, s % 2:s % 2 + 1], rsum[:, s % 2:s % 2 + 1]))
                    VE.tensor_scalar(Pb[:, s % 2, :], Pb[:, s % 2, :], rinv[:, s % 2:s % 2 + 1], None,
                                     ALU.mult).then_inc(a_p, 1)
                if ms:
                    mod_sum(ms[0])
                for m in ms[1:]:
                    mod_product(m)
                    mod_sum(m)
                if s % 4 == 2 and s // 4 < 7:
                    decay_arg(s // 4 + 1)
                if s and s % 8 == 0:
                    dve.wait_ge(a_hi, s // 8)
                    VE.tensor_tensor(H[:, 1, s // 8 - 1, :], PS[:, 4, :], H[:, 0, s // 8 - 1, :].bitcast(F32),
                                     ALU.subtract).then_inc(a_o, 1)
                if s > LAG and (s - LAG) % 8 == 0:
                    gn_gate((s - LAG) // 8 - 1)

            split_lo(dve, "w_out", 0)
            split_lo(dve, "w_out", 1)
            gn_gate(3)
            for t in range(3):
                gn_scale(t)
            for t in range(3):
                gn_low(t)
            gn_scale(3)
            gn_low(3)
            dve.wait_ge(mod_done, MOD_A + 2 * MODU - 16)
            own(VE.tensor_tensor(dert[:, DER["mod"] + 32:DER["mod"] + 95:2], PS[:, 7, 32:95:2],
                                 colt[:, COL["b_mod"] + 32:COL["b_mod"] + 95:2], ALU.add))
            own(VE.tensor_tensor(der("mod2", 0, MODU), PS[:, 7, 96:96 + MODU], col("b_mod2", 0, MODU), ALU.add))
            own(VE.tensor_tensor(der("p_mix", 0, KT), mod_pair(2, 0), col("g_post_mix", 0, KT), ALU.mult))
            own(stt(der("a_ffn", 0, KT), mod_pair(4, 0), 1.0, col("g_pre_ffn", 0, KT), ALU.add, ALU.mult))
            own(VE.tensor_tensor(der("p_ffn", 0, KT), mod_pair(5, 0), col("g_post_ffn", 0, KT), ALU.mult))
            own(stt(der("a_hy", 0, KT), der("mod2", KT, KT), 1.0, col("g_hy", 0, KT), ALU.add, ALU.mult))
            own(VE.tensor_tensor(der("p_hy", 0, KT), der("mod2", 2 * KT, KT), col("hy_b_out", 0, KT), ALU.mult))
            stt(der("a_ffn2", 0, KT), der("mod2", 4 * KT, KT), 1.0, col("g_ffn2", 0, KT), ALU.add,
                ALU.mult).then_inc(m_gain, 1)
            for n in range(2, 8):
                split_lo(dve, "w_out", n)
            split_lo(dve, "ffn_in", 0)
            scaled(2, Ym, "p_mix", (0, 1, 2))
            residuals(2, Ym, "p_mix")
            scaled(3, X, "a_ffn", (0, 1, 2))
            lows(3, 2 * KT, H, lambda kt: mod_col(3, kt), X, "a_ffn", range(0, 5))
            split_lo(dve, "ffn_in", 1)
            lows(3, 2 * KT, H, lambda kt: mod_col(3, kt), X, "a_ffn", range(5, KT))

            def ffn_four(i, first, last):
                for u in range(4):
                    if not (last and u >= 2):
                        split_lo(dve, "ffn_in", u + 2, i)
                    else:
                        split_lo(dve, "ffn_out", u - 2)
                    j = u // 2
                    if u % 2:
                        dve.wait_ge(w_done, i * 4 + (ORD["ffn_in"] + u + 1))
                        dve.wait_ge(h_sl, i * 2 + (j + 1))
                        if not first or u == 3:
                            dve.wait_ge(h_lo, i * 2 + j)
                        VE.tensor_tensor(hv[:, j, :], PS[:, u, :], sl[:, j, :], ALU.mult).then_inc(h_val, 1)
                        dve.wait_ge(h_hi, i * 2 + (j + 1))
                        VE.tensor_tensor(hid[:, 1, i * 2 + j, :], hv[:, j, :], hid[:, 0, i * 2 + j, :].bitcast(F32),
                                         ALU.subtract).then_inc(h_lo, 1)
            ffn_four(0, True, False)
            with dve.Fori(1, FT // 2 - 1) as i:
                ffn_four(i, False, False)
            ffn_four(FT // 2 - 1, False, True)
            with dve.Fori(0, 3) as i:
                for u in range(4):
                    split_lo(dve, "ffn_out", u + 2, i)
            for n in range(14, 16):
                split_lo(dve, "ffn_out", n)

            def filters(j):
                c, t = j // 4, j % 4
                cs = slice(c * 512, (c + 1) * 512)
                dve.wait_ge(s_dec[t], 16 * (c + 1))
                dve.wait_ge(k_h, j + 1)
                if j >= 2:
                    dve.wait_ge(k_hp, j - 1)
                    dve.wait_ge(k_abs, j - 1)
                VE.tensor_tensor(fA[:, j % 2, :], PS[:, 4, :], dect[:, t, :], ALU.mult)
                VE.tensor_tensor(fB[:, j % 2, :], PS[:, 5, :], dect[:, t, :], ALU.mult).then_inc(k_ab, 1)
                dve.wait_ge(k_ab, j + 1)
                if t == 0:
                    own(VE.memset(fB[0:1, j % 2, :], 0.0))
                VE.tensor_tensor(HP[:, t, cs], fA[:, j % 2, :], fB[:, j % 2, :], ALU.add)
                VE.tensor_tensor(HM[:, t, cs], fA[:, j % 2, :], fB[:, j % 2, :], ALU.subtract).then_inc(k_hp, 1)

            def lows_5(kts):
                lows(5, 3 * KT, H, lambda kt: mod2_col(0, kt), X, "a_hy", kts)

            split_lo(dve, "hy_in", 0)
            filters(0)
            scaled(4, Y, "p_ffn", (0, 1, 2))
            for j, kts in ((1, range(0, 2)), (2, range(2, 5)), (3, range(5, KT))):
                residuals(4, Y, "p_ffn", kts)
                filters(j)
            filters(4)
            split_lo(dve, "hy_in", 1)
            scaled(5, X, "a_hy", (0, 1, 2))
            filters(5)
            lows_5(range(0, 2))
            filters(6)
            lows_5(range(2, 4))
            filters(7)
            lows_5(range(4, KT))
            for k in range(4):
                c, f, b = k // 2, k % 2, 4 * (k % 2) + 2
                dve.wait_ge(k_e, k + 1)
                if k == 2:
                    dve.wait_ge(k_sum, 8)
                ke = kE[:, k % 2, :, :]
                for part in range(2):
                    VE.tensor_tensor(KS[:, c, f, part, :], ke[:, part, :], PS[:, b + part, :], ALU.add)
                VE.tensor_tensor(KS[:, c, f, 2, :], ke[:, 0, :], PS[:, b, :], ALU.subtract)
                VE.tensor_tensor(KS[:, c, f, 3, :], ke[:, 1, :], PS[:, b + 1, :], ALU.subtract).then_inc(k_k, 1)
            dve.wait_ge(k_col, 1)
            VE.reciprocal(der("inv_norm", 0, KT), PS[:, 0, 0:KT]).then_inc(k_inv, 1)

            dve.wait_ge(n_h, 4 * KT)
            VE.memset(cb_[:, :, 0:L + 2:L + 1], 0.0).then_inc(y_c, 1)

            def hy_four(i, gated, last):
                for u in range(4):
                    if not (last and u >= 2):
                        split_lo(dve, "hy_in", u + 2, i)
                    dve.wait_ge(y_b, i * 4 + (u + 1))
                    j = u // 2

                    def hcol(name, per, tap):
                        return colt[:, bass.ds(i * (4 * per) + (COL[name] + per * u + tap), 1)]
                    if gated:
                        dst = x1c[:, :] if u % 2 == 0 else ca[:, 1, :]
                    else:
                        dst = X0[:, i * 4 + (u - 16), :]
                    own(VE.tensor_scalar(ca[:, 0, :], cb_[:, u % 2, 1:L + 1], hcol("hy_sc_w", 3, 1),
                                         hcol("hy_sc_b", 1, 0), ALU.mult, ALU.add))
                    own(stt(ca[:, 0, :], cb_[:, u % 2, 0:L], hcol("hy_sc_w", 3, 0), ca[:, 0, :]))
                    stt(dst, cb_[:, u % 2, 2:L + 2], hcol("hy_sc_w", 3, 2), ca[:, 0, :]).then_inc(y_c, 1)
                    dve.wait_ge(y_c, i * 4 + (u + 2))
                    if gated and u % 2:
                        VE.tensor_tensor(Z[:, i * 2 + j, :], x1c[:, :], ca[:, 1, :], ALU.mult).then_inc(y_z, 1)
                        dve.wait_ge(y_z, i * 2 + (j + 1))
            with dve.Fori(0, 4) as i:
                own.enter(i, 8)
                hy_four(i, True, False)
            own.leave(4)
            hy_four(4, False, False)
            hy_four(5, False, True)

            def spectra_sums(k):
                z0, b = 4 * (k % 2), 4 * (k % 2)
                dve.wait_ge(z_e, k + 1)
                if k >= 2:
                    dve.wait_ge(z_q, k - 1)
                for part in range(2):
                    VE.tensor_tensor(zs[:, z0 + part, :], zE[:, part, :], PS[:, b + 2 + part, :], ALU.add)
                VE.tensor_tensor(zs[:, z0 + 2, :], zE[:, 0, :], PS[:, b + 2, :], ALU.subtract)
                VE.tensor_tensor(zs[:, z0 + 3, :], zE[:, 1, :], PS[:, b + 3, :], ALU.subtract).then_inc(z_b, 1)

            def spectra_products(k):
                c, f, z0 = k // 2, k % 2, 4 * (k % 2)
                kk = KS[:, c, f, :, :]
                dve.wait_ge(z_b, k + 1)
                for d in range(2):
                    VE.tensor_tensor(zpD[:, d, :], zs[:, z0 + 2 * d, :], kk[:, 2 * d, :], ALU.mult)
                    last = stt(zpD[:, 2 + d, :], zs[:, z0 + 2 * d + 1, :], 1.0 if f else col("not_first"),
                               kk[:, 2 * d + 1, :], ALU.mult, ALU.mult)
                own(last)
                for d in range(2):
                    last = VE.tensor_tensor(zpD[:, d, :], zpD[:, d, :], zpD[:, 2 + d, :], ALU.subtract)
                if f == 0:
                    own(last)
                if f == 0:
                    S, W, S_, W_ = zs[0:1, z0 + 1, :], zs[0:1, z0 + 3, :], kk[0:1, 1, :], kk[0:1, 3, :]
                    VE.tensor_tensor(row[:, 0, :], S, W_, ALU.mult)
                    own(VE.tensor_tensor(row[:, 1, :], W, S_, ALU.mult))
                    own(VE.tensor_tensor(row[:, 0, :], row[:, 0, :], row[:, 1, :], ALU.add))
                    own(VE.tensor_tensor(row[:, 1, :], S, S_, ALU.mult))
                    own(VE.tensor_tensor(zpD[0:1, 2, :], W, W_, ALU.mult))
                    last = VE.tensor_tensor(row[:, 1, :], row[:, 1, :], zpD[0:1, 2, :], ALU.subtract)
                last.then_inc(z_p, 1)

            def spectra_final(k):
                f = k % 2
                kk = KS[:, k // 2, f, :, :]
                dve.wait_ge(z_p, k + 1)
                dve.wait_ge(z_q, k + 1)
                VE.tensor_tensor(kk[:, 0, :], zpD[:, 0, :], zpD[:, 1, :], ALU.add)
                last = VE.tensor_tensor(kk[:, 2, :], zpD[:, 0, :], zpD[:, 1, :], ALU.subtract)
                if f == 0:
                    own(last)
                    dve.wait_ge(z_w, k + 1)
                    own(VE.tensor_copy(kk[0:1, 1, :], row[:, 0, :]))
                    last = VE.tensor_copy(kk[0:1, 3, :], row[:, 1, :])
                else:
                    own(last)
                    dve.wait_ge(z_w, k + 1)
                    last = VE.tensor_copy(row[:, 0, 0:1], row[:, 1, 0:1])
                last.then_inc(z_y, 1)
                dve.wait_ge(z_y, k + 1)

            spectra_sums(0)
            for k in range(4):
                spectra_products(k)
                if k < 3:
                    spectra_sums(k + 1)
                spectra_final(k)

            def inv_low(j):
                dve.wait_ge(i_hi, j + 1)
                VE.tensor_tensor(H[:, 1, j, :], yv[:, j % 2, :], H[:, 0, j, :].bitcast(F32),
                                 ALU.subtract).then_inc(i_h, 1)
            for j in range(KT):
                dve.wait_ge(i_ev, j + 1)
                own(stt(yt[:, j % 2, :], Z[:, j, :], col("hy_bias", j), yt[:, j % 2, :]))
                if j >= 2:
                    dve.wait_ge(i_h, j - 1)
                VE.tensor_tensor(yv[:, j % 2, :], yt[:, j % 2, :], X0[:, j, :], ALU.mult).then_inc(i_val, 1)
                if j:
                    inv_low(j - 1)
            inv_low(KT - 1)

            split_lo(dve, "hy_out", 0)
            split_lo(dve, "hy_out", 1)
            for n in range(8):
                if n + 2 < 8:
                    split_lo(dve, "hy_out", n + 2)
                dve.wait_ge(o_ev, n + 1)
                VE.tensor_tensor(X[:, n, :], X[:, n, :], hyt[:, n % 2, :], ALU.add).then_inc(n_x, 1)
            split_lo(dve, "up", 0)
            scaled(6, X, "a_ffn2", (0, 1, 2))
            lows(6, 4 * KT, H, lambda kt: mod2_col(3, kt), X, "a_ffn2", range(0, 5))
            split_lo(dve, "up", 1)
            lows(6, 4 * KT, H, lambda kt: mod2_col(3, kt), X, "a_ffn2", range(5, KT))

            dve.wait_ge(n_h, 5 * KT)
            VE.memset(gb[:, :, :, :], 0.0).then_inc(h_cv, 1)

            def up_low(i, j):
                dve.wait_ge(h_hi, i * 2 + (FT + j + 1))
                VE.tensor_tensor(hid[:, 1, i * 2 + j, :], hv[:, j % 2, :], hid[:, 0, i * 2 + j, :].bitcast(F32),
                                 ALU.subtract).then_inc(h_lo, 1)

            def up_four(i, first, last):
                for u in range(4):
                    if not (last and u >= 2):
                        split_lo(dve, "up", u + 2, i)
                    else:
                        split_lo(dve, "down", u - 2)
                    j = u // 2
                    if u % 2 == 0:
                        dve.wait_ge(h_g, i * 2 + (j + 1))
                        dve.wait_ge(h_tp, i * 2 + (j + 1))
                        dve.wait_ge(h_ct, i * 2 + (j + 1))
                        for tap in DVE_TAPS:
                            dy, dx = tap // 3, tap % 3
                            own(stt(cva[:, j, :, :], gb[:, j, dy:dy + ROWS, dx:dx + GRID_W],
                                    der("taps", 9 * j + tap), cva[:, j, :, :]))
                        if not (first and u == 0):
                            up_low(i, j - 1)
                    else:
                        dve.wait_ge(h_cp, i * 2 + (j + 1))
                        VE.tensor_tensor(cva[:, j, :, :], cva[:, j, :, :], cvb[:, :, :], ALU.add).then_inc(h_cv, 1)
                        dve.wait_ge(w_done, i * 4 + (ORD["up"] + u + 1))
                        dve.wait_ge(h_sl, i * 2 + (FT + j + 1))
                        dve.wait_ge(h_lo, i * 2 + (FT + j - 1))
                        VE.tensor_tensor(hv[:, j, :], PS[:, u, :], sl[:, j, :], ALU.mult).then_inc(h_val, 1)
            own.enter(0, 2 * len(DVE_TAPS))
            up_four(0, True, False)
            with dve.Fori(1, FT // 2 - 1) as i:
                own.repeat(i)
                up_four(i, False, False)
            own.leave(FT // 2 - 1)
            up_four(FT // 2 - 1, False, True)
            up_low(FT // 2 - 1, 1)


            def last_four(i, last):
                for u in range(4):
                    if not (last and u >= 2):
                        split_lo(dve, "down", u + 2, i)
                    j = u // 2
                    if u % 2:
                        dve.wait_ge(w_done, i * 4 + (ORD["down"] + u + 1))
                        stt(X[:, i * 2 + j, :], PS[:, j, :],
                            dert[:, bass.ds(i * 2 + (DER["mod2"] + 5 * KT + j), 1)],
                            X[:, i * 2 + j, :]).then_inc(n_x, 1)
            with dve.Fori(0, 3) as i:
                last_four(i, False)
            last_four(3, True)
            dve.wait_ge(n_rs, 8)
            for kt in (0, 1, 2, 4, 5, 6):
                stt(Y[:, kt, :], X[:, kt, :], col("g_final", kt), rstd[:, :], ALU.mult, ALU.mult).then_inc(n_fin[0], 1)
def tables():
    f32 = np.float32
    m = np.zeros((4, P, P), f32)
    m[0] = 1.0 / D
    i = np.arange(P)
    m[1] = (i[:, None] // HD == i[None, :] // HD) / f32(HD)
    m[2] = i[:, None] == (i[None, :] // HD) * HD + (i[None, :] + HALF) % HD
    m[3] = np.eye(P)
    n_freq = HD // 4
    inv_freq = (f32(10000.0) ** (-np.arange(n_freq, dtype=f32) / f32(n_freq))).astype(f32)
    tok = np.arange(L)
    ang = np.concatenate([(tok // GRID_W).astype(f32)[:, None] * inv_freq, (tok % GRID_W).astype(f32)[:, None] * inv_freq],
                         axis=1).T
    ang = np.tile(ang, (4, 1))
    sign = np.where(i % HD < HALF, -1.0, 1.0).astype(f32)[:, None]
    rope = np.stack([np.cos(ang), np.sin(ang) * sign], 1).astype(f32)
    f, p = np.arange(DIST)[None, :], i[:, None]
    d = f - (L - P) - p
    fc = np.arange(CDIST)[None, :]
    dist = np.concatenate([np.maximum(d, 0), np.maximum(-d, 0), d == 0, fc + P - p, L + P - fc + p], 1).astype(f32)
    t = np.linspace(0.0, 1.0, L, dtype=f32)[:, None]
    w = (f32(TWO_PI) * np.arange(L, dtype=f32)[:, None] / f32(L)).astype(f32)
    bands = np.linspace(1e-4, BANDS - 1, BANDS, dtype=f32)[None, :]
    pos = np.ascontiguousarray(np.concatenate([t, np.cos(bands * w), -np.sin(bands * w)], 1).T.astype(f32))
    deltas = np.linspace(np.log(1e-2) / 1.5, np.log(1e-2) / 0.3, D, dtype=f32)
    dec = np.exp(-t * np.abs(deltas)).astype(f32)
    tokens = [np.arange(256 * mt, 256 * mt + 256)[par::2] for par in range(2) for mt in range(2)]
    decay = np.stack([dec[x] for x in tokens]).reshape(4, P, 2, D // 2).transpose(2, 0, 1, 3)
    decay = np.ascontiguousarray(decay)
    freq, mm = np.arange(256), np.arange(256)
    fwd, inv = np.zeros((P, 4, 2, 256)), np.zeros((P, 4, 2, 256))
    for a in range(4):
        th = TWO_PI * np.outer(2 * mm + a // 2, freq) / (2 * L)
        fm = np.cos(th) if a % 2 == 0 else np.sin(th)
        im = 2.0 * fm
        if a % 2 == 0:
            im[:, 0] = 1.0
        else:
            fm[:, 0] = im[:, 0] = (-1.0) ** mm
        fwd[:, a] = fm.reshape(2, P, 256).transpose(1, 0, 2)
        inv[:, a] = im.T.reshape(2, P, 256).transpose(1, 0, 2) / (2 * L) / D
    return dict(mats=m, rope=rope, dist=dist, posT=pos, decay=decay, fwd=fwd.astype(f32), inv=inv.astype(f32))


def columns(v):
    return v.reshape(-1, P).T


def units(w_, order=None):
    k, n = w_.shape
    u = w_.reshape(k // P, P, n // P, P).transpose(2, 1, 0, 3)
    if order is not None:
        u = u[order]
    return np.ascontiguousarray(u.reshape(len(u), P, k))


def half_units(w_):
    u = units(w_)
    return np.ascontiguousarray(u.reshape(-1, P, 2, U2).transpose(0, 2, 1, 3).reshape(-1, P, U2))


def kernel(**a):
    import concourse.bacc as bacc
    from concourse.bass_utils import run_bass_kernel_spmd

    a = {k: np.asarray(v) for k, v in a.items()}
    heads = np.concatenate([np.arange(HD) + HD * h for t in range(4) for h in (t, 4 + t)])
    w_in = a["w_in"][0]
    w_in = np.concatenate([w_in[:, heads], w_in[:, 512:]], 1)
    w_out = a["w_out"][0]
    w_out = np.concatenate([w_out[heads], w_out[512:]], 0)
    qa, ka, va, qr, kr, vr, gr = 0, 4, 5, 6, 10, 14, 18
    order = [va] + [vr + i for i in range(4)] + [ka] + [kr + i for i in range(4)] + [qa + i for i in range(4)] + \
            [qr + i for i in range(4)] + [gr + i for i in range(4)]
    pair_order = [x for j in range(FT) for x in (j, FT + j)]
    gate_first = [x for j in range(FT) for x in (FT + j, j)]
    hy_order = [x for j in range(KT) for x in (KT + j, 2 * KT + j)] + list(range(KT))
    mod1 = units(a["w_mod"][0])
    weights = dict(
        mod_a=mod1[:16], mod_b=np.concatenate([mod1[16:], units(a["mod_w_2"][0])]), w_in=units(w_in, order),
        w_out=units(w_out), ffn_in=units(a["w_ffn_in"][0], pair_order), ffn_out=half_units(a["w_ffn_out"][0]),
        hy_in=units(a["hy_w_in_2"][0], hy_order), hy_out=units(a["hy_w_out_2"][0]),
        up=units(a["ffn_w_up_2"][0], gate_first), down=half_units(a["ffn_w_down_2"][0]))

    def rep(v):
        return np.broadcast_to(v.reshape(1, -1), (P, v.size))

    def two(v):
        return np.concatenate([v, v]).reshape(P, 1)
    sc_w = a["hy_sc_w_2"][0].reshape(3, 3 * KT, P)[:, hy_order]
    parts = dict(
        g_pre_mix=columns(a["g_pre_mix"][0]), g_post_mix=columns(a["g_post_mix"][0]),
        g_pre_ffn=columns(a["g_pre_ffn"][0]), g_post_ffn=columns(a["g_post_ffn"][0]),
        b_mod=np.repeat(columns(a["b_mod"][0]), 2, 1), b_mod2=columns(a["mod_b_2"][0]),
        g_hy=columns(a["norm_g_2"][0, 0]), g_ffn2=columns(a["norm_g_2"][0, 1]), g_final=columns(a["final_g_2"]),
        hy_b_in=columns(a["hy_b_in_2"][0])[:, hy_order], hy_sc_w=sc_w.transpose(2, 1, 0).reshape(P, -1),
        hy_sc_b=columns(a["hy_sc_b_2"][0])[:, hy_order], hy_bias=columns(a["hy_bias_2"][0]),
        hy_b_out=columns(a["hy_b_out_2"][0]),
        conv_w=a["ffn_conv_w_2"][0].reshape(9, FT, P).transpose(2, 1, 0).reshape(P, -1),
        conv_b=columns(a["ffn_conv_b_2"][0]), q_g=two(a["q_norm_g"][0]), k_g=two(a["k_norm_g"][0]),
        dec_f=rep(a["ret_decay_fwd"][0]), dec_b=rep(a["ret_decay_bwd"][0]), freq=two(a["hy_freq_2"][0]),
        fb1=two(a["hy_f_b1_2"][0]), fb2=two(a["hy_f_b2_2"][0]), fb3=two(a["hy_f_b3_2"][0]),
        eps=np.full((P, 1), EPS, np.float32), not_first=(np.arange(P) > 0).astype(np.float32).reshape(P, 1),
        c=np.stack([columns(a["c"][0]), columns(a["c_ctx"]), columns(a["c_2"][0])], 2).reshape(P, -1))
    cols = np.concatenate([parts[name] for name, _ in COLS], 1).astype(np.float32)
    fw = np.zeros((HYF, 3, HYF), np.float32)
    fw[0:2 * BANDS + 1, 0] = a["hy_f_w1_2"][0]
    fw[:, 1] = a["hy_f_w2_2"][0]
    fw[:, 2] = a["hy_f_w3_2"][0]

    def tiles(x):
        return np.ascontiguousarray(x[0].T.reshape(KT, P, -1).transpose(1, 0, 2))
    arrays = dict(xT=tiles(a["x"]), ctxT=tiles(a["ctx"]), cols=cols, fw=fw, fwout=a["hy_f_wout_2"][0], **tables())
    arrays = {k: np.ascontiguousarray(v) for k, v in arrays.items()}
    nc = bacc.Bacc("TRN2", target_bir_lowering=False, num_devices=1)
    aps = {k: nc.dram_tensor(k, v.shape, F32, kind="ExternalInput").ap() for k, v in arrays.items()}
    waps = {}
    for name, v in weights.items():
        arrays["w_" + name] = np.ascontiguousarray(v)
        waps[name] = nc.dram_tensor("w_" + name, v.shape, F32, kind="ExternalInput").ap()
    out = nc.dram_tensor("out", (P, KT, L), F32, kind="ExternalOutput").ap()
    build(nc, w=waps, out=out, **aps)
    r = run_bass_kernel_spmd(nc, [arrays], core_ids=[0])
    y = np.asarray(r.results[0]["out"])
    return np.ascontiguousarray(y.transpose(1, 0, 2).reshape(D, L).T)[None]
```
